# Optimizing a Trainium2 kernel written in Bass

```python
import math
import jax, jax.numpy as jnp
from jax import lax
import numpy as np

D_MODEL = 1024
BATCH = 1
SEQ = 1024
DEPTH = 2

EPS = 1e-6
D_MIX = D_MODEL

SSD_HEADS = 8
SSD_HEAD_DIM = 64
SSD_INNER = SSD_HEADS * SSD_HEAD_DIM
SSD_GROUPS = 2
SSD_HPG = SSD_HEADS // SSD_GROUPS
SSD_STATE = 128
SSD_CONV = 4
SSD_CHUNK = 128
SSD_XBC = SSD_INNER + 2 * SSD_GROUPS * SSD_STATE
DT_MIN = 0.001
DT_MAX = 0.1

MLA_HEADS = 4
MLA_NOPE = 64
MLA_ROPE = 32
MLA_V = 64
MLA_Q_RANK = 256
MLA_KV_RANK = 128
ROPE_THETA = 10000.0
MAX_POS_OFFSET = 1024

SWA_HEADS = 4
SWA_KV_HEADS = 2
SWA_HEAD_DIM = 64
WINDOW = 128

ATTN_BLOCK = 128

SSD_IN = SSD_INNER + SSD_XBC + SSD_HEADS
MLA_IN = MLA_Q_RANK + MLA_KV_RANK + MLA_ROPE
SWA_IN = (SWA_HEADS + 2 * SWA_KV_HEADS) * SWA_HEAD_DIM
D_IN = SSD_IN + MLA_IN + SWA_IN

D_FF = 2816
FFN_CONV = 3

kernel_name = "hybrid_ssd_mla_swa_convffn_adaln"

def rmsnorm(x, g):
    xf = x.astype(jnp.float32)
    y = xf * lax.rsqrt(jnp.mean(xf * xf, axis=-1, keepdims=True) + EPS)
    return (y * g.astype(jnp.float32)).astype(x.dtype)

def causal_dwconv(x, w, b):
    k_width = w.shape[0]
    s = x.shape[1]
    xp = jnp.pad(x, ((0, 0), (k_width - 1, 0), (0, 0)))
    y = b
    for k in range(k_width):
        y = y + xp[:, k:k + s] * w[k]
    return y

def apply_rope(x, cos, sin):
    xf = x.astype(jnp.float32)
    x1, x2 = jnp.split(xf, 2, axis=-1)
    return jnp.concatenate([x1 * cos - x2 * sin, x1 * sin + x2 * cos], axis=-1).astype(x.dtype)

def ssd_mixer(p, conv_w, conv_b, dt_bias, a_log, d_skip, norm_g):
    f32 = jnp.float32
    bsz, s, _ = p.shape
    nc, q = s // SSD_CHUNK, SSD_CHUNK
    z, xbc, dt = jnp.split(p, [SSD_INNER, SSD_INNER + SSD_XBC], axis=-1)
    xbc = jax.nn.silu(causal_dwconv(xbc, conv_w, conv_b))
    xs, bm, cm = jnp.split(xbc, [SSD_INNER, SSD_INNER + SSD_GROUPS * SSD_STATE], axis=-1)
    xs = xs.astype(f32).reshape(bsz, nc, q, SSD_GROUPS, SSD_HPG, SSD_HEAD_DIM)
    bm = bm.astype(f32).reshape(bsz, nc, q, SSD_GROUPS, SSD_STATE)
    cm = cm.astype(f32).reshape(bsz, nc, q, SSD_GROUPS, SSD_STATE)
    dt = jax.nn.softplus(dt.astype(f32) + dt_bias.astype(f32))
    a = -jnp.exp(a_log.astype(f32))
    dt_c = dt.reshape(bsz, nc, q, SSD_GROUPS, SSD_HPG)
    xdt = xs * dt_c[..., None]
    da = (dt * a).reshape(bsz, nc, q, SSD_HEADS).transpose(0, 1, 3, 2)
    a_h = jnp.cumsum(da, axis=-1).reshape(bsz, nc, SSD_GROUPS, SSD_HPG, q)
    causal = jnp.tril(jnp.ones((q, q), dtype=bool))
    seg = a_h[..., :, None] - a_h[..., None, :]
    decay = jnp.exp(jnp.where(causal, seg, -jnp.inf))
    cb = jnp.einsum('bclgn,bcsgn->bcgls', cm, bm)
    y_diag = jnp.einsum('bcghls,bcsghp->bclghp', cb[:, :, :, None] * decay, xdt)
    decay_to_end = jnp.exp(a_h[..., -1:] - a_h)
    states = jnp.einsum('bcsgn,bcghs,bcsghp->bcghpn', bm, decay_to_end, xdt)
    chunk_decay = jnp.exp(a_h[..., -1])

    def step(h, inp):
        st, dec = inp
        return h * dec[..., None, None] + st, h

    h0 = jnp.zeros((bsz, SSD_GROUPS, SSD_HPG, SSD_HEAD_DIM, SSD_STATE), f32)
    _, h_in = lax.scan(step, h0, (states.swapaxes(0, 1), chunk_decay.swapaxes(0, 1)))
    h_in = h_in.swapaxes(0, 1)
    y_off = jnp.einsum('bclgn,bcghpn,bcghl->bclghp', cm, h_in, jnp.exp(a_h))
    y = y_diag + y_off + xs * d_skip.astype(f32).reshape(SSD_GROUPS, SSD_HPG, 1)
    y = y.reshape(bsz, s, SSD_INNER) * jax.nn.silu(z.astype(f32))
    yg = y.reshape(bsz, s, SSD_GROUPS, SSD_INNER // SSD_GROUPS)
    yg = yg * lax.rsqrt(jnp.mean(yg * yg, axis=-1, keepdims=True) + EPS)
    y = yg.reshape(bsz, s, SSD_INNER) * norm_g.astype(f32)
    return y.astype(p.dtype)

def causal_block_attention(q, k, v, scale):
    bsz, s, h, dk = q.shape
    nb = s // ATTN_BLOCK
    qb = q.reshape(bsz, nb, ATTN_BLOCK, h, dk).swapaxes(0, 1)
    kpos = jnp.arange(s)

    def one_block(args):
        qi, i = args
        sc = jnp.einsum('bqhd,bkhd->bhqk', qi, k, preferred_element_type=jnp.float32) * scale
        qpos = i * ATTN_BLOCK + jnp.arange(ATTN_BLOCK)
        sc = jnp.where(kpos[None, :] <= qpos[:, None], sc, -jnp.inf)
        pr = jax.nn.softmax(sc, axis=-1).astype(v.dtype)
        return jnp.einsum('bhqk,bkhd->bqhd', pr, v)

    out = lax.map(one_block, (qb, jnp.arange(nb)))
    return out.swapaxes(0, 1).reshape(bsz, s, h * v.shape[-1])

def mla_mixer(p, q_norm_g, w_uq, kv_norm_g, w_ukv, cos, sin):
    bsz, s, _ = p.shape
    cq, ckv, k_rope = jnp.split(p, [MLA_Q_RANK, MLA_Q_RANK + MLA_KV_RANK], axis=-1)
    qh = (rmsnorm(cq, q_norm_g) @ w_uq).reshape(bsz, s, MLA_HEADS, MLA_NOPE + MLA_ROPE)
    q_nope, q_rope = jnp.split(qh, [MLA_NOPE], axis=-1)
    q_rope = apply_rope(q_rope, cos, sin)
    kv = (rmsnorm(ckv, kv_norm_g) @ w_ukv).reshape(bsz, s, MLA_HEADS, MLA_NOPE + MLA_V)
    k_nope, v = jnp.split(kv, [MLA_NOPE], axis=-1)
    k_rope = apply_rope(k_rope[:, :, None, :], cos, sin)
    qf = jnp.concatenate([q_nope, q_rope], axis=-1)
    kf = jnp.concatenate([k_nope, jnp.broadcast_to(k_rope, (bsz, s, MLA_HEADS, MLA_ROPE))], axis=-1)
    return causal_block_attention(qf, kf, v, 1.0 / math.sqrt(MLA_NOPE + MLA_ROPE))

def swa_sink_mixer(p, sinks):
    bsz, s, _ = p.shape
    grp = SWA_HEADS // SWA_KV_HEADS
    nb = s // WINDOW
    qd = SWA_HEADS * SWA_HEAD_DIM
    kd = SWA_KV_HEADS * SWA_HEAD_DIM
    q, k, v = jnp.split(p, [qd, qd + kd], axis=-1)
    qb = q.reshape(bsz, nb, WINDOW, SWA_KV_HEADS, grp, SWA_HEAD_DIM)

    def band(t):
        tp = jnp.pad(t.reshape(bsz, s, SWA_KV_HEADS, SWA_HEAD_DIM), ((0, 0), (WINDOW, 0), (0, 0), (0, 0)))
        tp = tp.reshape(bsz, nb + 1, WINDOW, SWA_KV_HEADS, SWA_HEAD_DIM)
        return jnp.concatenate([tp[:, :-1], tp[:, 1:]], axis=2)

    kb, vb = band(k), band(v)
    sc = jnp.einsum('bnqhgd,bnkhd->bnhgqk', qb, kb, preferred_element_type=jnp.float32)
    sc = sc * (1.0 / math.sqrt(SWA_HEAD_DIM))
    i = jnp.arange(WINDOW)[:, None]
    j = jnp.arange(2 * WINDOW)[None, :]
    rel = WINDOW + i - j
    blk = jnp.arange(nb)[:, None, None]
    valid = (rel >= 0) & (rel < WINDOW) & ((blk - 1) * WINDOW + j >= 0)
    sc = jnp.where(valid[None, :, None, None], sc, -jnp.inf)
    sink = jnp.broadcast_to(sinks.astype(jnp.float32).reshape(1, 1, SWA_KV_HEADS, grp, 1, 1),
                            sc.shape[:-1] + (1,))
    pr = jax.nn.softmax(jnp.concatenate([sc, sink], axis=-1), axis=-1)[..., :-1]
    o = jnp.einsum('bnhgqk,bnkhd->bnqhgd', pr.astype(vb.dtype), vb)
    return o.reshape(bsz, s, qd)

def setup_inputs(seed: int = 0) -> dict:
    key = jax.random.key(seed)
    ks = iter(jax.random.split(key, 32))
    f32 = jnp.float32
    L = DEPTH

    def nrm(shape, scale):
        return jax.random.normal(next(ks), shape, f32) * scale

    def gain(shape):
        return 1.0 + nrm(shape, 0.02)

    x = nrm((BATCH, SEQ, D_MODEL), 1.0)
    c = nrm((BATCH, D_MODEL), 1.0)
    offs = jax.random.randint(next(ks), (BATCH, 1), 0, MAX_POS_OFFSET, dtype=jnp.int32)
    positions = offs + jnp.arange(SEQ, dtype=jnp.int32)[None, :]
    ada_w = nrm((L, D_MODEL, 6 * D_MODEL), 0.5 * D_MODEL ** -0.5)
    ada_b = nrm((L, 6 * D_MODEL), 0.02)
    norm1_g = gain((L, D_MODEL))
    norm2_g = gain((L, D_MODEL))
    w_in = nrm((L, D_MODEL, D_IN), D_MODEL ** -0.5)
    ssd_conv_w = nrm((L, SSD_CONV, SSD_XBC), SSD_CONV ** -0.5)
    ssd_conv_b = nrm((L, SSD_XBC), 0.02)
    dt0 = jnp.exp(jax.random.uniform(next(ks), (L, SSD_HEADS), f32)
                  * (math.log(DT_MAX) - math.log(DT_MIN)) + math.log(DT_MIN))
    ssd_dt_bias = dt0 + jnp.log(-jnp.expm1(-dt0))
    ssd_a_log = jnp.log(jax.random.uniform(next(ks), (L, SSD_HEADS), f32, 1.0, 16.0))
    ssd_d = 1.0 + nrm((L, SSD_HEADS), 0.1)
    ssd_norm_g = gain((L, SSD_INNER))
    mla_q_norm_g = gain((L, MLA_Q_RANK))
    mla_w_uq = nrm((L, MLA_Q_RANK, MLA_HEADS * (MLA_NOPE + MLA_ROPE)), MLA_Q_RANK ** -0.5)
    mla_kv_norm_g = gain((L, MLA_KV_RANK))
    mla_w_ukv = nrm((L, MLA_KV_RANK, MLA_HEADS * (MLA_NOPE + MLA_V)), MLA_KV_RANK ** -0.5)
    swa_sinks = nrm((L, SWA_HEADS), 1.0)
    w_out = nrm((L, D_MIX, D_MODEL), D_MIX ** -0.5)
    ffn_w_up = nrm((L, D_MODEL, 2 * D_FF), D_MODEL ** -0.5)
    ffn_conv_w = nrm((L, FFN_CONV, 2 * D_FF), FFN_CONV ** -0.5)
    ffn_conv_b = nrm((L, 2 * D_FF), 0.02)
    ffn_w_down = nrm((L, D_FF, D_MODEL), D_FF ** -0.5)
    final_norm_g = gain((D_MODEL,))
    return {"x": x, "c": c, "positions": positions,
            "ada_w": ada_w, "ada_b": ada_b, "norm1_g": norm1_g, "norm2_g": norm2_g,
            "w_in": w_in, "ssd_conv_w": ssd_conv_w, "ssd_conv_b": ssd_conv_b,
            "ssd_dt_bias": ssd_dt_bias, "ssd_a_log": ssd_a_log, "ssd_d": ssd_d,
            "ssd_norm_g": ssd_norm_g, "mla_q_norm_g": mla_q_norm_g, "mla_w_uq": mla_w_uq,
            "mla_kv_norm_g": mla_kv_norm_g, "mla_w_ukv": mla_w_ukv, "swa_sinks": swa_sinks,
            "w_out": w_out, "ffn_w_up": ffn_w_up, "ffn_conv_w": ffn_conv_w,
            "ffn_conv_b": ffn_conv_b, "ffn_w_down": ffn_w_down, "final_norm_g": final_norm_g}

def reference(x, c, positions, ada_w, ada_b, norm1_g, norm2_g, w_in, ssd_conv_w, ssd_conv_b,
              ssd_dt_bias, ssd_a_log, ssd_d, ssd_norm_g, mla_q_norm_g, mla_w_uq, mla_kv_norm_g,
              mla_w_ukv, swa_sinks, w_out, ffn_w_up, ffn_conv_w, ffn_conv_b, ffn_w_down,
              final_norm_g):
    inv_freq = ROPE_THETA ** (-jnp.arange(0, MLA_ROPE, 2, dtype=jnp.float32) / MLA_ROPE)
    ang = positions.astype(jnp.float32)[..., None] * inv_freq
    cos = jnp.cos(ang)[:, :, None, :]
    sin = jnp.sin(ang)[:, :, None, :]
    c_act = jax.nn.silu(c)
    for l in range(DEPTH):
        mod = c_act @ ada_w[l] + ada_b[l]
        sh1, sc1, g1, sh2, sc2, g2 = [m[:, None, :] for m in jnp.split(mod, 6, axis=-1)]
        h = rmsnorm(x, norm1_g[l]) * (1.0 + sc1) + sh1
        proj = h @ w_in[l]
        p_ssd, p_mla, p_swa = jnp.split(proj, [SSD_IN, SSD_IN + MLA_IN], axis=-1)
        y_ssd = ssd_mixer(p_ssd, ssd_conv_w[l], ssd_conv_b[l], ssd_dt_bias[l], ssd_a_log[l],
                          ssd_d[l], ssd_norm_g[l])
        y_mla = mla_mixer(p_mla, mla_q_norm_g[l], mla_w_uq[l], mla_kv_norm_g[l], mla_w_ukv[l],
                          cos, sin)
        y_swa = swa_sink_mixer(p_swa, swa_sinks[l])
        y = jnp.concatenate([y_ssd, y_mla, y_swa], axis=-1) @ w_out[l]
        x = x + g1 * y
        h = rmsnorm(x, norm2_g[l]) * (1.0 + sc2) + sh2
        u = causal_dwconv(h @ ffn_w_up[l], ffn_conv_w[l], ffn_conv_b[l])
        a, b = jnp.split(u, 2, axis=-1)
        x = x + g2 * ((jax.nn.silu(a) * b) @ ffn_w_down[l])
    return rmsnorm(x, final_norm_g)


_drawn_inputs = setup_inputs


def setup_inputs(seed=0):
    import zlib

    import numpy as np

    out = dict(_drawn_inputs(seed))
    spreads = {}
    factors = {'norm1_g': 5.934,
     'norm2_g': 6.313,
     'ssd_conv_b': 6.497,
     'ssd_d': 200.0,
     'ssd_norm_g': 8.0,
     'mla_q_norm_g': 8.0,
     'mla_kv_norm_g': 8.0,
     'swa_sinks': 24.338,
     'ffn_conv_b': 7.017,
     'final_norm_g': 24.975}
    for name, (base, spread) in spreads.items():
        noise = np.random.default_rng([zlib.crc32(name.encode()), seed]).standard_normal(out[name].shape)
        drawn = base * np.exp(spread * noise) if base else spread * noise
        out[name] = __import__('jax').numpy.asarray(drawn.astype(out[name].dtype))
    for name, factor in factors.items():
        out[name] = (out[name] * factor).astype(out[name].dtype)
    return out
```

```python
from contextlib import ExitStack

import numpy as np
import concourse.bass as bass
from concourse import mybir

F32 = mybir.dt.float32
F32R = mybir.dt.float32r
I32 = mybir.dt.int32
ALU = mybir.AluOpType
ACT = mybir.ActivationFunctionType
AX = mybir.AxisListType

P = 128
T = 1024
D = 1024
KT = D // P
DEPTH = 2
EPS = 1e-6
HALF = 512
BLK = 128
NB = T // BLK

SSD_HEADS, SSD_INNER, SSD_XBC = 8, 512, 1024
MLA_H, MLA_NOPE, MLA_ROPE, MLA_V = 4, 64, 32, 64
MLA_QR, MLA_KVR = 256, 128
SWA_H, SWA_D = 4, 64
COL_Z, COL_XBC = 0, SSD_INNER
COL_DT = COL_XBC + SSD_XBC
COL_CQ = COL_DT + SSD_HEADS
COL_CKV = COL_CQ + MLA_QR
COL_KR = COL_CKV + MLA_KVR
COL_SQ = COL_KR + MLA_ROPE
COL_SK = COL_SQ + SWA_H * SWA_D
COL_SV = COL_SK + 2 * SWA_D
D_FF = 2816
FT = D_FF // P
NG = FT // 2
MLA_SCALE = float((MLA_NOPE + MLA_ROPE) ** -0.5)
SWA_SCALE = float(SWA_D ** -0.5)
NEG = -1.0e30

ADA_FIRST = 16
ADA_TILES = 6 * KT


def pack_list():
    packs = [("ada", m) for m in range(ADA_FIRST)]
    rest = list(range(ADA_FIRST, ADA_TILES))
    for t in range(20):
        packs.append(("win", t))
        packs += [("ada", rest.pop(0)) for _ in range(2) if rest]
    return packs + [("out", m) for m in range(KT)]


PACKS = pack_list()
N_PRE = len(PACKS)
N_OUT0 = N_PRE - KT
WIN_AT = {PACKS[n][1]: n for n in range(N_PRE) if PACKS[n][0] == "win"}
ADA_LAST = max(n for n in range(N_PRE) if PACKS[n][0] == "ada")
WIN_COLS = (
    [[(0, COL_SQ, 64), (64, COL_SQ + 128, 64)], [(0, COL_SQ + 64, 64), (64, COL_SQ + 192, 64)],
     [(0, COL_SK, 128)], [(0, COL_SV, 128)],
     [(0, COL_DT, 8), (64, COL_KR, 32), (96, COL_KR + 16, 16), (112, COL_KR, 16)]]
    + [[(0, COL_CQ + 128 * j, 128)] for j in range(2)] + [[(0, COL_CKV, 128)]]
    + [[(0, COL_XBC + 128 * j, 128)] for j in range(8)]
    + [[(0, COL_Z + 128 * j, 128)] for j in range(4)])
T_MISC, T_XBC, T_Z = 4, 8, 16


def pack_dmas(n):
    return len(WIN_COLS[PACKS[n][1]]) if PACKS[n][0] == "win" else 1


def loaded(n):
    return 16 * sum(pack_dmas(m) for m in range(n % 2, n + 1, 2))


R_N1, R_N2, R_ADAB, R_CW, R_CB, R_SN, R_QN, R_KN, R_END = 0, 8, 16, 64, 96, 104, 108, 110, 111
FR = 88


def build(nc, x, c, positions, ada_w, ada_b, norm1_g, norm2_g, w_in, ssd_conv_w, ssd_conv_b,
          ssd_dt_bias, ssd_a_log, ssd_d, ssd_norm_g, mla_q_norm_g, mla_w_uq, mla_kv_norm_g,
          mla_w_ukv, swa_sinks, w_out, ffn_w_up, ffn_conv_w, ffn_conv_b, ffn_w_down,
          final_norm_g, rope_consts, out):
    K = 1024
    base = 16512
    at = {"x": base, "h": base + 32 * K, "hl": base + 96 * K, "raw": base + 112 * K,
          "e": base + 120 * K, "f": base + 184 * K}

    def place(name, shape, dt, offset):
        return nc.alloc_sbuf_tensor_at(name, shape, dt, offset=offset)

    small_at = [at["f"] + 20 * K]

    def small(name, shape, dt=F32):
        n = int(np.prod(shape[1:])) * 4
        t = place(name, shape, dt, small_at[0])
        small_at[0] += (n + 31) // 32 * 32
        assert small_at[0] <= 229368, name
        return t

    xT = place("xT", [P, KT, T], F32, at["x"])
    hHi = place("hHi", [P, KT, T], F32R, at["h"])
    hLo = place("hLo", [P, KT, T], F32R, at["h"] + 32 * K)
    raw = [place(f"raw{s}", [P, 1024], F32, at["raw"] + 4 * K * s) for s in range(2)]
    wHi = [place(f"wHi{s}", [P, 1024], F32R, at["hl"] + 8 * K * s) for s in range(2)]
    wLo = [place(f"wLo{s}", [P, 1024], F32R, at["hl"] + 8 * K * s + 4 * K) for s in range(2)]
    nt = [place(f"nt{i}", [P, T], F32, at["f"] + 4 * K * i) for i in range(4)]
    cs = place("cs", [P, T], F32, at["f"] + 16 * K)
    E = [at["e"] + 4 * K * i for i in range(16)]
    X4 = at["x"] + 16 * K
    sq = place("swaQ", [P, 2, T], F32, E[0])
    sk = place("swaK", [P, T], F32, E[2])
    sv = place("swaV", [P, T], F32, E[3])
    misc = place("misc", [P, T], F32, E[4])
    cq = place("cq", [P, 2, T], F32, E[5])
    ckv = place("ckv", [P, T], F32, E[7])
    xbc = place("xbc", [P, 8, T], F32, E[8])
    zs = place("zs", [P, 4, T], F32, X4)
    sHi = place("swaHi", [P, 2, T], F32R, E[4])
    sLo = place("swaLo", [P, 2, T], F32R, E[6])
    mHi = place("mlaHi", [P, 2, T], F32R, E[0])
    mLo = place("mlaLo", [P, 2, T], F32R, E[2])
    yHi = place("ssdHi", [P, 4, T], F32R, E[12])
    yLo = place("ssdLo", [P, 4, T], F32R, E[8])
    R = [at["h"] + 4 * K * i for i in range(16)]
    qh = [place(f"mlaQ{h}", [P, T], F32, R[h]) for h in range(4)]
    kh = [place(f"mlaK{h}", [P, T], F32, R[4 + h]) for h in range(4)]
    vt = place("mlaV", [P, NB, 256], F32, R[8])
    svt = place("swaVtok", [P, NB, P], F32, R[10])
    rt = place("ropeTmp", [P, T], F32, R[11])
    wuq = place("wuq", [P, 2, MLA_H, P], F32, R[12])
    wukv = place("wukv", [P, MLA_H, P], F32, R[13])
    otok = [place(f"otok{i}", [P, 256], F32, R[14] + K * i) for i in range(2)]
    stat = place("stat", [P, 2, 6, 4], F32, R[15])
    pr = [place(f"prob{i}", [P, T], F32, at["hl"] + 4 * K * i) for i in range(2)]
    pt = [place(f"probT{i}", [P, T], F32, at["hl"] + 8 * K + 4 * K * i) for i in range(2)]
    xd = place("xdt", [P, NB, 8, 64], F32, R[0])
    xe = place("xdtEnd", [P, NB, 8, 64], F32, R[4])
    bt = [place(f"Btok{g}", [P, NB, P], F32, R[8 + g]) for g in range(2)]
    Mt = [place(f"Mt{i}", [P, 4, P], F32, R[10] + 2 * K * i) for i in range(2)]
    ea = [place(f"ea{i}", [P, 4, P], F32, R[11] + 2 * K * i) for i in range(2)]
    yt = [place(f"yt{i}", [P, 4, P], F32, R[12] + 2 * K * i) for i in range(2)]
    hst = place("hstate", [P, 8, 64], F32, R[13])
    cbm = [place(f"cbm{i}", [P, P], F32, R[13] + 2 * K + 512 * i) for i in range(2)]
    adt = place("adt", [P, NB, 40], F32, R[14])
    aend = place("aend", [P, NB, 8], F32, R[14] + 1280)
    dec = place("dec", [P, NB, 8], F32, R[14] + 1280 + 256)
    dte = place("dte", [P, NB, 8], F32, R[14] + 1280 + 512)
    gHi = [[place(f"gHi{q}{k}", [P, T], F32R, E[4 * q + 2 * k]) for k in range(2)] for q in range(2)]
    gLo = [[place(f"gLo{q}{k}", [P, T], F32R, E[4 * q + 2 * k + 1]) for k in range(2)] for q in range(2)]
    ua = [place(f"ua{k}", [P, T], F32, E[8 + 2 * k]) for k in range(2)]
    ub = [place(f"ub{k}", [P, T], F32, E[9 + 2 * k]) for k in range(2)]
    ident = small("ident", [P, P])
    band = small("band", [P, 2, P])
    caus01 = small("caus01", [P, P])
    prm = small("prm", [P, R_END + 1])
    ffp = small("ffp", [P, 2 * FR])
    mod = small("mod", [P, ADA_TILES])
    scl = small("scl", [P, 2, KT])
    cc = small("cc", [P, KT, 2], F32R)
    dcol = small("dcol", [P, 4])
    ropec = small("ropec", [P, 4])
    hp = small("hp", [8, 3])
    sink = small("sink", [P, SWA_H])
    eps = small("eps", [P, 1])
    fng = small("fng", [P, KT])

    bank = [nc.alloc_psum_tensor(f"bank{i}", [P, 1024], F32) for i in range(4)]

    def half(pair, i):
        return bank[pair][:, HALF * i:HALF * (i + 1)]

    xtail = nc.dram_tensor("xtail", [P, 4, T], F32, kind="Internal").ap()

    def sems(stack, names):
        return {n: stack.enter_context(nc.semaphore(n)) for n in names}

    def fview(t):
        return t.bitcast(F32)

    xin = [place(f"xin{i}", [P, D], F32, E[i]) for i in range(NB)]
    crow = place("crow", [8, P], F32, E[8])
    fnrow = place("fnrow", [8, P], F32, E[9])
    posi = place("posi", [P, T], I32, E[10])
    cact = place("cact", [P, KT], F32, E[11])
    two_pi = 6.283185307179586
    parts, rest = [], two_pi
    for bits in (5, 13, 21):
        q = float(np.floor(rest * 2.0 ** bits) / 2.0 ** bits)
        parts.append(q)
        rest -= q
    parts.append(float(np.float32(rest)))
    with ExitStack() as st:
        s = sems(st, ["x_loaded", "small_loaded", "ident_ready", "pool_step", "x_transposed",
                      "x_copied_act", "x_copied_dve", "c_transposed", "c_act", "angle", "rope_sin",
                      "cc_hi", "dve_step"])
        with nc.Block() as block:

            @block.sync
            def _(sp):
                sp.dma_start(crow[:], c.rearrange("b (k p) -> (b k) p", p=P)).then_inc(s["small_loaded"], 16)
                sp.dma_start(fnrow[:], final_norm_g.rearrange("(k p) -> k p", p=P)).then_inc(s["small_loaded"], 16)
                sp.dma_start(ropec[:], rope_consts).then_inc(s["small_loaded"], 16)
                sp.dma_start(posi[64:128, :], positions.to_broadcast([64, T])).then_inc(s["small_loaded"], 16)
                for t in range(NB):
                    sp.dma_start(xin[t][:], x[0, t * P:(t + 1) * P, :]).then_inc(s["x_loaded"], 16)

            @block.gpsimd
            def _(pool):
                pool.memset(ident[:], 0.0).then_inc(s["pool_step"], 1)
                pool.memset(band[:], 0.0).then_inc(s["pool_step"], 1)
                pool.memset(caus01[:], 1.0).then_inc(s["pool_step"], 1)
                pool.memset(cs[0:64, :], 0.0).then_inc(s["pool_step"], 1)
                pool.memset(eps[:], EPS).then_inc(s["pool_step"], 1)
                pool.wait_ge(s["pool_step"], 5)
                pool.affine_select(out=ident[:], in_=ident[:], compare_op=ALU.not_equal, fill=1.0, base=0,
                                   pattern=[[-1, P]], channel_multiplier=1).then_inc(s["ident_ready"], 1)
                pool.affine_select(out=band[:, 0, :], in_=band[:, 0, :], compare_op=ALU.is_gt, fill=NEG, base=0,
                                   pattern=[[1, P]], channel_multiplier=-1).then_inc(s["ident_ready"], 1)
                pool.affine_select(out=band[:, 1, :], in_=band[:, 1, :], compare_op=ALU.is_ge, fill=NEG, base=0,
                                   pattern=[[-1, P]], channel_multiplier=1).then_inc(s["ident_ready"], 1)
                pool.affine_select(out=caus01[:], in_=caus01[:], compare_op=ALU.is_ge, fill=0.0, base=0,
                                   pattern=[[1, P]], channel_multiplier=-1).then_inc(s["ident_ready"], 1)

            @block.tensor
            def _(pe):
                pe.wait_ge(s["ident_ready"], 4)
                pe.wait_ge(s["small_loaded"], 64)
                pe.transpose(bank[3][:, 0:8], crow[:], ident[0:8, 0:8])
                pe.transpose(bank[3][:, 8:16], fnrow[:], ident[0:8, 0:8]).then_inc(s["c_transposed"], 1)
                pe.wait_ge(s["x_loaded"], 16 * NB)
                for t in range(NB):
                    if t >= 2:
                        pe.wait_ge(s["x_copied_act" if t % 2 == 0 else "x_copied_dve"], t // 2)
                    for k in range(KT):
                        mm = pe.transpose(bank[t % 2][:, k * P:(k + 1) * P], xin[t][:, k * P:(k + 1) * P], ident[:])
                    mm.then_inc(s["x_transposed"], 1)

            def copy_x(eng, t, sem):
                eng.wait_ge(s["x_transposed"], t + 1)
                src = bank[t % 2][:].rearrange("p (k t) -> p k t", k=KT)
                dst = xT[:, :, t * P:(t + 1) * P]
                (eng.activation(dst, src, ACT.Copy) if sem == "x_copied_act" else eng.tensor_copy(dst, src)).then_inc(s[sem], 1)

            @block.scalar
            def _(act):
                act.wait_ge(s["c_transposed"], 1)
                act.activation(fng[:], bank[3][:, 8:16], ACT.Copy).then_inc(s["c_act"], 1)
                act.activation(cact[:], bank[3][:, 0:8], ACT.Silu).then_inc(s["c_act"], 1)
                act.wait_ge(s["c_act"], 2)
                act.activation(cc[:, :, 0], cact[:], ACT.Copy).then_inc(s["cc_hi"], 1)
                act.wait_ge(s["angle"], 1)
                act.activation(nt[1][64:128, :], nt[0][64:128, :], ACT.Sin).then_inc(s["rope_sin"], 1)
                for t in range(0, NB, 2):
                    copy_x(act, t, "x_copied_act")

            @block.vector
            def _(dve):
                step = [0]

                def link(ins):
                    step[0] += 1
                    ins.then_inc(s["dve_step"], 1)
                    dve.wait_ge(s["dve_step"], step[0])

                lo, ang, k = slice(64, 128), nt[0], nt[1]
                dve.wait_ge(s["small_loaded"], 64)
                dve.wait_ge(s["ident_ready"], 4)
                link(dve.tensor_copy(nt[2][lo, :], posi[lo, :]))
                link(dve.tensor_scalar(ang[lo, :], nt[2][lo, :], ropec[lo, 0:1], None, ALU.mult))
                link(dve.tensor_scalar(k[lo, :], ang[lo, :], 1.0 / two_pi, ropec[lo, 1:2], ALU.mult, ALU.add))
                link(dve.tensor_scalar(k[lo, :], k[lo, :], 12582912.0, None, ALU.add))
                link(dve.tensor_scalar(k[lo, :], k[lo, :], -12582912.0, None, ALU.add))
                for q in parts:
                    link(dve.scalar_tensor_tensor(out=ang[lo, :], in0=k[lo, :], scalar=-q, in1=ang[lo, :],
                                                  op0=ALU.mult, op1=ALU.add))
                link(dve.tensor_scalar(ang[lo, :], ang[lo, :], ropec[lo, 2:3], None, ALU.add))
                dve.tensor_scalar(ang[lo, :], ang[lo, :], 3.1415925, -3.1415925, ALU.min, ALU.max).then_inc(s["angle"], 1)
                dve.wait_ge(s["cc_hi"], 1)
                dve.tensor_tensor(cc[:, :, 1], cact[:], fview(cc[:, :, 0]), ALU.subtract)
                dve.wait_ge(s["rope_sin"], 1)
                dve.tensor_scalar(cs[lo, :], nt[1][lo, :], ropec[lo, 3:4], None, ALU.mult)
                for t in range(1, NB, 2):
                    copy_x(dve, t, "x_copied_dve")

    names = """raw_loaded0 raw_loaded1 split_hi split_lo pack_used params_loaded uproj_loaded
        tail_saved tail_loaded params_transposed params_copied mod_first mod_rest dve_step act_step
        n1_sq n1_acc n1_sum n1_sqrt n1_recip n1_scaled n1_hi n1_lo
        n2_sq n2_acc n2_sum n2_sqrt n2_recip n2_scaled n2_hi n2_lo
        pair_free0 pair_free1 conv_base conv_tap xbc_act
        misc_clear dt_abs dt_exp dt_sum dt_ln dt_ready
        mn_sq mn_sum mn_sqrt mn_dve mp_full mp_q mp_kv rope_dve
        sw_vt sw_vcopied sw_s sw_m sw_n sw_e sw_t sw_ca sw_cd sw_o sw_x sw_y sw_hi sw_lo
        ml_s ml_n ml_e ml_t ml_ca ml_cd ml_o ml_x ml_y ml_hi ml_lo
        sd_xe sd_xe0 sd_t sd_c sd_xt sd_xd sd_bt sd_bc sd_cb sd_seg sd_dec sd_M sd_yd sd_ed sd_st sd_ea sd_y
        sd_h sd_sq sd_ss sd_rt sd_rd sd_hi sd_lo
        x_updated down_full down_free0 down_free1 up_base up_tap up_silu up_mul up_hi up_lo""".split()
    with nc.Fori(0, DEPTH) as layer, ExitStack() as st:
        s = sems(st, names)

        def of_layer(w):
            return w[bass.ds(layer, 1)]

        w_in_l, ada_l, out_l = of_layer(w_in), of_layer(ada_w), of_layer(w_out)
        up_l, down_l = of_layer(ffn_w_up), of_layer(ffn_w_down)

        def up_pack(G):
            return N_PRE if type(G) is int and G == 0 else N_PRE - 2 + 6 * G

        def down_pack(G):
            return N_PRE + 4 + 6 * G if type(G) is int and G == NG - 1 else N_PRE + 8 + 6 * G

        def run_mlp(eng, up, finish, down):
            up(0, 0, ("up", 1))
            finish(0, 0)
            up(1, 1, ("down", 0))
            finish(1, 1)
            down(0, 0, ("up", 2))
            up(2, 0, ("down", 1))
            finish(2, 0)
            down(1, 1, ("up", 3))
            with eng.Fori(0, (NG - 5) // 2) as i:
                for q in range(2):
                    G = 2 * i + (3 + q)
                    up(G, 1 - q, ("down", G - 1))
                    finish(G, 1 - q)
                    down(G - 1, q, ("up", G + 1))
            up(NG - 2, 1, ("down", NG - 3))
            finish(NG - 2, 1)
            down(NG - 3, 0, ("up", NG - 1))
            up(NG - 1, 0, ("down", NG - 2))
            finish(NG - 1, 0)
            down(NG - 2, 1, ("down", NG - 1))
            down(NG - 1, 0, None)

        def nothing(G, par):
            pass

        def copiers(u):
            if u >= 4 * MLA_H:
                return "ad"
            return "a" if u % 2 else "d"

        def copies_done(eng, u):
            for who, sem in (("a", "ml_ca"), ("d", "ml_cd")):
                n = sum(who in copiers(v) for v in range(u + 1))
                if n:
                    eng.wait_ge(s[sem], n)

        def ml_copy(eng, u, who, sem):
            if who not in copiers(u):
                return
            i = u // MLA_H
            a, b = (0, min(i + 1, 4)) if who == "a" or i < 4 else (4, i + 1)
            eng.wait_ge(s["ml_t"], u + 1)
            if u >= 2:
                eng.wait_ge(s["ml_o"], u - 1)
            else:
                eng.wait_ge(s["sw_o"], NB)
            src, dst = bank[2][:, a * P:b * P], pt[u % 2][:, a * P:b * P]
            (eng.activation(dst, src, ACT.Copy) if who == "a" else eng.tensor_copy(dst, src)).then_inc(s[sem], 1)

        with nc.Block() as block:
            @block.sync
            def _(sp):
                prow = nt[3]
                rows = [(norm1_g, R_N1, 8), (norm2_g, R_N2, 8), (ada_b, R_ADAB, 48), (ssd_conv_w, R_CW, 32),
                        (ssd_conv_b, R_CB, 8), (ssd_norm_g, R_SN, 4), (mla_q_norm_g, R_QN, 2), (mla_kv_norm_g, R_KN, 1)]
                load = lambda dst, src: sp.dma_start(dst, src).then_inc(s["params_loaded"], 16)
                for w, r, n in rows:
                    src = of_layer(w)
                    src = src.rearrange("o a (k p) -> (o a k) p", p=P) if len(w.shape) == 3 else src.rearrange("o (k p) -> (o k) p", p=P)
                    load(prow[r:r + n, 0:P], src)
                taps = of_layer(ffn_conv_w).rearrange("o a (k p) -> (o a k) p", p=P)
                load(prow[0:FR, P:2 * P], taps[0:FR])
                load(prow[0:132 - FR, 2 * P:3 * P], taps[FR:132])
                load(prow[132 - FR:FR, 2 * P:3 * P], of_layer(ffn_conv_b).rearrange("o (k p) -> (o k) p", p=P))
                for i, w in enumerate((ssd_dt_bias, ssd_a_log, ssd_d)):
                    load(hp[:, i:i + 1], of_layer(w).rearrange("o h -> h o"))
                load(sink[:], of_layer(swa_sinks).to_broadcast([P, SWA_H]))

                def load_pack(n, kind, m):
                    if n >= 2:
                        sp.wait_ge(s["split_hi"], n - 1)
                        sp.wait_ge(s["split_lo"], n - 1)
                    sem = s[f"raw_loaded{n % 2}"]
                    dst = raw[n % 2][:].rearrange("p (k m) -> p k m", k=KT)
                    if kind == "win":
                        w = w_in_l.rearrange("o (k p) m -> p (o k) m", p=P)
                        for a, b, width in WIN_COLS[m]:
                            sp.dma_start(dst[:, :, a:a + width], w[:, :, b:b + width]).then_inc(sem, 16)
                    else:
                        w = (ada_l if kind == "ada" else out_l).rearrange("o (k p) m -> p (o k) m", p=P)
                        sp.dma_start(dst, w[:, :, m * P:(m + 1) * P]).then_inc(sem, 16)

                for n, (kind, m) in enumerate(PACKS):
                    if kind == "win" and m == T_XBC:
                        sp.wait_ge(s["n1_lo"], KT)
                        sp.dma_start(xtail, xT[:, 4:8, :]).then_inc(s["tail_saved"], 16)
                    if n == N_OUT0:
                        sp.wait_ge(s["pack_used"], N_OUT0)
                        for k in range(2):
                            wq = of_layer(mla_w_uq)[:, k * P:(k + 1) * P, :].rearrange("o p (h d) -> p (o h) d", h=MLA_H)
                            sp.dma_start(wuq[:, k, :, 0:96], wq).then_inc(s["uproj_loaded"], 16)
                            sp.dma_start(wuq[:, k, :, 96:112], wq[:, :, 80:96]).then_inc(s["uproj_loaded"], 16)
                            sp.dma_start(wuq[:, k, :, 112:128], wq[:, :, 64:80]).then_inc(s["uproj_loaded"], 16)
                        sp.dma_start(wukv[:], of_layer(mla_w_ukv).rearrange("o p (h d) -> p (o h) d", h=MLA_H)).then_inc(s["uproj_loaded"], 16)
                    if n == N_OUT0 + 2:
                        sp.wait_ge(s["sd_y"], NB)
                        sp.dma_start(xT[:, 4:8, :], xtail).then_inc(s["tail_loaded"], 16)
                    load_pack(n, kind, m)

                def raw_free(n):
                    sp.wait_ge(s["split_hi"], n - 1)
                    sp.wait_ge(s["split_lo"], n - 1)

                def load_up(G, par, nxt):
                    for j in range(4):
                        raw_free(up_pack(G) + j)
                        col = ((j // 2) + (j % 2) * FT) * P + G * 2 * P
                        w = up_l.rearrange("o (k p) m -> p (o k) m", p=P)[:, :, bass.ds(col, P)]
                        sp.dma_start(raw[j % 2][:].rearrange("p (k m) -> p k m", k=KT), w).then_inc(s[f"raw_loaded{j % 2}"], 16)

                def load_down(G, par, nxt):
                    for j in range(2):
                        raw_free(down_pack(G) + j)
                        w = down_l[:, bass.ds(G * 2 * P, 2 * P), HALF * j:HALF * (j + 1)].rearrange("o (k p) m -> p (o k) m", p=P)
                        sp.dma_start(raw[j][:].rearrange("p (k m) -> p k m", k=2), w).then_inc(s[f"raw_loaded{j}"], 16)

                run_mlp(sp, load_up, nothing, load_down)

            def split(eng, slot, n, landed, *slot_free):
                if eng is nc.gpsimd:
                    eng.wait_ge(s["split_hi"], n + 1)
                eng.wait_ge(s[f"raw_loaded{slot}"], landed)
                for sem, v in slot_free:
                    eng.wait_ge(s[sem], v)
                if eng is nc.gpsimd:
                    eng.tensor_tensor(wLo[slot][:], raw[slot][:], fview(wHi[slot][:]), ALU.subtract).then_inc(s["split_lo"], 1)
                else:
                    eng.activation(wHi[slot][:], raw[slot][:], ACT.Copy).then_inc(s["split_hi"], 1)

            def split_pre(eng, n):
                if n == WIN_AT[T_MISC]:
                    eng.wait_ge(s["misc_clear"], 1)
                if n in (N_OUT0, N_OUT0 + 1):
                    split(eng, n % 2, n, loaded(n), ("ml_y", NB))
                elif n >= 2:
                    split(eng, n % 2, n, loaded(n), ("pack_used", n - 1))
                else:
                    split(eng, n % 2, n, loaded(n))

            def split_up(eng, G, j):
                landed = loaded(N_PRE - 2 + j % 2) + 16 * (3 * G + j // 2 + (1 if type(G) is int and G == 0 else 0))
                if type(G) is int and G < 2 and j < 2 or j >= 2:
                    free = ("pack_used", N_PRE + 4 * G + j - 1)
                else:
                    free = ("down_full", 8 * (G - 2) + 4 * (j + 1))
                split(eng, j % 2, up_pack(G) + j, landed, free)

            def split_down(eng, G, j):
                final = type(G) is int and G == NG - 1
                landed = loaded(N_PRE - 2 + j) + 16 * (3 * G + (3 if final else 5))
                free = ("down_full", 8 * (NG - 2) + 4 * (j + 1)) if final else ("pack_used", N_PRE + 4 * (G + 1) + 3 + j)
                split(eng, j, down_pack(G) + j, landed, free)

            @block.tensor
            def _(pe):
                mm = pe.matmul
                ones = caus01[:, P - 1:P].to_broadcast([P, P])

                def dense(pair, w_hi, w_lo, r_hi, r_lo, kts, k_ready=None):
                    for k in range(kts):
                        if k_ready is not None:
                            pe.wait_ge(s[k_ready], k + 1)
                        for q, (w, r) in enumerate(((w_hi, r_hi), (w_hi, r_lo), (w_lo, r_hi))):
                            for hf in range(2):
                                last = mm(half(pair, hf), w(k), r(k)[:, HALF * hf:HALF * (hf + 1)],
                                          start=k == 0 and q == 0, stop=k == kts - 1 and q == 2)
                    return last

                pe.wait_ge(s["params_loaded"], 16 * 15)
                pe.transpose(bank[3][:, 0:R_END], nt[3][0:R_END, 0:P], ident[0:R_END, 0:R_END])
                pe.transpose(bank[3][:, P:P + FR], nt[3][0:FR, P:2 * P], ident[0:FR, 0:FR])
                pe.transpose(bank[3][:, 2 * P:2 * P + FR], nt[3][0:FR, 2 * P:3 * P], ident[0:FR, 0:FR])
                for h in range(SSD_HEADS):
                    last = mm(bank[3][64 * (h % 2):64 * (h % 2) + 64, 3 * P + h // 2:3 * P + h // 2 + 1],
                              ident[0:8, h:h + 1].to_broadcast([8, 64]), hp[:, 2:3], start=True, stop=True)
                last.then_inc(s["params_transposed"], 1)

                def norm_sum(i):
                    pe.wait_ge(s[f"n{i}_acc"], KT - 1)
                    for hf in range(2):
                        last = mm(half(1, hf), ones, nt[2][:, HALF * hf:HALF * (hf + 1)], start=True, stop=True)
                    last.then_inc(s[f"n{i}_sum"], 1)

                def ada(n, m):
                    w = wHi[n % 2], wLo[n % 2]
                    pair = 2 if m < ADA_FIRST else 3
                    for k in range(KT):
                        for q in range(2):
                            last = mm(bank[pair][:, 2 * m:2 * m + 2], w[q][:, k * P:(k + 1) * P], cc[:, k, :],
                                      start=k == 0 and q == 0, stop=k == KT - 1 and q == 1)
                    last.then_inc(s["pack_used"], 1)

                def tile_of(n, w):
                    return lambda k: w[n % 2][:, k * P:(k + 1) * P]

                for n, (kind, m) in enumerate(PACKS[:N_OUT0]):
                    if kind == "ada" and m == ADA_FIRST - 1:
                        norm_sum(1)
                    if kind == "ada" and m == ADA_FIRST:
                        pe.wait_ge(s["params_copied"], 4)
                    pe.wait_ge(s["split_lo"], n + 1)
                    if kind == "ada":
                        ada(n, m)
                        continue
                    if m >= 2:
                        pe.wait_ge(s[f"pair_free{m % 2}"], m // 2)
                    if m == 1:
                        pe.wait_ge(s["n1_sqrt"], 1)
                    dense(m % 2, tile_of(n, wHi), tile_of(n, wLo), lambda k: hHi[:, k, :], lambda k: hLo[:, k, :],
                          KT, "n1_lo" if m == 0 else None).then_inc(s["pack_used"], 1)

                pe.wait_ge(s["pair_free0"], 10)
                pe.wait_ge(s["pair_free1"], 10)
                pe.wait_ge(s["mn_sq"], 2)
                for hf in range(2):
                    for k in range(2):
                        last = mm(half(0, hf), ones, nt[k][:, HALF * hf:HALF * (hf + 1)], start=k == 0, stop=k == 1)
                last.then_inc(s["mn_sum"], 1)
                pe.wait_ge(s["mn_sq"], 3)
                for hf in range(2):
                    last = mm(half(1, hf), ones, nt[2][:, HALF * hf:HALF * (hf + 1)], start=True, stop=True)
                last.then_inc(s["mn_sum"], 1)
                pe.wait_ge(s["mod_rest"], 2)
                for b in range(NB):
                    last = pe.transpose(bank[3][:, b * P:(b + 1) * P], sv[:, b * P:(b + 1) * P], ident[:])
                last.then_inc(s["sw_vt"], 1)
                pe.wait_ge(s["uproj_loaded"], 16 * 7)
                pe.wait_ge(s["mn_dve"], 3)
                for h in range(MLA_H):
                    if h < 2:
                        pe.wait_ge(s["mn_sqrt"], h + 1)
                    else:
                        pe.wait_ge(s["mp_q"], 3 * (h - 1))
                        pe.wait_ge(s["mp_kv"], h - 1)
                    for hf in range(2):
                        for k in range(2):
                            last = mm(half(h % 2, hf), wuq[:, k, h, :], cq[:, k, HALF * hf:HALF * (hf + 1)], start=k == 0, stop=k == 1)
                    last.then_inc(s["mp_full"], 1)
                pe.wait_ge(s["mn_dve"], 5)
                for h in range(MLA_H):
                    pe.wait_ge(s["mp_kv"], 3 + h)
                    if h < 2:
                        pe.wait_ge(s["mp_q"], 3 * (3 + h))
                    for hf in range(2):
                        last = mm(bank[h % 2][0:64, HALF * hf:HALF * (hf + 1)], wukv[:, h, 0:64], ckv[:, HALF * hf:HALF * (hf + 1)], start=True, stop=True)
                    last.then_inc(s["mp_full"], 1)
                for u in range(2):
                    pe.wait_ge(s["mp_kv"], 7 + u)
                    for b in range(4 * u, 4 * u + 4):
                        last = mm(bank[u][:, (b % 4) * 256:(b % 4 + 1) * 256], ckv[:, b * P:(b + 1) * P], wukv[:, :, 64:128],
                                  start=True, stop=True)
                    last.then_inc(s["mp_full"], 1)

                def sw_scores(i):
                    if i < 2:
                        pe.wait_ge(s["mp_kv"], 9 + i)
                    else:
                        pe.wait_ge(s["sw_m"], i - 1)
                    lo = max(i - 1, 0) * BLK
                    for h in range(SWA_H):
                        r = slice(64 * (h // 2), 64 * (h // 2) + 64)
                        o = bank[i % 2][:, h * 256 + (0 if i else BLK):(h + 1) * 256]
                        last = mm(o, sq[r, h % 2, i * BLK:(i + 1) * BLK], sk[r, lo:(i + 1) * BLK], start=True, stop=True)
                    last.then_inc(s["sw_s"], 1)

                def sw_transposes(i):
                    pe.wait_ge(s["sw_e"], i + 1)
                    if i >= 1:
                        pe.wait_ge(s["sw_ca"], i)
                        pe.wait_ge(s["sw_cd"], i)
                    for h in range(SWA_H):
                        for b in range(0 if i else 1, 2):
                            q = (2 * h + b) * P
                            last = pe.transpose(bank[2][:, q:q + P], pr[i % 2][:, q:q + P], ident[:])
                    last.then_inc(s["sw_t"], 1)

                def sw_out(i):
                    pe.wait_ge(s["sw_ca"], i + 1)
                    pe.wait_ge(s["sw_cd"], i + 1)
                    if i == 0:
                        pe.wait_ge(s["sw_vcopied"], 1)
                    else:
                        pe.wait_ge(s["sw_x"], i)
                    for h in range(SWA_H):
                        for b in range(0 if i else 1, 2):
                            last = mm(half(3, 0)[:, h * 64:(h + 1) * 64], pt[i % 2][:, (2 * h + b) * P:(2 * h + b + 1) * P],
                                      svt[:, i - 1 + b, (h // 2) * 64:(h // 2) * 64 + 64], start=b == (0 if i else 1), stop=b == 1)
                    last.then_inc(s["sw_o"], 1)

                def to_features(i, x_sem, lo_sem, y_sem):
                    pe.wait_ge(s[x_sem], i + 1)
                    if i >= 1:
                        pe.wait_ge(s[lo_sem], i)
                    for k in range(2):
                        last = pe.transpose(half(3, 1)[:, k * P:(k + 1) * P], otok[i % 2][:, k * P:(k + 1) * P], ident[:])
                    last.then_inc(s[y_sem], 1)

                sw_scores(0)
                for i in range(NB):
                    if i + 1 < NB:
                        sw_scores(i + 1)
                    sw_transposes(i)
                    sw_out(i)
                    if i >= 1:
                        to_features(i - 1, "sw_x", "sw_lo", "sw_y")
                to_features(NB - 1, "sw_x", "sw_lo", "sw_y")

                def ml_scores(u):
                    i, h = divmod(u, MLA_H)
                    if u < 2:
                        pe.wait_ge(s["sw_m"], NB - 1 + u)
                        pe.wait_ge(s["rope_dve"], 6)
                        pe.wait_ge(s["mp_q"], 12)
                    else:
                        pe.wait_ge(s["ml_e"], u - 1)
                    n = (i + 1) * BLK
                    for a in range(0, n, HALF):
                        b = min(a + HALF, n)
                        last = mm(bank[u % 2][:, a:b], qh[h][0:96, i * BLK:n], kh[h][0:96, a:b], start=True, stop=True)
                    last.then_inc(s["ml_s"], 1)

                def ml_transposes(u):
                    i = u // MLA_H
                    pe.wait_ge(s["ml_e"], u + 1)
                    if u >= 1:
                        copies_done(pe, u - 1)
                    else:
                        pe.wait_ge(s["sw_ca"], NB)
                        pe.wait_ge(s["sw_cd"], NB)
                    for b in range(i + 1):
                        last = pe.transpose(bank[2][:, b * P:(b + 1) * P], pr[u % 2][:, b * P:(b + 1) * P], ident[:])
                    last.then_inc(s["ml_t"], 1)

                def ml_out(u):
                    i, h = divmod(u, MLA_H)
                    copies_done(pe, u)
                    if h == 0:
                        pe.wait_ge(s["ml_x" if i else "sw_x"], i if i else NB)
                    for b in range(i + 1):
                        last = mm(half(3, 0)[:, h * 64:(h + 1) * 64], pt[u % 2][:, b * P:(b + 1) * P],
                                  vt[:, b, h * 64:(h + 1) * 64], start=b == 0, stop=b == i)
                    last.then_inc(s["ml_o"], 1)

                ml_scores(0)
                for u in range(4 * NB):
                    if u + 1 < 4 * NB:
                        ml_scores(u + 1)
                    ml_transposes(u)
                    if u == 0:
                        pe.wait_ge(s["sw_lo"], NB)
                    ml_out(u)
                    if u % 4 == 1 and u > 4:
                        to_features(u // 4 - 1, "ml_x", "ml_lo", "ml_y")
                to_features(NB - 1, "ml_x", "ml_lo", "ml_y")

                pe.wait_ge(s["dt_ready"], 1)
                for b in range(NB):
                    last = pe.transpose(half(3, 0)[:, b * 40:(b + 1) * 40], cs[0:40, b * P:(b + 1) * P], ident[0:40, 0:40])
                last.then_inc(s["sd_t"], 1)
                pe.wait_ge(s["sd_c"], 1)
                pe.wait_ge(s["ml_lo"], NB)
                mm(half(3, 1)[:, 0:64], ident[:, P - 1:P].to_broadcast([P, P]), adt[:, :, 0:8], start=True, stop=True).then_inc(s["sd_t"], 1)
                for j in range(4):
                    if j < 2:
                        pe.wait_ge(s["ml_e"], 4 * NB)
                    else:
                        pe.wait_ge(s["sd_xd"], j - 1)
                    pe.wait_ge(s["xbc_act"], j + 1)
                    for b in range(NB):
                        last = pe.transpose(bank[j % 2][:, b * P:(b + 1) * P], xbc[:, j, b * P:(b + 1) * P], ident[:])
                    last.then_inc(s["sd_xt"], 1)
                pe.wait_ge(s["xbc_act"], 8)
                for g in range(2):
                    pe.wait_ge(s["sd_xd"], 3 + g)
                    for b in range(NB):
                        last = pe.transpose(bank[g][:, b * P:(b + 1) * P], xbc[:, 4 + g, b * P:(b + 1) * P], ident[:])
                    last.then_inc(s["sd_xt"], 1)

                def sd_front(v):
                    ch, g = divmod(v, 2)
                    c0 = slice(ch * BLK, (ch + 1) * BLK)
                    if v < 2:
                        pe.wait_ge(s["sd_bt"], 2)
                    else:
                        pe.wait_ge(s["sd_seg"], v - 1)
                    for q in range(4):
                        h = 4 * g + q
                        last = mm(half(v % 2, 0)[:, q * P:(q + 1) * P], ident[0:8, h:h + 1].to_broadcast([8, P]), cs[0:8, c0],
                                  start=True, stop=True)
                    last.then_inc(s["sd_bc"], 1)
                    if v >= 2:
                        pe.wait_ge(s["sd_M"], v - 1)
                    mm(half(2, v % 2)[:, 0:P], xbc[:, 4 + g, c0], xbc[:, 6 + g, c0], start=True, stop=True).then_inc(s["sd_cb"], 1)

                def sd_decay(ch):
                    c0 = slice(ch * BLK, (ch + 1) * BLK)
                    if ch >= 1:
                        pe.wait_ge(s["sd_ea"], ch)
                    else:
                        pe.wait_ge(s["sd_c"], 2)
                    for h in range(SSD_HEADS):
                        last = mm(half(3, 1)[64 * (h % 2):64 * (h % 2) + 64, (h // 2) * P:(h // 2 + 1) * P],
                                  ident[0:8, h:h + 1].to_broadcast([8, 64]), cs[0:8, c0], start=True, stop=True)
                    last.then_inc(s["sd_ed"], 1)

                def sd_back(v):
                    ch, g = divmod(v, 2)
                    c0 = slice(ch * BLK, (ch + 1) * BLK)
                    pe.wait_ge(s["sd_M"], v + 1)
                    if g == 0:
                        pe.wait_ge(s["sd_h"], 1 + 2 * ch)
                        if ch >= 1:
                            pe.wait_ge(s["sd_y"], ch)
                    for q in range(4):
                        h = 4 * g + q
                        r = slice(64 * (h % 2), 64 * (h % 2) + 64)
                        last = mm(half(3, 0)[r, (h // 2) * P:(h // 2 + 1) * P], xd[:, ch, h, :], Mt[v % 2][:, q, :], start=True, stop=True)
                    last.then_inc(s["sd_yd"], 1)
                    for q in range(2):
                        j = 2 * g + q
                        mm(half(0, 1)[:, j * P:(j + 1) * P], hst[:, 2 * j:2 * j + 2, :], xbc[:, 6 + g, c0], start=True, stop=True)
                    mm(half(1, 1)[:, g * 256:(g + 1) * 256], bt[g][:, ch, :], xe[:, ch, 4 * g:4 * g + 4, :], start=True, stop=True).then_inc(s["sd_st"], 1)

                sd_front(0)
                sd_decay(0)
                for v in range(2 * NB):
                    if v + 1 < 2 * NB:
                        sd_front(v + 1)
                    sd_back(v)
                    if v % 2 == 1 and v + 1 < 2 * NB:
                        sd_decay(v // 2 + 1)
                pe.wait_ge(s["sd_h"], 1 + 2 * NB)
                for g in range(2):
                    pe.wait_ge(s["sd_sq"], 2 * g + 2)
                    for hf in range(2):
                        for k in range(2):
                            last = mm(half(g, hf), ones, nt[2 * g + k][:, HALF * hf:HALF * (hf + 1)], start=k == 0, stop=k == 1)
                    last.then_inc(s["sd_ss"], 1)

                y_hi = [yHi[:, j, :] for j in range(4)] + [mHi[:, j, :] for j in range(2)] + [sHi[:, j, :] for j in range(2)]
                y_lo = [yLo[:, j, :] for j in range(4)] + [mLo[:, j, :] for j in range(2)] + [sLo[:, j, :] for j in range(2)]
                for m in range(KT):
                    n = N_OUT0 + m
                    pe.wait_ge(s["split_lo"], n + 1)
                    if m == 0:
                        pe.wait_ge(s["sd_lo"], 4)
                    if m >= 2:
                        pe.wait_ge(s["x_updated"], m - 1)
                    dense(m % 2, tile_of(n, wHi), tile_of(n, wLo), lambda k: y_hi[k], lambda k: y_lo[k], KT).then_inc(s["pack_used"], 1)

                pe.wait_ge(s["x_updated"], KT)
                norm_sum(2)

                def up(G, par, nxt):
                    first = type(G) is int and G == 0
                    for j in range(4):
                        pe.wait_ge(s["split_lo"], up_pack(G) + j + 1)
                        if first and j < 2:
                            if j == 1:
                                pe.wait_ge(s["n2_sqrt"], 1)
                        else:
                            pe.wait_ge(s["up_tap"], 8 * G + 2 * j - 2)
                        dense(j % 2, lambda k: wHi[j % 2][:, k * P:(k + 1) * P], lambda k: wLo[j % 2][:, k * P:(k + 1) * P],
                              lambda k: hHi[:, k, :], lambda k: hLo[:, k, :], KT,
                              "n2_lo" if first and j == 0 else None).then_inc(s["pack_used"], 1)

                def down(G, par, nxt):
                    pe.wait_ge(s["up_lo"], 2 * G + 2)
                    for m in range(KT):
                        j, col = m // 4, (m % 4) * P
                        if m % 4 == 0:
                            pe.wait_ge(s["split_lo"], down_pack(G) + j + 1)
                        pe.wait_ge(s[f"down_free{m % 2}"], 4 * G + m // 2)
                        dense(2 + m % 2, lambda k: wHi[j][:, k * HALF + col:k * HALF + col + P],
                              lambda k: wLo[j][:, k * HALF + col:k * HALF + col + P],
                              lambda k: gHi[par][k][:], lambda k: gLo[par][k][:], 2).then_inc(s["down_full"], 1)

                run_mlp(pe, up, nothing, down)

            def run_splitter(eng, after_up, finish):
                def split_next(nxt, j):
                    if nxt is not None:
                        (split_up if nxt[0] == "up" else split_down)(eng, nxt[1], j)

                def up(G, par, nxt):
                    for j in range(4):
                        if j < 2:
                            split_up(eng, G, j + 2)
                        else:
                            split_next(nxt, j - 2)
                        after_up(G, par, j)

                def down(G, par, nxt):
                    for j in range(2):
                        split_next(nxt, j)

                run_mlp(eng, up, finish, down)

            @block.gpsimd
            def _(pool):
                for n in range(N_PRE):
                    if n == WIN_AT[T_MISC]:
                        pool.wait_ge(s["split_hi"], n - 1)
                        pool.wait_ge(s["split_lo"], n - 1)
                        pool.memset(raw[n % 2][:].rearrange("p (k m) -> p k m", k=KT)[:, :, 8:64], 0.0).then_inc(s["misc_clear"], 1)
                    split_pre(pool, n)
                for j in range(2):
                    split_up(pool, 0, j)

                def g_lo(G, par, c):
                    pool.wait_ge(s["up_hi"], 2 * G + c + 1)
                    pool.tensor_tensor(gLo[par][c][:], ua[c][:], fview(gHi[par][c][:]), ALU.subtract).then_inc(s["up_lo"], 1)

                run_splitter(pool, lambda G, par, j: g_lo(G, par, 0) if j == 3 else None, lambda G, par: g_lo(G, par, 1))

            @block.scalar
            def _(act):
                A = act.activation

                def norm_squares(i, k):
                    if i == 2:
                        act.wait_ge(s["x_updated"], k + 1)
                    if k >= 3:
                        act.wait_ge(s[f"n{i}_acc"], k - 2)
                    A(nt[2 if k == 0 else k % 2][:], xT[:, k, :], ACT.Square).then_inc(s[f"n{i}_sq"], 1)

                def norm_apply(i):
                    act.wait_ge(s[f"n{i}_sum"], 1)
                    A(nt[3][:], bank[1][:], ACT.Sqrt, bias=eps[:], scale=1.0 / D).then_inc(s[f"n{i}_sqrt"], 1)
                    for k in range(KT):
                        act.wait_ge(s[f"n{i}_scaled"], k + 1)
                        A(hHi[:, k, :], nt[k % 2][:], ACT.Identity, bias=mod[:, (i - 1) * 3 * KT + k:(i - 1) * 3 * KT + k + 1]).then_inc(s[f"n{i}_hi"], 1)

                act.wait_ge(s["params_transposed"], 1)
                A(prm[:, 0:R_END], bank[3][:, 0:R_END], ACT.Copy).then_inc(s["params_copied"], 1)
                A(ffp[:, 0:FR], bank[3][:, P:P + FR], ACT.Copy).then_inc(s["params_copied"], 1)
                A(ffp[:, FR:2 * FR], bank[3][:, 2 * P:2 * P + FR], ACT.Copy).then_inc(s["params_copied"], 1)
                A(dcol[:], bank[3][:, 3 * P:3 * P + 4], ACT.Copy).then_inc(s["params_copied"], 1)
                for n in range(2):
                    split_pre(act, n)
                for k in range(KT):
                    norm_squares(1, k)
                    split_pre(act, 2 + 2 * k)
                    split_pre(act, 3 + 2 * k)
                norm_apply(1)
                silu_due = [None]

                def silu_of(j):
                    act.wait_ge(s[f"pair_free{j % 2}"], (T_XBC + j) // 2 + 1)
                    A(xbc[:, j, :], xbc[:, j, :], ACT.Silu).then_inc(s["xbc_act"], 1)

                for n in range(ADA_FIRST, N_OUT0):
                    if n + 2 < N_OUT0:
                        split_pre(act, n + 2)
                    kind, m = PACKS[n]
                    if kind != "win":
                        continue
                    act.wait_ge(s["pack_used"], n + 1)
                    ps, free = bank[m % 2][:], s[f"pair_free{m % 2}"]
                    if m < T_XBC:
                        dst = ([sq[:, 0, :], sq[:, 1, :], sk[:], sv[:], misc[:], cq[:, 0, :], cq[:, 1, :], ckv[:]])[m]
                        A(dst, ps, ACT.Copy).then_inc(free, 1)
                        if m == T_MISC + 1:
                            act.wait_ge(s["pair_free0"], 3)
                            A(nt[0][0:8, :], misc[0:8, :], ACT.Abs, bias=hp[:, 0:1]).then_inc(s["dt_abs"], 1)
                            act.wait_ge(s["dt_abs"], 1)
                            A(nt[1][0:8, :], nt[0][0:8, :], ACT.Exp, scale=-1.0).then_inc(s["dt_exp"], 1)
                            A(hp[:, 1:2], hp[:, 1:2], ACT.Exp).then_inc(s["dt_exp"], 1)
                            act.wait_ge(s["dt_sum"], 1)
                            A(nt[3][0:8, :], nt[2][0:8, :], ACT.Ln).then_inc(s["dt_ln"], 1)
                    elif m < T_Z:
                        j = m - T_XBC
                        A(xbc[:, j, :], ps, ACT.Identity, bias=prm[:, R_CB + j:R_CB + j + 1],
                          scale=prm[:, R_CW + 24 + j:R_CW + 25 + j]).then_inc(s["conv_base"], 1)
                        if j >= 1:
                            silu_of(j - 1)
                    else:
                        if m == T_Z:
                            silu_of(7)
                            act.wait_ge(s["tail_saved"], 16)
                        A(zs[:, m - T_Z, :], ps, ACT.Silu).then_inc(free, 1)

                act.wait_ge(s["dt_ready"], 1)
                for k, src in enumerate((cq[:, 0, :], cq[:, 1, :], ckv[:])):
                    act.wait_ge(s[f"pair_free{(5 + k) % 2}"], (5 + k) // 2 + 1)
                    A(nt[k][:], src, ACT.Square).then_inc(s["mn_sq"], 1)
                act.wait_ge(s["mn_sum"], 1)
                A(nt[3][:], bank[0][:], ACT.Sqrt, bias=eps[:], scale=1.0 / MLA_QR).then_inc(s["mn_sqrt"], 1)
                act.wait_ge(s["mn_sum"], 2)
                A(nt[0][:], bank[1][:], ACT.Sqrt, bias=eps[:], scale=1.0 / MLA_KVR).then_inc(s["mn_sqrt"], 1)
                act.wait_ge(s["sw_vt"], 1)
                A(svt[:], bank[3][:].rearrange("p (b d) -> p b d", b=NB), ACT.Copy).then_inc(s["sw_vcopied"], 1)
                for h in range(MLA_H):
                    act.wait_ge(s["mp_full"], h + 1)
                    A(qh[h][0:64, :], bank[h % 2][0:64, :], ACT.Copy).then_inc(s["mp_kv"], 1)
                for h in range(MLA_H):
                    act.wait_ge(s["mp_full"], 5 + h)
                    A(kh[h][0:64, :], bank[h % 2][0:64, :], ACT.Copy).then_inc(s["mp_kv"], 1)
                for u in range(2):
                    act.wait_ge(s["mp_full"], 9 + u)
                    A(vt[:, 4 * u:4 * u + 4, :], bank[u][:].rearrange("p (b d) -> p b d", b=4), ACT.Copy).then_inc(s["mp_kv"], 1)

                def y_hi(i, y_sem, hi_sem, dst):
                    act.wait_ge(s[y_sem], i + 1)
                    A(dst[:, :, i * BLK:(i + 1) * BLK], half(3, 1)[:, 0:256].rearrange("p (k t) -> p k t", k=2), ACT.Copy).then_inc(s[hi_sem], 1)

                def sw_exp(i):
                    act.wait_ge(s["sw_n"], i + 1)
                    st_ = stat[:, i % 2]
                    for h in range(SWA_H):
                        a = pr[i % 2][:, h * 256 + (0 if i else BLK):(h + 1) * 256]
                        A(a, a, ACT.Exp, bias=st_[:, 1, h:h + 1], accum_out=st_[:, 2, h:h + 1])
                    A(st_[:, 4, :], st_[:, 3, :], ACT.Exp).then_inc(s["sw_e"], 1)

                sw_exp(0)
                act.wait_ge(s["rope_dve"], 6)
                for i in range(NB):
                    if i + 1 < NB:
                        sw_exp(i + 1)
                    act.wait_ge(s["sw_t"], i + 1)
                    if i >= 2:
                        act.wait_ge(s["sw_o"], i - 1)
                    lo = 0 if i else 1
                    view = lambda t: t.rearrange("p (h b k) -> p h b k", h=2, b=2)[:, :, lo:2, :]
                    A(view(pt[i % 2][:, 0:HALF]), view(half(2, 0)), ACT.Copy).then_inc(s["sw_ca"], 1)
                    if i >= 1:
                        y_hi(i - 1, "sw_y", "sw_hi", sHi)
                y_hi(NB - 1, "sw_y", "sw_hi", sHi)

                def ml_exp(u):
                    i, h = divmod(u, MLA_H)
                    n = (i + 1) * BLK
                    act.wait_ge(s["ml_n"], u + 1)
                    if u < 2:
                        act.wait_ge(s["sw_t"], NB)
                    else:
                        act.wait_ge(s["ml_t"], u - 1)
                    A(pr[u % 2][:, 0:n], bank[u % 2][:, 0:n], ACT.Exp, bias=stat[:, i % 2, 1, h:h + 1],
                      scale=MLA_SCALE, accum_out=stat[:, i % 2, 2, h:h + 1]).then_inc(s["ml_e"], 1)

                ml_exp(0)
                for u in range(4 * NB):
                    if u + 1 < 4 * NB:
                        ml_exp(u + 1)
                    ml_copy(act, u, "a", "ml_ca")
                    if u % 4 == 2 and u > 4:
                        y_hi(u // 4 - 1, "ml_y", "ml_hi", mHi)
                y_hi(NB - 1, "ml_y", "ml_hi", mHi)
                for n in range(2):
                    split_pre(act, N_OUT0 + n)

                act.wait_ge(s["sd_t"], 1)
                A(adt[:], half(3, 0)[:, 0:320].rearrange("p (b r) -> p b r", b=NB), ACT.Copy).then_inc(s["sd_c"], 1)
                act.wait_ge(s["sd_t"], 2)
                A(aend[:], half(3, 1)[:, 0:64].rearrange("p (b r) -> p b r", b=NB), ACT.Copy).then_inc(s["sd_c"], 1)
                act.wait_ge(s["sd_c"], 2)
                A(dec[:], aend[:], ACT.Exp).then_inc(s["sd_c"], 1)
                act.wait_ge(s["sd_xe0"], 1)
                A(dte[:], dte[:], ACT.Exp).then_inc(s["sd_c"], 1)
                for g in range(2):
                    act.wait_ge(s["sd_xt"], 5 + g)
                    A(bt[g][:], bank[g][:].rearrange("p (b n) -> p b n", b=NB), ACT.Copy).then_inc(s["sd_bt"], 1)
                for v in range(2 * NB):
                    if v % 2 == 0:
                        act.wait_ge(s["sd_ed"], v // 2 + 1)
                        if v >= 4:
                            act.wait_ge(s["sd_y"], v // 2 - 1)
                        A(ea[(v // 2) % 2][:], half(3, 1).rearrange("p (j l) -> p j l", j=4), ACT.Exp).then_inc(s["sd_ea"], 1)
                    act.wait_ge(s["sd_seg"], v + 1)
                    A(Mt[v % 2][:], Mt[v % 2][:], ACT.Exp).then_inc(s["sd_dec"], 1)
                act.wait_ge(s["sd_y"], NB)
                for j in range(4):
                    A(nt[j][:], xbc[:, j, :], ACT.Square).then_inc(s["sd_sq"], 1)
                for g in range(2):
                    act.wait_ge(s["sd_ss"], g + 1)
                    A(nt[2 * g][:], bank[g][:], ACT.Sqrt, bias=eps[:], scale=1.0 / 256).then_inc(s["sd_rt"], 1)
                for j in range(4):
                    act.wait_ge(s["sd_rd"], 1 + j + 1 + j // 2)
                    A(yHi[:, j, :], xbc[:, j, :], ACT.Copy).then_inc(s["sd_hi"], 1)

                for m in range(KT):
                    if m + 2 < KT:
                        split_pre(act, N_OUT0 + m + 2)
                    else:
                        split_up(act, 0, m + 2 - KT)
                    norm_squares(2, m)
                norm_apply(2)

                def after_up(G, par, j):
                    c, is_b = divmod(j, 2)
                    act.wait_ge(s["pack_used"], N_PRE + 4 * G + j + 1)
                    first = type(G) is int and G == 0
                    if not first:
                        act.wait_ge(s["up_mul" if is_b else "up_lo"], 2 * G - 1 + c)
                    col = 2 * G + c + is_b * FT
                    A((ub if is_b else ua)[c][:], bank[is_b][:], ACT.Identity, bias=ffp[:, bass.ds(col + 3 * 2 * FT, 1)],
                      scale=ffp[:, bass.ds(col + 2 * 2 * FT, 1)]).then_inc(s["up_base"], 1)
                    if is_b:
                        act.wait_ge(s["up_tap"], 8 * G + 4 * c + 2)
                        A(ua[c][:], ua[c][:], ACT.Silu).then_inc(s["up_silu"], 1)
                    if j == 2:
                        g_hi(G, par, 0)

                def g_hi(G, par, c):
                    act.wait_ge(s["up_mul"], 2 * G + c + 1)
                    if not (type(G) is int and G < 2):
                        act.wait_ge(s["down_full"], 8 * (G - 1))
                    A(gHi[par][c][:], ua[c][:], ACT.Copy).then_inc(s["up_hi"], 1)

                run_splitter(act, after_up, lambda G, par: g_hi(G, par, 1))

            @block.vector
            def _(dve):
                step = [0]

                def link(ins):
                    step[0] += 1
                    ins.then_inc(s["dve_step"], 1)
                    dve.wait_ge(s["dve_step"], step[0])

                def norm_adds(i, k):
                    dve.wait_ge(s[f"n{i}_sq"], k + 1)
                    if k >= 2:
                        dve.wait_ge(s[f"n{i}_acc"], k - 1)
                    dve.tensor_tensor(nt[2][:], nt[2][:], nt[k % 2][:], ALU.add).then_inc(s[f"n{i}_acc"], 1)

                def norm_apply(i):
                    dve.wait_ge(s[f"n{i}_sqrt"], 1)
                    dve.reciprocal(nt[3][:], nt[3][:]).then_inc(s[f"n{i}_recip"], 1)
                    dve.wait_ge(s[f"n{i}_recip"], 1)
                    shift = (i - 1) * 3 * KT

                    def scaled(k):
                        if k >= 2:
                            dve.wait_ge(s[f"n{i}_lo"], k - 1)
                        dve.scalar_tensor_tensor(out=nt[k % 2][:], in0=xT[:, k, :], scalar=scl[:, i - 1, k:k + 1], in1=nt[3][:],
                                                 op0=ALU.mult, op1=ALU.mult).then_inc(s[f"n{i}_scaled"], 1)

                    scaled(0)
                    for k in range(KT):
                        if k + 1 < KT:
                            scaled(k + 1)
                        dve.wait_ge(s[f"n{i}_hi"], k + 1)
                        dve.scalar_tensor_tensor(out=hLo[:, k, :], in0=nt[k % 2][:], scalar=mod[:, shift + k:shift + k + 1],
                                                 in1=fview(hHi[:, k, :]), op0=ALU.add, op1=ALU.subtract).then_inc(s[f"n{i}_lo"], 1)

                def modulation(first, last, pair, sem):
                    ps = bank[pair][:, 2 * first:2 * last].rearrange("p (m c) -> p m c", c=2)
                    dst = mod[:, first:last]
                    dve.tensor_tensor(dst, ps[:, :, 0], prm[:, R_ADAB + first:R_ADAB + last], ALU.add).then_inc(s[sem], 1)
                    dve.wait_ge(s[sem], 1)
                    dve.tensor_tensor(dst, ps[:, :, 1], dst, ALU.add).then_inc(s[sem], 1)
                    dve.wait_ge(s[sem], 2)

                for k in range(1, KT):
                    norm_adds(1, k)
                dve.wait_ge(s["params_copied"], 4)
                dve.wait_ge(s["pack_used"], ADA_FIRST)
                modulation(0, ADA_FIRST, 2, "mod_first")
                link(dve.scalar_tensor_tensor(out=scl[:, 0, :], in0=mod[:, KT:2 * KT], scalar=1.0, in1=prm[:, R_N1:R_N1 + KT],
                                              op0=ALU.add, op1=ALU.mult))
                norm_apply(1)

                def dt_work():
                    dve.wait_ge(s["pair_free0"], 3)
                    n0, n1, n2, n3 = (t[0:8, :] for t in nt)
                    raw_dt = misc[0:8, :]
                    dve.wait_ge(s["dt_exp"], 2)
                    link(dve.tensor_scalar(hp[:, 1:2], hp[:, 1:2], -1.0, None, ALU.mult))
                    dve.tensor_scalar(n2, n1, 1.0, None, ALU.add).then_inc(s["dt_sum"], 1)
                    dve.wait_ge(s["dt_ln"], 1)
                    link(dve.tensor_scalar(n2, n2, -1.0, None, ALU.add))
                    link(dve.tensor_scalar(n0, n2, 0.0, None, ALU.is_equal))
                    link(dve.tensor_tensor(n2, n2, n0, ALU.add))
                    link(dve.reciprocal(n2, n2))
                    link(dve.tensor_tensor(n3, n3, n1, ALU.mult))
                    link(dve.tensor_tensor(n3, n3, n2, ALU.mult))
                    link(dve.tensor_tensor(n1, n1, n0, ALU.mult))
                    link(dve.tensor_tensor(n3, n3, n1, ALU.add))
                    link(dve.tensor_scalar(n0, raw_dt, hp[:, 0:1], 0.0, ALU.add, ALU.max))
                    link(dve.tensor_tensor(n2, n0, n3, ALU.add))
                    link(dve.tensor_copy(cs[32:40, :], n2))
                    link(dve.tensor_scalar(n1, n2, hp[:, 1:2], None, ALU.mult))
                    link(dve.tensor_scalar(n0, n2, 0.0, 1.0, ALU.mult, ALU.add))
                    for b in range(NB):
                        c0 = slice(b * BLK, (b + 1) * BLK)
                        last = dve.tensor_tensor_scan(cs[0:8, c0], n0[:, c0], n1[:, c0], 0.0, ALU.mult, ALU.add)
                    last.then_inc(s["dt_ready"], 1)

                dt_work()
                for j in range(8):
                    m = T_XBC + j
                    ps = bank[m % 2]
                    dve.wait_ge(s["conv_base"], j + 1)
                    for d in (1, 2, 3):
                        if d > 1:
                            dve.wait_ge(s["conv_tap"], 2 * j + d - 1)
                        col = R_CW + (3 - d) * 8 + j
                        ins = dve.scalar_tensor_tensor(out=xbc[:, j, d:T], in0=ps[:, 0:T - d], scalar=prm[:, col:col + 1],
                                                       in1=xbc[:, j, d:T], op0=ALU.mult, op1=ALU.add)
                        ins.then_inc(s["conv_tap"] if d < 3 else s[f"pair_free{m % 2}"], 1)
                dve.wait_ge(s["pack_used"], ADA_LAST + 1)
                modulation(ADA_FIRST, ADA_TILES, 3, "mod_rest")
                link(dve.scalar_tensor_tensor(out=scl[:, 1, :], in0=mod[:, 4 * KT:5 * KT], scalar=1.0, in1=prm[:, R_N2:R_N2 + KT],
                                              op0=ALU.add, op1=ALU.mult))

                def mn(ins, n):
                    ins.then_inc(s["mn_dve"], 1)
                    if n:
                        dve.wait_ge(s["mn_dve"], n)

                dve.wait_ge(s["mn_sqrt"], 1)
                mn(dve.reciprocal(nt[3][:], nt[3][:]), 1)
                for k in range(2):
                    mn(dve.scalar_tensor_tensor(out=cq[:, k, :], in0=cq[:, k, :], scalar=prm[:, R_QN + k:R_QN + k + 1], in1=nt[3][:],
                                                op0=ALU.mult, op1=ALU.mult), 0)
                dve.wait_ge(s["mn_sqrt"], 2)
                mn(dve.reciprocal(nt[0][:], nt[0][:]), 4)
                mn(dve.scalar_tensor_tensor(out=ckv[:], in0=ckv[:], scalar=prm[:, R_KN:R_KN + 1], in1=nt[0][:],
                                            op0=ALU.mult, op1=ALU.mult), 0)
                a, b = slice(64, 96), slice(96, 128)

                def rope(ins, n):
                    ins.then_inc(s["rope_dve"], 1)
                    dve.wait_ge(s["rope_dve"], n)

                rope(dve.tensor_tensor(rt[a, :], misc[b, :], cs[b, :], ALU.mult), 1)
                rope(dve.tensor_tensor(kh[0][a, :], misc[a, :], cs[a, :], ALU.mult), 2)
                for n, h in enumerate((1, 2, 3, 0)):
                    rope(dve.tensor_tensor(kh[h][a, :], kh[0][a, :], rt[a, :], ALU.add), 3 + n)
                for h in range(MLA_H):
                    dve.wait_ge(s["mp_full"], h + 1)
                    ps = bank[h % 2]
                    if h:
                        dve.wait_ge(s["mp_q"], 3 * h)
                    dve.tensor_tensor(rt[a, :], ps[b, :], cs[b, :], ALU.mult).then_inc(s["mp_q"], 1)
                    dve.tensor_tensor(qh[h][a, :], ps[a, :], cs[a, :], ALU.mult).then_inc(s["mp_q"], 1)
                    dve.wait_ge(s["mp_q"], 3 * h + 2)
                    dve.tensor_tensor(qh[h][a, :], qh[h][a, :], rt[a, :], ALU.add).then_inc(s["mp_q"], 1)

                def sw_max(i):
                    dve.wait_ge(s["sw_s"], i + 1)
                    if i >= 2:
                        dve.wait_ge(s["sw_t"], i - 1)
                    lo = 0 if i else 1
                    p4 = pr[i % 2][:].rearrange("p (h b k) -> p h b k", h=4, b=2)
                    s4 = bank[i % 2][:].rearrange("p (h b k) -> p h b k", h=4, b=2)
                    st_ = stat[:, i % 2]
                    if i:
                        dve.scalar_tensor_tensor(out=p4.rearrange("p h b k -> p h (b k)"), in0=s4.rearrange("p h b k -> p h (b k)"), scalar=SWA_SCALE,
                                                 in1=band[:].rearrange("p b k -> p (b k)").unsqueeze(1).to_broadcast([P, 4, 2 * P]),
                                                 op0=ALU.mult, op1=ALU.add).then_inc(s["sw_m"], 1)
                    else:
                        dve.scalar_tensor_tensor(out=p4[:, :, 1, :], in0=s4[:, :, 1, :], scalar=SWA_SCALE,
                                                 in1=band[:, 1, :].unsqueeze(1).to_broadcast([P, 4, P]),
                                                 op0=ALU.mult, op1=ALU.add).then_inc(s["sw_m"], 1)
                    dve.wait_ge(s["sw_m"], i + 1)
                    src = p4.rearrange("p h b k -> p h (b k)") if i else p4[:, :, 1, :]
                    link(dve.tensor_reduce(st_[:, 0, :], src, AX.X, ALU.max))
                    link(dve.tensor_tensor(st_[:, 0, :], st_[:, 0, :], sink[:], ALU.max))
                    link(dve.tensor_scalar(st_[:, 1, :], st_[:, 0, :], -1.0, None, ALU.mult))
                    dve.tensor_tensor(st_[:, 3, :], st_[:, 1, :], sink[:], ALU.add).then_inc(s["sw_n"], 1)

                def sw_norm(i):
                    st_ = stat[:, i % 2]
                    dve.wait_ge(s["sw_e"], i + 1)
                    link(dve.tensor_tensor(st_[:, 5, :], st_[:, 2, :], st_[:, 4, :], ALU.add))
                    link(dve.reciprocal(st_[:, 5, :], st_[:, 5, :]))
                    normalise(i, "sw_o", i + 1, "sw_y", "sw_x")

                def normalise(i, o_sem, o_val, y_sem, x_sem):
                    dve.wait_ge(s[o_sem], o_val)
                    if i >= 2:
                        dve.wait_ge(s[y_sem], i - 1)
                    dve.tensor_tensor(otok[i % 2][:].rearrange("p (h d) -> p h d", h=4),
                                      half(3, 0)[:, 0:256].rearrange("p (h d) -> p h d", h=4),
                                      stat[:, i % 2, 5, :].unsqueeze(2).to_broadcast([P, 4, 64]), ALU.mult).then_inc(s[x_sem], 1)

                def y_lo(i, hi_sem, lo_sem, hi, lo):
                    dve.wait_ge(s[hi_sem], i + 1)
                    blk = slice(i * BLK, (i + 1) * BLK)
                    dve.tensor_tensor(lo[:, :, blk], half(3, 1)[:, 0:256].rearrange("p (k t) -> p k t", k=2),
                                      fview(hi[:, :, blk]), ALU.subtract).then_inc(s[lo_sem], 1)

                sw_max(0)
                for i in range(NB):
                    if i + 1 < NB:
                        sw_max(i + 1)
                    dve.wait_ge(s["sw_t"], i + 1)
                    if i >= 2:
                        dve.wait_ge(s["sw_o"], i - 1)
                    lo = 0 if i else 1
                    view = lambda t: t.rearrange("p (h b k) -> p h b k", h=2, b=2)[:, :, lo:2, :]
                    dve.tensor_copy(view(pt[i % 2][:, HALF:T]), view(half(2, 1))).then_inc(s["sw_cd"], 1)
                    sw_norm(i)
                    if i >= 1:
                        y_lo(i - 1, "sw_hi", "sw_lo", sHi, sLo)
                y_lo(NB - 1, "sw_hi", "sw_lo", sHi, sLo)

                def ml_max(u):
                    i, h = divmod(u, MLA_H)
                    n = (i + 1) * BLK
                    dve.wait_ge(s["ml_s"], u + 1)
                    diag = bank[u % 2][:, i * BLK:n]
                    link(dve.tensor_tensor(diag, diag, band[:, 1, :], ALU.add))
                    link(dve.tensor_reduce(stat[:, i % 2, 0, h:h + 1], bank[u % 2][:, 0:n], AX.X, ALU.max))
                    dve.tensor_scalar(stat[:, i % 2, 1, h:h + 1], stat[:, i % 2, 0, h:h + 1], -MLA_SCALE, None, ALU.mult).then_inc(s["ml_n"], 1)

                def ml_norm(i):
                    dve.wait_ge(s["ml_e"], 4 * i + 4)
                    link(dve.reciprocal(stat[:, i % 2, 5, :], stat[:, i % 2, 2, :]))
                    normalise(i, "ml_o", 4 * i + 4, "ml_y", "ml_x")

                ml_max(0)
                for u in range(4 * NB):
                    if u + 1 < 4 * NB:
                        ml_max(u + 1)
                    ml_copy(dve, u, "d", "ml_cd")
                    if u % 4 == 0 and u:
                        ml_norm(u // 4 - 1)
                    if u % 4 == 3 and u > 4:
                        y_lo(u // 4 - 1, "ml_hi", "ml_lo", mHi, mLo)
                ml_norm(NB - 1)
                y_lo(NB - 1, "ml_hi", "ml_lo", mHi, mLo)

                dve.wait_ge(s["sd_c"], 2)
                dve.tensor_tensor(dte[:], aend[:], adt[:, :, 0:8], ALU.subtract).then_inc(s["sd_xe0"], 1)
                dve.memset(hst[:], 0.0).then_inc(s["sd_h"], 1)

                def x_end(j):
                    if j == 0:
                        dve.wait_ge(s["sd_c"], 4)
                    dve.wait_ge(s["sd_xd"], j + 1)
                    o = slice(2 * j, 2 * j + 2)
                    dve.tensor_tensor(xe[:, :, o, :], xd[:, :, o, :], dte[:, :, o].unsqueeze(3).to_broadcast([P, NB, 2, 64]), ALU.mult).then_inc(s["sd_xe"], 1)

                for j in range(4):
                    dve.wait_ge(s["sd_xt"], j + 1)
                    o = slice(2 * j, 2 * j + 2)
                    dve.tensor_tensor(xd[:, :, o, :], bank[j % 2][:].rearrange("p (b h d) -> p b h d", b=NB, h=2),
                                      adt[:, :, 32 + 2 * j:34 + 2 * j].unsqueeze(3).to_broadcast([P, NB, 2, 64]), ALU.mult).then_inc(s["sd_xd"], 1)
                    if j >= 1:
                        x_end(j - 1)
                x_end(3)

                def decay_min(v):
                    ch, g = divmod(v, 2)
                    dve.wait_ge(s["sd_bc"], v + 1)
                    if v >= 2:
                        dve.wait_ge(s["sd_yd"], v - 1)
                    for q in range(4):
                        h = 4 * g + q
                        last = dve.tensor_scalar(Mt[v % 2][:, q, :], half(v % 2, 0)[:, q * P:(q + 1) * P], adt[:, ch, h:h + 1], 0.0,
                                                 ALU.subtract, ALU.min)
                    last.then_inc(s["sd_seg"], 1)

                def mix(v):
                    dve.wait_ge(s["sd_cb"], v + 1)
                    link(dve.tensor_tensor(cbm[v % 2][:], half(2, v % 2)[:, 0:P], caus01[:], ALU.mult))
                    dve.wait_ge(s["sd_dec"], v + 1)
                    dve.tensor_tensor(Mt[v % 2][:], Mt[v % 2][:], cbm[v % 2][:].unsqueeze(1).to_broadcast([P, 4, P]), ALU.mult).then_inc(s["sd_M"], 1)

                def chunk_out(ch):
                    c0 = slice(ch * BLK, (ch + 1) * BLK)
                    y = yt[ch % 2]
                    dve.wait_ge(s["sd_st"], 2 * ch + 2)
                    dve.wait_ge(s["sd_ea"], ch + 1)
                    dve.tensor_tensor(hst[:], hst[:], dec[:, ch, :].unsqueeze(2).to_broadcast([P, 8, 64]), ALU.mult).then_inc(s["sd_h"], 1)
                    dve.wait_ge(s["sd_h"], 2 + 2 * ch)
                    dve.tensor_tensor(hst[:], hst[:], half(1, 1).rearrange("p (h d) -> p h d", h=8), ALU.add).then_inc(s["sd_h"], 1)
                    link(dve.tensor_tensor(y[:], half(0, 1).rearrange("p (j l) -> p j l", j=4), ea[ch % 2][:], ALU.mult))
                    link(dve.tensor_tensor(y[:], half(3, 0).rearrange("p (j l) -> p j l", j=4), y[:], ALU.add))
                    for j in range(4):
                        last = dve.scalar_tensor_tensor(out=y[:, j, :], in0=xbc[:, j, c0], scalar=dcol[:, j:j + 1], in1=y[:, j, :],
                                                        op0=ALU.mult, op1=ALU.add)
                    link(last)
                    dve.tensor_tensor(xbc[:, 0:4, c0], y[:], zs[:, :, c0], ALU.mult).then_inc(s["sd_y"], 1)

                decay_min(0)
                for v in range(2 * NB):
                    if v + 1 < 2 * NB:
                        decay_min(v + 1)
                    mix(v)
                    if v % 2:
                        chunk_out(v // 2)
                k = 0
                for g in range(2):
                    dve.wait_ge(s["sd_rt"], g + 1)
                    dve.reciprocal(nt[2 * g][:], nt[2 * g][:]).then_inc(s["sd_rd"], 1)
                    k += 1
                    dve.wait_ge(s["sd_rd"], k)
                    for j in (2 * g, 2 * g + 1):
                        dve.scalar_tensor_tensor(out=xbc[:, j, :], in0=xbc[:, j, :], scalar=prm[:, R_SN + j:R_SN + j + 1],
                                                 in1=nt[2 * g][:], op0=ALU.mult, op1=ALU.mult).then_inc(s["sd_rd"], 1)
                        k += 1
                for j in range(4):
                    dve.wait_ge(s["sd_hi"], j + 1)
                    dve.tensor_tensor(yLo[:, j, :], xbc[:, j, :], fview(yHi[:, j, :]), ALU.subtract).then_inc(s["sd_lo"], 1)

                for m in range(KT):
                    dve.wait_ge(s["pack_used"], N_OUT0 + m + 1)
                    if m == 4:
                        dve.wait_ge(s["tail_loaded"], 16)
                    dve.scalar_tensor_tensor(out=xT[:, m, :], in0=bank[m % 2][:], scalar=mod[:, 2 * KT + m:2 * KT + m + 1],
                                             in1=xT[:, m, :], op0=ALU.mult, op1=ALU.add).then_inc(s["x_updated"], 1)
                    if m >= 2:
                        norm_adds(2, m - 1)
                norm_adds(2, KT - 1)
                norm_apply(2)

                def up(G, par, nxt):
                    for j in range(4):
                        c, is_b = divmod(j, 2)
                        w = 4 * G + j
                        y = (ub if is_b else ua)[c]
                        dve.wait_ge(s["up_base"], w + 1)
                        for d in (1, 2):
                            if d == 2:
                                dve.wait_ge(s["up_tap"], 2 * w + 1)
                            col = 2 * G + c + is_b * FT + (2 - d) * 2 * FT
                            dve.scalar_tensor_tensor(out=y[:, d:T], in0=bank[is_b][:, 0:T - d], scalar=ffp[:, bass.ds(col, 1)],
                                                     in1=y[:, d:T], op0=ALU.mult, op1=ALU.add).then_inc(s["up_tap"], 1)
                        if is_b:
                            dve.wait_ge(s["up_silu"], 2 * G + c + 1)
                            dve.wait_ge(s["up_tap"], 2 * w + 2)
                            dve.tensor_tensor(ua[c][:], ua[c][:], ub[c][:], ALU.mult).then_inc(s["up_mul"], 1)

                def down(G, par, nxt):
                    for m in range(KT):
                        dve.wait_ge(s["down_full"], 8 * G + m + 1)
                        if not (type(G) is int and G == 0):
                            dve.wait_ge(s[f"down_free{m % 2}"], 4 * (G - 1) + m // 2 + 1)
                        dve.scalar_tensor_tensor(out=xT[:, m, :], in0=bank[2 + m % 2][:], scalar=mod[:, 5 * KT + m:5 * KT + m + 1],
                                                 in1=xT[:, m, :], op0=ALU.mult, op1=ALU.add).then_inc(s[f"down_free{m % 2}"], 1)

                run_mlp(dve, up, nothing, down)

        with nc.Block() as block:
            @block.sync
            def _(sp):
                for name in names:
                    sp.sem_clear(s[name])

    xout = [place(f"xout{i}", [P, D], F32, E[i]) for i in range(4)]
    with ExitStack() as st:
        s = sems(st, ["sq", "acc", "sum", "sqrt", "recip", "normed", "transposed", "copied_act", "copied_dve", "out_written"])
        with nc.Block() as block:
            def copy_out(eng, t, sem):
                eng.wait_ge(s["transposed"], t + 1)
                if t >= 4:
                    eng.wait_ge(s["out_written"], 16 * (t - 3))
                src, dst = bank[t % 4][:], xout[t % 4][:]
                (eng.activation(dst, src, ACT.Copy) if sem == "copied_act" else eng.tensor_copy(dst, src)).then_inc(s[sem], 1)

            @block.scalar
            def _(act):
                for k in range(KT):
                    if k >= 3:
                        act.wait_ge(s["acc"], k - 2)
                    act.activation(nt[2 if k == 0 else k % 2][:], xT[:, k, :], ACT.Square).then_inc(s["sq"], 1)
                act.wait_ge(s["sum"], 1)
                act.activation(nt[3][:], bank[1][:], ACT.Sqrt, bias=eps[:], scale=1.0 / D).then_inc(s["sqrt"], 1)
                for t in range(0, NB, 2):
                    copy_out(act, t, "copied_act")

            @block.vector
            def _(dve):
                for k in range(1, KT):
                    dve.wait_ge(s["sq"], k + 1)
                    if k >= 2:
                        dve.wait_ge(s["acc"], k - 1)
                    dve.tensor_tensor(nt[2][:], nt[2][:], nt[k % 2][:], ALU.add).then_inc(s["acc"], 1)
                dve.wait_ge(s["sqrt"], 1)
                dve.reciprocal(nt[3][:], nt[3][:]).then_inc(s["recip"], 1)
                dve.wait_ge(s["recip"], 1)
                for k in range(KT):
                    dve.scalar_tensor_tensor(out=xT[:, k, :], in0=xT[:, k, :], scalar=fng[:, k:k + 1], in1=nt[3][:],
                                             op0=ALU.mult, op1=ALU.mult).then_inc(s["normed"], 1)
                for t in range(1, NB, 2):
                    copy_out(dve, t, "copied_dve")

            @block.tensor
            def _(pe):
                pe.wait_ge(s["acc"], KT - 1)
                for hf in range(2):
                    last = pe.matmul(half(1, hf), caus01[:, P - 1:P].to_broadcast([P, P]), nt[2][:, HALF * hf:HALF * (hf + 1)], start=True, stop=True)
                last.then_inc(s["sum"], 1)
                pe.wait_ge(s["sqrt"], 1)
                for t in range(NB):
                    if t >= 4:
                        pe.wait_ge(s["copied_act" if t % 2 == 0 else "copied_dve"], (t - 4) // 2 + 1)
                    for k in range(KT):
                        if t == 0:
                            pe.wait_ge(s["normed"], k + 1)
                        last = pe.transpose(bank[t % 4][:, k * P:(k + 1) * P], xT[:, k, t * P:(t + 1) * P], ident[:])
                    last.then_inc(s["transposed"], 1)

            @block.sync
            def _(sp):
                for t in range(NB):
                    sp.wait_ge(s["copied_act" if t % 2 == 0 else "copied_dve"], t // 2 + 1)
                    if t:
                        sp.wait_ge(s["out_written"], 16 * t)
                    sp.dma_start(out[0, t * P:(t + 1) * P, :], xout[t % 4][:]).then_inc(s["out_written"], 16)
                sp.wait_ge(s["out_written"], 16 * NB)


_INS = ["x", "c", "positions", "ada_w", "ada_b", "norm1_g", "norm2_g", "w_in", "ssd_conv_w", "ssd_conv_b",
        "ssd_dt_bias", "ssd_a_log", "ssd_d", "ssd_norm_g", "mla_q_norm_g", "mla_w_uq", "mla_kv_norm_g",
        "mla_w_ukv", "swa_sinks", "w_out", "ffn_w_up", "ffn_conv_w", "ffn_conv_b", "ffn_w_down", "final_norm_g"]


def rope_constants():
    k = np.zeros((P, 4), np.float32)
    inv = np.float32(10000.0) ** (-np.arange(0, MLA_ROPE, 2, dtype=np.float32) / np.float32(MLA_ROPE))
    k[64:, 0] = np.tile(inv, 4)
    k[64:96, 1], k[64:96, 2] = 0.25, np.pi / 2
    k[:, 3] = 1.0
    k[96:112, 3] = -1.0
    return k


def kernel(**inputs):
    import numpy as _np
    import concourse.bacc as _bacc
    from concourse import mybir as _mybir
    from concourse.bass_utils import run_bass_kernel_spmd as _run

    nc = _bacc.Bacc("TRN2", target_bir_lowering=False, num_devices=1)
    arrays, args = {}, []
    held = [(n, inputs[n]) for n in _INS] + [("rope_consts", rope_constants())]
    for name, a in held:
        a = _np.ascontiguousarray(a)
        arrays[f"in_{name}_dram"] = a
        args.append(nc.dram_tensor(f"in_{name}_dram", a.shape, _mybir.dt.from_np(a.dtype), kind="ExternalInput").ap())
    args.append(nc.dram_tensor("out_0_dram", (1, T, D), F32, kind="ExternalOutput").ap())
    build(nc, *args)
    r = _run(nc, [arrays], core_ids=[0])
    return r.results[0]["out_0_dram"]
```

```python
from contextlib import ExitStack

import numpy as np
import concourse.bass as bass
from concourse import mybir

F32 = mybir.dt.float32
F32R = mybir.dt.float32r
I32 = mybir.dt.int32
ALU = mybir.AluOpType
ACT = mybir.ActivationFunctionType
AX = mybir.AxisListType

P = 128
T = 1024
D = 1024
KT = D // P
DEPTH = 2
EPS = 1e-6
HALF = 512
BLK = 128
NB = T // BLK

SSD_HEADS, SSD_INNER, SSD_XBC = 8, 512, 1024
MLA_H, MLA_NOPE, MLA_ROPE, MLA_V = 4, 64, 32, 64
MLA_QR, MLA_KVR = 256, 128
SWA_H, SWA_D = 4, 64
COL_Z, COL_XBC = 0, SSD_INNER
COL_DT = COL_XBC + SSD_XBC
COL_CQ = COL_DT + SSD_HEADS
COL_CKV = COL_CQ + MLA_QR
COL_KR = COL_CKV + MLA_KVR
COL_SQ = COL_KR + MLA_ROPE
COL_SK = COL_SQ + SWA_H * SWA_D
COL_SV = COL_SK + 2 * SWA_D
D_FF = 2816
FT = D_FF // P
NG = FT // 2
MLA_SCALE = float((MLA_NOPE + MLA_ROPE) ** -0.5)
SWA_SCALE = float(SWA_D ** -0.5)
NEG = -1.0e30

N_WIN = 20
ADA_AT = (1, 6, 7)
PACKS = [("win", t) for t in range(N_WIN)] + [("out", m) for m in range(KT)]
N_PRE = len(PACKS)
N_OUT0 = N_PRE - KT
WIN_AT = {PACKS[n][1]: n for n in range(N_PRE) if PACKS[n][0] == "win"}
ADA_FIRST = 2 * KT
ADA_TILES = 6 * KT
ADA_PACKS = 4 * KT
WIN_COLS = (
    [[(0, COL_SQ, 64), (64, COL_SQ + 128, 64)], [(0, COL_SQ + 64, 64), (64, COL_SQ + 192, 64)],
     [(0, COL_SK, 128)], [(0, COL_SV, 128)],
     [(0, COL_DT, 8), (64, COL_KR, 32), (96, COL_KR + 16, 16), (112, COL_KR, 16)]]
    + [[(0, COL_CQ + 128 * j, 128)] for j in range(2)] + [[(0, COL_CKV, 128)]]
    + [[(0, COL_XBC + 128 * j, 128)] for j in range(8)]
    + [[(0, COL_Z + 128 * j, 128)] for j in range(4)])
T_MISC, T_XBC, T_Z = 4, 8, 16


def pack_dmas(n):
    return len(WIN_COLS[PACKS[n][1]]) if PACKS[n][0] == "win" else 1


def loaded(n):
    return 16 * sum(pack_dmas(m) for m in range(n % 2, n + 1, 2))


R_N1, R_N2, R_ADAB, R_CW, R_CB, R_SN, R_QN, R_KN, R_END = 0, 8, 16, 64, 96, 104, 108, 110, 111
FR = 88


def build(nc, x, c, positions, ada_w, ada_b, norm1_g, norm2_g, w_in, ssd_conv_w, ssd_conv_b,
          ssd_dt_bias, ssd_a_log, ssd_d, ssd_norm_g, mla_q_norm_g, mla_w_uq, mla_kv_norm_g,
          mla_w_ukv, swa_sinks, w_out, ffn_w_up, ffn_conv_w, ffn_conv_b, ffn_w_down,
          final_norm_g, rope_consts, out):
    K = 1024
    base = 16512
    at = {"x": base, "h": base + 32 * K, "hl": base + 96 * K, "raw": base + 112 * K,
          "e": base + 120 * K, "f": base + 184 * K}

    def place(name, shape, dt, offset):
        return nc.alloc_sbuf_tensor_at(name, shape, dt, offset=offset)

    small_at = [at["f"] + 20 * K]

    def small(name, shape, dt=F32):
        n = int(np.prod(shape[1:])) * 4
        t = place(name, shape, dt, small_at[0])
        small_at[0] += (n + 31) // 32 * 32
        assert small_at[0] <= 229368, name
        return t

    xT = place("xT", [P, KT, T], F32, at["x"])
    hHi = place("hHi", [P, KT, T], F32R, at["h"])
    hLo = place("hLo", [P, KT, T], F32R, at["h"] + 32 * K)
    raw = [place(f"raw{s}", [P, 1024], F32, at["raw"] + 4 * K * s) for s in range(2)]
    wHi = [place(f"wHi{s}", [P, 1024], F32R, at["hl"] + 8 * K * s) for s in range(2)]
    wLo = [place(f"wLo{s}", [P, 1024], F32R, at["hl"] + 8 * K * s + 4 * K) for s in range(2)]
    nt = [place(f"nt{i}", [P, T], F32, at["f"] + 4 * K * i) for i in range(4)]
    cs = place("cs", [P, T], F32, at["f"] + 16 * K)
    E = [at["e"] + 4 * K * i for i in range(16)]
    X4 = at["x"] + 16 * K
    sq = place("swaQ", [P, 2, T], F32, E[0])
    sk = place("swaK", [P, T], F32, E[2])
    sv = place("swaV", [P, T], F32, E[3])
    misc = place("misc", [P, T], F32, E[4])
    cq = place("cq", [P, 2, T], F32, E[5])
    ckv = place("ckv", [P, T], F32, E[7])
    xbc = place("xbc", [P, 8, T], F32, E[8])
    zs = place("zs", [P, 4, T], F32, X4)
    sHi = place("swaHi", [P, 2, T], F32R, E[4])
    sLo = place("swaLo", [P, 2, T], F32R, E[6])
    mHi = place("mlaHi", [P, 2, T], F32R, E[0])
    mLo = place("mlaLo", [P, 2, T], F32R, E[2])
    yHi = place("ssdHi", [P, 4, T], F32R, E[12])
    yLo = place("ssdLo", [P, 4, T], F32R, E[8])
    adaE = [place(f"adaE{k}", [P, D], F32, E[8 + k]) for k in range(KT)]
    R = [at["h"] + 4 * K * i for i in range(16)]
    qh = [place(f"mlaQ{h}", [P, T], F32, R[h]) for h in range(4)]
    kh = [place(f"mlaK{h}", [P, T], F32, R[4 + h]) for h in range(4)]
    vt = place("mlaV", [P, NB, 256], F32, R[8])
    svt = place("swaVtok", [P, NB, P], F32, E[3])
    rt = place("ropeTmp", [P, T], F32, R[11])
    wuq = place("wuq", [P, 2, MLA_H, P], F32, at["f"] + 12 * K)
    wukv = place("wukv", [P, MLA_H, P], F32, at["f"] + 8 * K)
    otok = [place(f"otok{i}", [P, 256], F32, R[14] + K * i) for i in range(2)]
    stat = place("stat", [P, 3, 6, 4], F32, R[15])
    pr = [place(f"prob{i}", [P, T], F32, at["hl"] + 4 * K * i) for i in range(2)]
    pt = [place(f"probT{i}", [P, T], F32, at["hl"] + 8 * K + 4 * K * i) for i in range(2)]
    xd = place("xdt", [P, NB, 8, 64], F32, R[0])
    xe = place("xdtEnd", [P, NB, 8, 64], F32, R[4])
    bt = [place(f"Btok{g}", [P, NB, P], F32, R[8 + g]) for g in range(2)]
    Mt = [place(f"Mt{i}", [P, 4, P], F32, R[10] + 2 * K * i) for i in range(2)]
    Cs = [place(f"Cdec{i}", [P, 4, P], F32, R[11] + 2 * K * i) for i in range(2)]
    hst = [place(f"hstate{i}", [P, 8, 64], F32, R[12] + 2 * K * i) for i in range(2)]
    cbm = [place(f"cbm{i}", [P, P], F32, R[13] + 512 * i) for i in range(2)]
    sqc = [place(f"sqc{i}", [P, 4, P], F32, R[15] + 2 * K * i) for i in range(2)]
    adt = place("adt", [P, NB, 40], F32, R[14])
    aend = place("aend", [P, NB, 8], F32, R[14] + 1280)
    dec = place("dec", [P, NB, 8], F32, R[14] + 1280 + 256)
    dte = place("dte", [P, NB, 8], F32, R[14] + 1280 + 512)
    gHi = [[place(f"gHi{q}{k}", [P, T], F32R, E[4 * q + 2 * k]) for k in range(2)] for q in range(2)]
    gLo = [[place(f"gLo{q}{k}", [P, T], F32R, E[4 * q + 2 * k + 1]) for k in range(2)] for q in range(2)]
    ua = [place(f"ua{k}", [P, T], F32, E[8 + 2 * k]) for k in range(2)]
    ub = [place(f"ub{k}", [P, T], F32, E[9 + 2 * k]) for k in range(2)]
    ident = small("ident", [P, P])
    band = small("band", [P, 2, P])
    caus01 = small("caus01", [P, P])
    prm = small("prm", [P, R_END + 1])
    ffp = small("ffp", [P, 2 * FR])
    mod = small("mod", [P, ADA_TILES])
    scl = small("scl", [P, 2, KT])
    cact = small("cact", [P, KT])
    dcol = small("dcol", [P, 4])
    ropec = small("ropec", [P, 4])
    hp = small("hp", [8, 3])
    sink = small("sink", [P, SWA_H])
    eps = small("eps", [P, 1])
    rst = small("rst", [P, 16])
    fng = small("fng", [P, KT])

    bank = [nc.alloc_psum_tensor(f"bank{i}", [P, 1024], F32) for i in range(4)]

    def half(pair, i):
        return bank[pair][:, HALF * i:HALF * (i + 1)]

    xtail = nc.dram_tensor("xtail", [P, 4, T], F32, kind="Internal").ap()

    def sems(stack, names):
        return {n: stack.enter_context(nc.semaphore(n)) for n in names}

    def fview(t):
        return t.bitcast(F32)

    xin = [place(f"xin{i}", [P, D], F32, E[i]) for i in range(NB)]
    crow = place("crow", [8, P], F32, E[8])
    fnrow = place("fnrow", [8, P], F32, E[9])
    posi = place("posi", [P, T], I32, E[10])
    adaw = [place(f"adaw{i}", [P, D], F32, at["h"] + 4 * K * i) for i in range(2 * KT)]
    adas = [place(f"adas{g}", [P, D], F32, E[12 + g]) for g in range(2)]
    two_pi = 6.283185307179586
    parts, rest = [], two_pi
    for bits in (5, 13, 21):
        q = float(np.floor(rest * 2.0 ** bits) / 2.0 ** bits)
        parts.append(q)
        rest -= q
    parts.append(float(np.float32(rest)))
    with ExitStack() as st:
        s = sems(st, ["x_loaded", "small_loaded", "ident_ready", "pool_step", "x_transposed",
                      "x_copied_act", "x_copied_dve", "c_transposed", "c_act", "angle", "rope_sin",
                      "ada_loaded", "ada_done", "ada_sum", "dve_step"])
        with nc.Block() as block:

            @block.sync
            def _(sp):
                sp.dma_start(crow[:], c.rearrange("b (k p) -> (b k) p", p=P)).then_inc(s["small_loaded"], 16)
                sp.dma_start(fnrow[:], final_norm_g.rearrange("(k p) -> k p", p=P)).then_inc(s["small_loaded"], 16)
                sp.dma_start(ropec[:], rope_consts).then_inc(s["small_loaded"], 16)
                sp.dma_start(posi[64:128, :], positions.to_broadcast([64, T])).then_inc(s["small_loaded"], 16)
                for t in range(NB):
                    sp.dma_start(xin[t][:], x[0, t * P:(t + 1) * P, :]).then_inc(s["x_loaded"], 16)
                for i in range(2 * KT):
                    g, k = divmod(i, KT)
                    sp.dma_start(adaw[i][:], ada_w[0, k * P:(k + 1) * P, g * D:(g + 1) * D]).then_inc(s["ada_loaded"], 16)

            @block.gpsimd
            def _(pool):
                pool.memset(ident[:], 0.0).then_inc(s["pool_step"], 1)
                pool.memset(band[:], 0.0).then_inc(s["pool_step"], 1)
                pool.memset(caus01[:], 1.0).then_inc(s["pool_step"], 1)
                pool.memset(cs[0:64, :], 0.0).then_inc(s["pool_step"], 1)
                pool.memset(eps[:], EPS).then_inc(s["pool_step"], 1)
                pool.wait_ge(s["pool_step"], 5)
                pool.affine_select(out=ident[:], in_=ident[:], compare_op=ALU.not_equal, fill=1.0, base=0,
                                   pattern=[[-1, P]], channel_multiplier=1).then_inc(s["ident_ready"], 1)
                pool.affine_select(out=band[:, 0, :], in_=band[:, 0, :], compare_op=ALU.is_gt, fill=NEG, base=0,
                                   pattern=[[1, P]], channel_multiplier=-1).then_inc(s["ident_ready"], 1)
                pool.affine_select(out=band[:, 1, :], in_=band[:, 1, :], compare_op=ALU.is_ge, fill=NEG, base=0,
                                   pattern=[[-1, P]], channel_multiplier=1).then_inc(s["ident_ready"], 1)
                pool.affine_select(out=caus01[:], in_=caus01[:], compare_op=ALU.is_ge, fill=0.0, base=0,
                                   pattern=[[1, P]], channel_multiplier=-1).then_inc(s["ident_ready"], 1)

            @block.tensor
            def _(pe):
                pe.wait_ge(s["ident_ready"], 4)
                pe.wait_ge(s["small_loaded"], 64)
                pe.transpose(bank[3][:, 0:8], crow[:], ident[0:8, 0:8])
                pe.transpose(bank[3][:, 8:16], fnrow[:], ident[0:8, 0:8]).then_inc(s["c_transposed"], 1)
                pe.wait_ge(s["x_loaded"], 16 * NB)
                for t in range(NB):
                    if t >= 2:
                        pe.wait_ge(s["x_copied_act" if t % 2 == 0 else "x_copied_dve"], t // 2)
                    for k in range(KT):
                        mm = pe.transpose(bank[t % 2][:, k * P:(k + 1) * P], xin[t][:, k * P:(k + 1) * P], ident[:])
                    mm.then_inc(s["x_transposed"], 1)
                for g in range(2):
                    pe.wait_ge(s["ada_done"], KT * (g + 1))
                    for m in range(KT):
                        mm = pe.matmul(bank[2][:, g * KT + m:g * KT + m + 1], adas[g][:, m * P:(m + 1) * P], caus01[:, P - 1:P], start=True, stop=True)
                    mm.then_inc(s["ada_sum"], 1)

            def copy_x(eng, t, sem):
                eng.wait_ge(s["x_transposed"], t + 1)
                src = bank[t % 2][:].rearrange("p (k t) -> p k t", k=KT)
                dst = xT[:, :, t * P:(t + 1) * P]
                (eng.activation(dst, src, ACT.Copy) if sem == "x_copied_act" else eng.tensor_copy(dst, src)).then_inc(s[sem], 1)

            @block.scalar
            def _(act):
                act.wait_ge(s["c_transposed"], 1)
                act.activation(fng[:], bank[3][:, 8:16], ACT.Copy).then_inc(s["c_act"], 1)
                act.activation(cact[:], bank[3][:, 0:8], ACT.Silu).then_inc(s["c_act"], 1)
                act.wait_ge(s["angle"], 1)
                act.activation(nt[1][64:128, :], nt[0][64:128, :], ACT.Sin).then_inc(s["rope_sin"], 1)
                for t in range(0, NB, 2):
                    copy_x(act, t, "x_copied_act")

            @block.vector
            def _(dve):
                step = [0]

                def link(ins):
                    step[0] += 1
                    ins.then_inc(s["dve_step"], 1)
                    dve.wait_ge(s["dve_step"], step[0])

                lo, ang, k = slice(64, 128), nt[0], nt[1]
                dve.wait_ge(s["small_loaded"], 64)
                dve.wait_ge(s["ident_ready"], 4)
                link(dve.tensor_copy(nt[2][lo, :], posi[lo, :]))
                link(dve.tensor_scalar(ang[lo, :], nt[2][lo, :], ropec[lo, 0:1], None, ALU.mult))
                link(dve.tensor_scalar(k[lo, :], ang[lo, :], 1.0 / two_pi, ropec[lo, 1:2], ALU.mult, ALU.add))
                link(dve.tensor_scalar(k[lo, :], k[lo, :], 12582912.0, None, ALU.add))
                link(dve.tensor_scalar(k[lo, :], k[lo, :], -12582912.0, None, ALU.add))
                for q in parts:
                    link(dve.scalar_tensor_tensor(out=ang[lo, :], in0=k[lo, :], scalar=-q, in1=ang[lo, :],
                                                  op0=ALU.mult, op1=ALU.add))
                link(dve.tensor_scalar(ang[lo, :], ang[lo, :], ropec[lo, 2:3], None, ALU.add))
                dve.tensor_scalar(ang[lo, :], ang[lo, :], 3.1415925, -3.1415925, ALU.min, ALU.max).then_inc(s["angle"], 1)
                dve.wait_ge(s["rope_sin"], 1)
                dve.tensor_scalar(cs[lo, :], nt[1][lo, :], ropec[lo, 3:4], None, ALU.mult)
                for t in range(1, NB, 2):
                    copy_x(dve, t, "x_copied_dve")
                dve.wait_ge(s["c_act"], 2)
                dve.wait_ge(s["ada_loaded"], 16 * 2 * KT)
                for i in range(2 * KT):
                    g, k = divmod(i, KT)
                    if k == 0:
                        ins = dve.tensor_scalar(adas[g][:], adaw[i][:], cact[:, 0:1], None, ALU.mult)
                    else:
                        dve.wait_ge(s["ada_done"], i)
                        ins = dve.scalar_tensor_tensor(out=adas[g][:], in0=adaw[i][:], scalar=cact[:, k:k + 1], in1=adas[g][:],
                                                       op0=ALU.mult, op1=ALU.add)
                    ins.then_inc(s["ada_done"], 1)
                dve.wait_ge(s["ada_sum"], 2)
                dve.tensor_copy(mod[:, 0:ADA_FIRST], bank[2][:, 0:ADA_FIRST])

    names = """raw_loaded0 raw_loaded1 split_hi split_lo pack_used params_loaded uproj_loaded
        tail_saved tail_loaded params_transposed params_copied mod_first mod_rest ada_loaded0 ada_loaded1 ada_early ada_early_loaded0 ada_early_loaded1 ada_part ada_used ada_prod dve_step act_step
        n1_sq n1_acc n1_sum n1_rstd n1_spread n1_scaled n1_hi n1_lo
        n2_sq n2_acc n2_sum n2_rstd n2_spread n2_scaled n2_hi n2_lo
        pair_free0 pair_free1 conv_base conv_tap xbc_act
        misc_clear dt_abs dt_exp dt_sum dt_ln dt_ready
        mn_sq mn_sum mn_rstd mn_dve mp_full mp_q mp_kv rope_dve
        sw_vt sw_vcopied sw_s sw_m sw_n sw_e sw_t sw_ca sw_cd sw_o sw_x sw_y sw_hi sw_lo
        ml_s ml_n ml_e ml_t ml_ca ml_cd ml_o ml_x ml_y ml_hi ml_lo
        sd_xe sd_xe0 sd_t sd_c sd_xt sd_xd sd_bt sd_bc sd_cb sd_seg sd_dec sd_M sd_yd sd_eb sd_cs sd_st sd_y
        sd_h sd_sq sd_ss sd_rstd sd_spread sd_rd sd_hi sd_lo
        x_updated down_full down_free0 down_free1 up_base up_tap up_silu up_mul up_hi up_lo""".split()
    with nc.Fori(0, DEPTH) as layer, ExitStack() as st:
        s = sems(st, names)

        def of_layer(w):
            return w[bass.ds(layer, 1)]

        w_in_l, ada_l, out_l = of_layer(w_in), of_layer(ada_w), of_layer(w_out)
        assert DEPTH == 2
        ada_next = ada_w[bass.ds(1 - layer, 1)]
        up_l, down_l = of_layer(ffn_w_up), of_layer(ffn_w_down)

        def up_pack(G):
            return N_PRE if type(G) is int and G == 0 else N_PRE - 2 + 6 * G

        def down_pack(G):
            return N_PRE + 4 + 6 * G if type(G) is int and G == NG - 1 else N_PRE + 8 + 6 * G

        def run_mlp(eng, up, finish, down):
            up(0, 0, ("up", 1))
            finish(0, 0)
            up(1, 1, ("down", 0))
            finish(1, 1)
            down(0, 0, ("up", 2))
            up(2, 0, ("down", 1))
            finish(2, 0)
            down(1, 1, ("up", 3))
            with eng.Fori(0, (NG - 5) // 2) as i:
                for q in range(2):
                    G = 2 * i + (3 + q)
                    up(G, 1 - q, ("down", G - 1))
                    finish(G, 1 - q)
                    down(G - 1, q, ("up", G + 1))
            up(NG - 2, 1, ("down", NG - 3))
            finish(NG - 2, 1)
            down(NG - 3, 0, ("up", NG - 1))
            up(NG - 1, 0, ("down", NG - 2))
            finish(NG - 1, 0)
            down(NG - 2, 1, ("down", NG - 1))
            down(NG - 1, 0, None)

        def ada_at(j):
            return (half(3, 1) if j < 2 else half(3, 0))[:, 256 + KT * j:256 + KT * (j + 1)]

        def nothing(G, par):
            pass

        def copiers(u):
            if u >= 4 * MLA_H:
                return "ad"
            return "a" if u % 2 else "d"

        def copies_done(eng, u):
            for who, sem in (("a", "ml_ca"), ("d", "ml_cd")):
                n = sum(who in copiers(v) for v in range(u + 1))
                if n:
                    eng.wait_ge(s[sem], n)

        def ml_copy(eng, u, who, sem):
            if who not in copiers(u):
                return
            i = u // MLA_H
            a, b = (0, min(i + 1, 4)) if who == "a" or i < 4 else (4, i + 1)
            eng.wait_ge(s["ml_t"], u + 1)
            if u >= 2:
                eng.wait_ge(s["ml_o"], u - 1)
            else:
                eng.wait_ge(s["sw_o"], NB)
            src, dst = bank[2][:, a * P:b * P], pt[u % 2][:, a * P:b * P]
            (eng.activation(dst, src, ACT.Copy) if who == "a" else eng.tensor_copy(dst, src)).then_inc(s[sem], 1)

        with nc.Block() as block:
            @block.sync
            def _(sp):
                prow = nt[3]
                rows = [(norm1_g, R_N1, 8), (norm2_g, R_N2, 8), (ada_b, R_ADAB, 48), (ssd_conv_w, R_CW, 32),
                        (ssd_conv_b, R_CB, 8), (ssd_norm_g, R_SN, 4), (mla_q_norm_g, R_QN, 2), (mla_kv_norm_g, R_KN, 1)]
                load = lambda dst, src: sp.dma_start(dst, src).then_inc(s["params_loaded"], 16)
                for w, r, n in rows:
                    src = of_layer(w)
                    src = src.rearrange("o a (k p) -> (o a k) p", p=P) if len(w.shape) == 3 else src.rearrange("o (k p) -> (o k) p", p=P)
                    load(prow[r:r + n, 0:P], src)
                taps = of_layer(ffn_conv_w).rearrange("o a (k p) -> (o a k) p", p=P)
                load(prow[0:FR, P:2 * P], taps[0:FR])
                load(prow[0:132 - FR, 2 * P:3 * P], taps[FR:132])
                load(prow[132 - FR:FR, 2 * P:3 * P], of_layer(ffn_conv_b).rearrange("o (k p) -> (o k) p", p=P))
                for i, w in enumerate((ssd_dt_bias, ssd_a_log, ssd_d)):
                    load(hp[:, i:i + 1], of_layer(w).rearrange("o h -> h o"))
                load(sink[:], of_layer(swa_sinks).to_broadcast([P, SWA_H]))

                def load_pack(n, kind, m):
                    if n >= 2:
                        sp.wait_ge(s["split_hi"], n - 1)
                        sp.wait_ge(s["split_lo"], n - 1)
                    sem = s[f"raw_loaded{n % 2}"]
                    dst = raw[n % 2][:].rearrange("p (k m) -> p k m", k=KT)
                    if kind == "win":
                        w = w_in_l.rearrange("o (k p) m -> p (o k) m", p=P)
                        for a, b, width in WIN_COLS[m]:
                            sp.dma_start(dst[:, :, a:a + width], w[:, :, b:b + width]).then_inc(sem, 16)
                    else:
                        w = out_l.rearrange("o (k p) m -> p (o k) m", p=P)
                        sp.dma_start(dst, w[:, :, m * P:(m + 1) * P]).then_inc(sem, 16)

                def load_ada():
                    for r in range(ADA_PACKS):
                        j, k = 2 + r // KT, r % KT
                        if r < 2:
                            sp.wait_ge(s["split_hi"], N_WIN - 1 + r)
                            sp.wait_ge(s["split_lo"], N_WIN - 1 + r)
                        else:
                            sp.wait_ge(s["ada_used"], r - 1)
                        w, col = (ada_l, (j + 2) * D) if j < 4 else (ada_next, (j - 4) * D)
                        sp.dma_start(raw[r % 2][:], w[:, k * P:(k + 1) * P, col:col + D].rearrange("o p m -> (o p) m")).then_inc(s[f"ada_loaded{r % 2}"], 16)

                def load_early(j):
                    for k in range(KT):
                        if j:
                            sp.wait_ge(s["ada_early"], k + 1)
                        sp.dma_start(adaE[k][:], ada_l[:, k * P:(k + 1) * P, (j + 2) * D:(j + 3) * D].rearrange("o p m -> (o p) m")).then_inc(s[f"ada_early_loaded{j}"], 16)

                for n, (kind, m) in enumerate(PACKS):
                    if kind == "win" and m in (2, 4):
                        load_early(m // 2 - 1)
                    if kind == "win" and m == N_WIN - 2:
                        sp.wait_ge(s["dt_ready"], 1)
                        sp.wait_ge(s["mn_sum"], 1)
                        for k in range(2):
                            wq = of_layer(mla_w_uq)[:, k * P:(k + 1) * P, :].rearrange("o p (h d) -> p (o h) d", h=MLA_H)
                            sp.dma_start(wuq[:, k, :, 0:96], wq).then_inc(s["uproj_loaded"], 16)
                            sp.dma_start(wuq[:, k, :, 96:112], wq[:, :, 80:96]).then_inc(s["uproj_loaded"], 16)
                            sp.dma_start(wuq[:, k, :, 112:128], wq[:, :, 64:80]).then_inc(s["uproj_loaded"], 16)
                        sp.dma_start(wukv[:], of_layer(mla_w_ukv).rearrange("o p (h d) -> p (o h) d", h=MLA_H)).then_inc(s["uproj_loaded"], 16)
                    if kind == "win" and m == T_XBC:
                        sp.wait_ge(s["n1_lo"], KT)
                        sp.dma_start(xtail, xT[:, 4:8, :]).then_inc(s["tail_saved"], 16)
                    if n == N_OUT0:
                        load_ada()
                        sp.wait_ge(s["ada_used"], ADA_PACKS)
                    if n == N_OUT0 + 2:
                        sp.wait_ge(s["sd_y"], NB)
                        sp.dma_start(xT[:, 4:8, :], xtail).then_inc(s["tail_loaded"], 16)
                    load_pack(n, kind, m)

                def raw_free(n):
                    sp.wait_ge(s["split_hi"], n - 1)
                    sp.wait_ge(s["split_lo"], n - 1)

                def load_up(G, par, nxt):
                    for j in range(4):
                        raw_free(up_pack(G) + j)
                        col = ((j // 2) + (j % 2) * FT) * P + G * 2 * P
                        w = up_l.rearrange("o (k p) m -> p (o k) m", p=P)[:, :, bass.ds(col, P)]
                        sp.dma_start(raw[j % 2][:].rearrange("p (k m) -> p k m", k=KT), w).then_inc(s[f"raw_loaded{j % 2}"], 16)

                def load_down(G, par, nxt):
                    for j in range(2):
                        raw_free(down_pack(G) + j)
                        w = down_l[:, bass.ds(G * 2 * P, 2 * P), HALF * j:HALF * (j + 1)].rearrange("o (k p) m -> p (o k) m", p=P)
                        sp.dma_start(raw[j][:].rearrange("p (k m) -> p k m", k=2), w).then_inc(s[f"raw_loaded{j}"], 16)

                run_mlp(sp, load_up, nothing, load_down)

            def split(eng, slot, n, landed, *slot_free):
                if eng is nc.gpsimd:
                    eng.wait_ge(s["split_hi"], n + 1)
                eng.wait_ge(s[f"raw_loaded{slot}"], landed)
                for sem, v in slot_free:
                    eng.wait_ge(s[sem], v)
                if eng is nc.gpsimd:
                    eng.tensor_tensor(wLo[slot][:], raw[slot][:], fview(wHi[slot][:]), ALU.subtract).then_inc(s["split_lo"], 1)
                else:
                    eng.activation(wHi[slot][:], raw[slot][:], ACT.Copy).then_inc(s["split_hi"], 1)

            def split_pre(eng, n):
                if n == WIN_AT[T_MISC]:
                    eng.wait_ge(s["misc_clear"], 1)
                if n in (N_OUT0, N_OUT0 + 1):
                    split(eng, n % 2, n, loaded(n), ("ml_y", NB))
                elif n >= 2:
                    split(eng, n % 2, n, loaded(n), ("pack_used", n - 1))
                else:
                    split(eng, n % 2, n, loaded(n))

            def split_up(eng, G, j):
                landed = loaded(N_PRE - 2 + j % 2) + 16 * (3 * G + j // 2 + (1 if type(G) is int and G == 0 else 0))
                if type(G) is int and G < 2 and j < 2 or j >= 2:
                    free = ("pack_used", N_PRE + 4 * G + j - 1)
                else:
                    free = ("down_full", 8 * (G - 2) + 4 * (j + 1))
                split(eng, j % 2, up_pack(G) + j, landed, free)

            def split_down(eng, G, j):
                final = type(G) is int and G == NG - 1
                landed = loaded(N_PRE - 2 + j) + 16 * (3 * G + (3 if final else 5))
                free = ("down_full", 8 * (NG - 2) + 4 * (j + 1)) if final else ("pack_used", N_PRE + 4 * (G + 1) + 3 + j)
                split(eng, j, down_pack(G) + j, landed, free)

            @block.tensor
            def _(pe):
                mm = pe.matmul
                ones = caus01[:, P - 1:P]

                def dense_step(pair, k, w_hi, w_lo, r_hi, r_lo, first, last_k):
                    for q, (w, r) in enumerate(((w_hi, r_hi), (w_hi, r_lo), (w_lo, r_hi))):
                        for hf in range(2):
                            last = mm(half(pair, hf), w(k), r(k)[:, HALF * hf:HALF * (hf + 1)],
                                      start=first and q == 0, stop=last_k and q == 2)
                    return last

                def dense(pair, w_hi, w_lo, r_hi, r_lo, kts):
                    for k in range(kts):
                        last = dense_step(pair, k, w_hi, w_lo, r_hi, r_lo, k == 0, k == kts - 1)
                    return last

                def dense_two(n0, r_hi, r_lo, ks, k_ready):
                    for t, k in [(0, ks[0]), (0, ks[1])] + [(t, ks[i + 2 - 2 * t]) for i in range(KT - 2) for t in (0, 1)] + [(1, ks[-2]), (1, ks[-1])]:
                        if t == 0 and k in k_ready:
                            pe.wait_ge(s[k_ready[k][0]], k_ready[k][1])
                        if k == ks[0]:
                            pe.wait_ge(s["split_lo"], n0 + t + 1)
                        last = dense_step(t, k, tile_of(t, wHi), tile_of(t, wLo), r_hi, r_lo, k == ks[0], k == ks[-1])
                        if k == ks[-1]:
                            last.then_inc(s["pack_used"], 1)

                def tile_of(n, w):
                    return lambda k: w[n % 2][:, k * P:(k + 1) * P]

                def h_hi(k):
                    return hHi[:, k, :]

                def h_lo(k):
                    return hLo[:, k, :]

                def spread(out_, column):
                    return mm(out_, column.to_broadcast([P, P]), ident[:], start=True, stop=True)

                pe.wait_ge(s["params_loaded"], 16 * 15)
                pe.transpose(bank[3][:, 0:R_END], nt[3][0:R_END, 0:P], ident[0:R_END, 0:R_END])
                pe.transpose(bank[3][:, P:P + FR], nt[3][0:FR, P:2 * P], ident[0:FR, 0:FR])
                pe.transpose(bank[3][:, 2 * P:2 * P + FR], nt[3][0:FR, 2 * P:3 * P], ident[0:FR, 0:FR])
                for h in range(SSD_HEADS):
                    last = mm(bank[3][64 * (h % 2):64 * (h % 2) + 64, 3 * P + h // 2:3 * P + h // 2 + 1],
                              ident[0:8, h:h + 1].to_broadcast([8, 64]), hp[:, 2:3], start=True, stop=True)
                last.then_inc(s["params_transposed"], 1)

                def norm_sum(i):
                    pe.wait_ge(s[f"n{i}_acc"], KT - 1)
                    for b in range(NB):
                        last = mm(half(3, 1)[:, b:b + 1], nt[2][:, b * P:(b + 1) * P], ones, start=True, stop=True)
                    last.then_inc(s[f"n{i}_sum"], 1)
                    pe.wait_ge(s[f"n{i}_rstd"], 2)
                    for b in range(NB):
                        last = spread(bank[2][:, b * P:(b + 1) * P], rst[:, b:b + 1])
                    last.then_inc(s[f"n{i}_spread"], 1)

                def ada_sum(j):
                    pe.wait_ge(s["ada_early" if j < 2 else "ada_used"], KT * (j % 2 + 1 if j < 2 else j - 1))
                    for m in range(KT):
                        last = mm(ada_at(j)[:, m:m + 1], nt[(2 if j < 2 else 0) + j % 2][:, m * P:(m + 1) * P],
                                  caus01[:, P - 1:P], start=True, stop=True)
                    last.then_inc(s["ada_part"], 1)

                norm_sum(1)
                dense_two(0, h_hi, h_lo, range(KT), {k: ("n1_lo", k + 1) for k in range(KT)})
                for m in range(2, N_WIN):
                    pe.wait_ge(s["split_lo"], m + 1)
                    pe.wait_ge(s[f"pair_free{m % 2}"], m // 2)
                    dense(m % 2, tile_of(m, wHi), tile_of(m, wLo), h_hi, h_lo, KT).then_inc(s["pack_used"], 1)
                    if m == 4:
                        pe.wait_ge(s["params_copied"], 4)
                        ada_sum(0)
                        ada_sum(1)
                    if m == 13:
                        pe.wait_ge(s["mn_sq"], 3)
                        for b in range(NB):
                            for k in range(2):
                                mm(half(2, 0)[:, b:b + 1], nt[k][:, b * P:(b + 1) * P], ones, start=k == 0, stop=k == 1)
                            last = mm(half(2, 0)[:, NB + b:NB + b + 1], nt[2][:, b * P:(b + 1) * P], ones, start=True, stop=True)
                        last.then_inc(s["mn_sum"], 1)
                    if m == 15:
                        pe.wait_ge(s["mod_rest"], 1)
                        pe.wait_ge(s["mn_rstd"], 3)
                        for b in range(2 * NB):
                            last = spread(bank[2 + b // NB][:, (b % NB) * P:(b % NB + 1) * P], rst[:, b:b + 1])
                        last.then_inc(s["mn_sum"], 1)
                    if m == 17:
                        pe.wait_ge(s["mn_dve"], 3)
                        for b in range(NB):
                            last = pe.transpose(bank[3][:, b * P:(b + 1) * P], sv[:, b * P:(b + 1) * P], ident[:])
                        last.then_inc(s["sw_vt"], 1)
                pe.wait_ge(s["pair_free0"], 10)
                pe.wait_ge(s["pair_free1"], 10)

                pe.wait_ge(s["uproj_loaded"], 16 * 7)
                pe.wait_ge(s["sw_vcopied"], 1)
                for h in range(MLA_H):
                    for hf in range(2):
                        for k in range(2):
                            last = mm(half(h, hf), wuq[:, k, h, :], cq[:, k, HALF * hf:HALF * (hf + 1)], start=k == 0, stop=k == 1)
                    last.then_inc(s["mp_full"], 1)
                for h in range(MLA_H):
                    pe.wait_ge(s["mp_kv"], h + 1)
                    pe.wait_ge(s["mp_q"], 3 * (h + 1))
                    for hf in range(2):
                        last = mm(bank[h][0:64, HALF * hf:HALF * (hf + 1)], wukv[:, h, 0:64], ckv[:, HALF * hf:HALF * (hf + 1)], start=True, stop=True)
                    last.then_inc(s["mp_full"], 1)
                for u in range(2):
                    pe.wait_ge(s["mp_kv"], 7 + u)
                    for b in range(4 * u, 4 * u + 4):
                        last = mm(bank[2 + u][:, (b % 4) * 256:(b % 4 + 1) * 256], ckv[:, b * P:(b + 1) * P], wukv[:, :, 64:128],
                                  start=True, stop=True)
                    last.then_inc(s["mp_full"], 1)

                def sw_scores(i):
                    if i < 2:
                        pe.wait_ge(s["mp_kv"], 5 + i)
                    else:
                        pe.wait_ge(s["sw_m"], i - 1)
                    lo = max(i - 1, 0) * BLK
                    for h in range(SWA_H):
                        r = slice(64 * (h // 2), 64 * (h // 2) + 64)
                        o = bank[i % 2][:, h * 256 + (0 if i else BLK):(h + 1) * 256]
                        last = mm(o, sq[r, h % 2, i * BLK:(i + 1) * BLK], sk[r, lo:(i + 1) * BLK], start=True, stop=True)
                    last.then_inc(s["sw_s"], 1)

                def sw_transposes(i):
                    pe.wait_ge(s["sw_e"], i + 1)
                    if i == 0:
                        pe.wait_ge(s["mp_kv"], 10)
                    if i >= 1:
                        pe.wait_ge(s["sw_ca"], i)
                        pe.wait_ge(s["sw_cd"], i)
                    for h in range(SWA_H):
                        for b in range(0 if i else 1, 2):
                            q = (2 * h + b) * P
                            last = pe.transpose(bank[2][:, q:q + P], pr[i % 2][:, q:q + P], ident[:])
                    last.then_inc(s["sw_t"], 1)

                def sw_out(i):
                    pe.wait_ge(s["sw_ca"], i + 1)
                    pe.wait_ge(s["sw_cd"], i + 1)
                    if i >= 1:
                        pe.wait_ge(s["sw_x"], i)
                    if i == 4:
                        ada_sum(2)
                    for h in range(SWA_H):
                        for b in range(0 if i else 1, 2):
                            last = mm(half(3, 0)[:, h * 64:(h + 1) * 64], pt[i % 2][:, (2 * h + b) * P:(2 * h + b + 1) * P],
                                      svt[:, i - 1 + b, (h // 2) * 64:(h // 2) * 64 + 64], start=b == (0 if i else 1), stop=b == 1)
                    last.then_inc(s["sw_o"], 1)

                def to_features(i, x_sem, lo_sem, y_sem):
                    pe.wait_ge(s[x_sem], i + 1)
                    if i >= 1:
                        pe.wait_ge(s[lo_sem], i)
                    for k in range(2):
                        last = pe.transpose(half(3, 1)[:, k * P:(k + 1) * P], otok[i % 2][:, k * P:(k + 1) * P], ident[:])
                    last.then_inc(s[y_sem], 1)

                sw_scores(0)
                for i in range(NB):
                    if i + 1 < NB:
                        sw_scores(i + 1)
                    sw_transposes(i)
                    if i >= 1:
                        sw_out(i - 1)
                    if i >= 2:
                        to_features(i - 2, "sw_x", "sw_lo", "sw_y")
                sw_out(NB - 1)
                to_features(NB - 2, "sw_x", "sw_lo", "sw_y")
                to_features(NB - 1, "sw_x", "sw_lo", "sw_y")

                def ml_scores(u):
                    i, h = divmod(u, MLA_H)
                    if u < 2:
                        pe.wait_ge(s["sw_m"], NB - 1 + u)
                        pe.wait_ge(s["rope_dve"], 6)
                        pe.wait_ge(s["mp_q"], 12)
                    else:
                        pe.wait_ge(s["ml_e"], u - 1)
                    n = (i + 1) * BLK
                    for a in range(0, n, HALF):
                        b = min(a + HALF, n)
                        last = mm(bank[u % 2][:, a:b], qh[h][0:96, i * BLK:n], kh[h][0:96, a:b], start=True, stop=True)
                    last.then_inc(s["ml_s"], 1)

                def ml_transposes(u):
                    i = u // MLA_H
                    pe.wait_ge(s["ml_e"], u + 1)
                    if u >= 1:
                        copies_done(pe, u - 1)
                    else:
                        pe.wait_ge(s["sw_ca"], NB)
                        pe.wait_ge(s["sw_cd"], NB)
                    for b in range(i + 1):
                        last = pe.transpose(bank[2][:, b * P:(b + 1) * P], pr[u % 2][:, b * P:(b + 1) * P], ident[:])
                    last.then_inc(s["ml_t"], 1)

                def ml_out(u):
                    i, h = divmod(u, MLA_H)
                    copies_done(pe, u)
                    if h == 0:
                        pe.wait_ge(s["ml_x" if i else "sw_x"], i if i else NB)
                        if i in ADA_AT:
                            ada_sum(3 + ADA_AT.index(i))
                    for b in range(i + 1):
                        last = mm(half(3, 0)[:, h * 64:(h + 1) * 64], pt[u % 2][:, b * P:(b + 1) * P],
                                  vt[:, b, h * 64:(h + 1) * 64], start=b == 0, stop=b == i)
                    last.then_inc(s["ml_o"], 1)

                ml_scores(0)
                for u in range(4 * NB):
                    if u + 1 < 4 * NB:
                        ml_scores(u + 1)
                    ml_transposes(u)
                    if u == 0:
                        pe.wait_ge(s["sw_lo"], NB)
                    else:
                        ml_out(u - 1)
                    if u % 4 == 2 and u > 4:
                        to_features(u // 4 - 1, "ml_x", "ml_lo", "ml_y")
                ml_out(4 * NB - 1)
                to_features(NB - 1, "ml_x", "ml_lo", "ml_y")

                pe.wait_ge(s["dt_ready"], 1)
                pe.wait_ge(s["mod_rest"], 3)
                for b in range(NB):
                    last = pe.transpose(half(3, 0)[:, b * 40:(b + 1) * 40], cs[0:40, b * P:(b + 1) * P], ident[0:40, 0:40])
                last.then_inc(s["sd_t"], 1)
                pe.wait_ge(s["sd_c"], 1)
                pe.wait_ge(s["ml_lo"], NB)
                mm(half(3, 1)[:, 0:64], ident[:, P - 1:P].to_broadcast([P, P]), adt[:, :, 0:8], start=True, stop=True).then_inc(s["sd_t"], 1)
                for j in range(4):
                    if j < 2:
                        pe.wait_ge(s["ml_e"], 4 * NB)
                    else:
                        pe.wait_ge(s["sd_xd"], j - 1)
                    pe.wait_ge(s["xbc_act"], j + 1)
                    for b in range(NB):
                        last = pe.transpose(bank[j % 2][:, b * P:(b + 1) * P], xbc[:, j, b * P:(b + 1) * P], ident[:])
                    last.then_inc(s["sd_xt"], 1)
                pe.wait_ge(s["xbc_act"], 8)
                for g in range(2):
                    pe.wait_ge(s["sd_xd"], 3 + g)
                    for b in range(NB):
                        last = pe.transpose(bank[g][:, b * P:(b + 1) * P], xbc[:, 4 + g, b * P:(b + 1) * P], ident[:])
                    last.then_inc(s["sd_xt"], 1)

                def square_sums(ch):
                    pe.wait_ge(s["sd_sq"], ch + 1)
                    for g in range(2):
                        for k in range(2):
                            last = mm(half(2, 1)[:, 256 + NB * g + ch:257 + NB * g + ch], sqc[ch % 2][:, 2 * g + k, :], ones, start=k == 0, stop=k == 1)
                    last.then_inc(s["sd_ss"], 1)

                def sd_front(v):
                    ch, g = divmod(v, 2)
                    c0 = slice(ch * BLK, (ch + 1) * BLK)
                    if v < 2:
                        pe.wait_ge(s["sd_bt"], 2)
                        pe.wait_ge(s["sd_xe"], 4)
                    else:
                        pe.wait_ge(s["sd_eb"], v - 1)
                    for q in range(4):
                        h = 4 * g + q
                        last = mm(half(v % 2, 0)[:, q * P:(q + 1) * P], ident[0:8, h:h + 1].to_broadcast([8, P]), cs[0:8, c0],
                                  start=True, stop=True)
                    last.then_inc(s["sd_bc"], 1)
                    if v >= 2:
                        pe.wait_ge(s["sd_M"], v - 1)
                    if v % 2 and ch >= 4:
                        square_sums(ch - 4)
                    mm(half(2, v % 2)[:, 0:P], xbc[:, 4 + g, c0], xbc[:, 6 + g, c0], start=True, stop=True).then_inc(s["sd_cb"], 1)
                    if ch == NB - 1:
                        return
                    if g == 0 and ch >= 2:
                        pe.wait_ge(s["sd_h"], 2 * ch - 1)
                    mm(half(ch % 2, 1)[:, g * 256:(g + 1) * 256], bt[g][:, ch, :], xe[:, ch, 4 * g:4 * g + 4, :], start=True, stop=True).then_inc(s["sd_st"], 1)

                def sd_back(v):
                    ch, g = divmod(v, 2)
                    if g == 0:
                        pe.wait_ge(s["sd_h"], 1 + 2 * ch)
                        if ch >= 2:
                            pe.wait_ge(s["sd_y"], ch - 1)
                    pe.wait_ge(s["sd_M"], v + 1)
                    pe.wait_ge(s["sd_cs"], v + 1)
                    for q in range(4):
                        h = 4 * g + q
                        o = half(3, ch % 2)[64 * (h % 2):64 * (h % 2) + 64, (h // 2) * P:(h // 2 + 1) * P]
                        mm(o, xd[:, ch, h, :], Mt[v % 2][:, q, :], start=True, stop=False)
                        last = mm(o, hst[ch % 2][:, h, :], Cs[v % 2][:, q, :], start=False, stop=True)
                    last.then_inc(s["sd_yd"], 1)

                sd_front(0)
                sd_front(1)
                for v in range(2 * NB):
                    sd_back(v)
                    if v + 2 < 2 * NB:
                        sd_front(v + 2)
                pe.wait_ge(s["sd_M"], 2 * NB)
                for ch in range(NB - 4, NB):
                    square_sums(ch)
                y_hi = [yHi[:, j, :] for j in range(4)] + [mHi[:, j, :] for j in range(2)] + [sHi[:, j, :] for j in range(2)]
                y_lo = [yLo[:, j, :] for j in range(4)] + [mLo[:, j, :] for j in range(2)] + [sLo[:, j, :] for j in range(2)]
                pe.wait_ge(s["sd_rstd"], 2)
                for b in range(2 * NB):
                    last = spread(bank[2 + b // NB][:, (b % NB) * P:(b % NB + 1) * P], rst[:, b:b + 1])
                last.then_inc(s["sd_spread"], 1)
                pe.wait_ge(s["sd_h"], 2 * NB - 1)
                dense_two(N_OUT0, lambda k: y_hi[k], lambda k: y_lo[k], [4, 5, 6, 7, 0, 1, 2, 3], {k: ("sd_lo", k + 1) for k in range(4)})
                for m in range(2, KT):
                    n = N_OUT0 + m
                    pe.wait_ge(s["split_lo"], n + 1)
                    pe.wait_ge(s["x_updated"], m - 1)
                    dense(m % 2, tile_of(n, wHi), tile_of(n, wLo), lambda k: y_hi[k], lambda k: y_lo[k], KT).then_inc(s["pack_used"], 1)

                pe.wait_ge(s["x_updated"], KT)
                norm_sum(2)

                def up(G, par, nxt):
                    first = type(G) is int and G == 0
                    if first:
                        dense_two(N_PRE, h_hi, h_lo, range(KT), {k: ("n2_lo", k + 1) for k in range(KT)})
                    for j in range(2 if first else 0, 4):
                        pe.wait_ge(s["split_lo"], up_pack(G) + j + 1)
                        pe.wait_ge(s["up_tap"], 8 * G + 2 * j - 2)
                        dense(j % 2, tile_of(j, wHi), tile_of(j, wLo), h_hi, h_lo, KT).then_inc(s["pack_used"], 1)

                def down(G, par, nxt):
                    pe.wait_ge(s["up_lo"], 2 * G + 2)
                    for m in range(KT):
                        j, col = m // 4, (m % 4) * P
                        if m % 4 == 0:
                            pe.wait_ge(s["split_lo"], down_pack(G) + j + 1)
                        pe.wait_ge(s[f"down_free{m % 2}"], 4 * G + m // 2)
                        dense(2 + m % 2, lambda k: wHi[j][:, k * HALF + col:k * HALF + col + P],
                              lambda k: wLo[j][:, k * HALF + col:k * HALF + col + P],
                              lambda k: gHi[par][k][:], lambda k: gLo[par][k][:], 2).then_inc(s["down_full"], 1)

                run_mlp(pe, up, nothing, down)

            def run_splitter(eng, after_up, finish):
                def split_next(nxt, j):
                    if nxt is not None:
                        (split_up if nxt[0] == "up" else split_down)(eng, nxt[1], j)

                def up(G, par, nxt):
                    for j in range(4):
                        if j < 2:
                            split_up(eng, G, j + 2)
                        else:
                            split_next(nxt, j - 2)
                        after_up(G, par, j)

                def down(G, par, nxt):
                    for j in range(2):
                        split_next(nxt, j)

                run_mlp(eng, up, finish, down)

            @block.gpsimd
            def _(pool):
                def ada_products():
                    pool.wait_ge(s["mn_sum"], 1)
                    for r in range(ADA_PACKS):
                        j, k = divmod(r, KT)
                        acc, w = nt[j % 2][:], raw[r % 2][:]
                        pool.wait_ge(s[f"ada_loaded{r % 2}"], 16 * (r // 2 + 1))
                        ck = cact[:, k:k + 1].to_broadcast([P, D])
                        if k == 0:
                            if j >= 2:
                                pool.wait_ge(s["ada_part"], j + 1)
                            pool.tensor_tensor(acc, w, ck, ALU.mult).then_inc(s["ada_used"], 1)
                        else:
                            pool.tensor_tensor(w, w, ck, ALU.mult).then_inc(s["ada_prod"], 1)
                            pool.wait_ge(s["ada_prod"], r - j)
                            pool.wait_ge(s["ada_used"], r)
                            pool.tensor_tensor(acc, acc, w, ALU.add).then_inc(s["ada_used"], 1)

                for n in range(N_PRE):
                    if n == WIN_AT[T_MISC]:
                        pool.wait_ge(s["split_hi"], n - 1)
                        pool.wait_ge(s["split_lo"], n - 1)
                        pool.memset(raw[n % 2][:].rearrange("p (k m) -> p k m", k=KT)[:, :, 8:64], 0.0).then_inc(s["misc_clear"], 1)
                    if n == N_OUT0:
                        ada_products()
                    split_pre(pool, n)
                for j in range(2):
                    split_up(pool, 0, j)

                def g_lo(G, par, c):
                    pool.wait_ge(s["up_hi"], 2 * G + c + 1)
                    pool.tensor_tensor(gLo[par][c][:], ua[c][:], fview(gHi[par][c][:]), ALU.subtract).then_inc(s["up_lo"], 1)

                run_splitter(pool, lambda G, par, j: g_lo(G, par, 0) if j == 3 else None, lambda G, par: g_lo(G, par, 1))

            @block.scalar
            def _(act):
                A = act.activation

                def root(sums, dst, n, sum_sem, sem, count=1):
                    act.wait_ge(s[sum_sem], count)
                    A(dst, sums, ACT.Sqrt, bias=eps[:], scale=1.0 / n).then_inc(s[sem], 1)

                def norm_squares(i, k):
                    if i == 2:
                        act.wait_ge(s["x_updated"], k + 1)
                    if k >= 3:
                        act.wait_ge(s[f"n{i}_acc"], k - 2)
                    A(nt[2 if k == 0 else k % 2][:], xT[:, k, :], ACT.Square).then_inc(s[f"n{i}_sq"], 1)

                def norm_apply(i):
                    root(half(3, 1)[:, 0:NB], rst[:, 0:NB], D, f"n{i}_sum", f"n{i}_rstd")
                    for k in range(KT):
                        act.wait_ge(s[f"n{i}_scaled"], k + 1)
                        A(hHi[:, k, :], nt[k % 2][:], ACT.Identity, bias=mod[:, (i - 1) * 3 * KT + k:(i - 1) * 3 * KT + k + 1]).then_inc(s[f"n{i}_hi"], 1)

                act.wait_ge(s["params_transposed"], 1)
                A(prm[:, 0:R_END], bank[3][:, 0:R_END], ACT.Copy).then_inc(s["params_copied"], 1)
                A(ffp[:, 0:FR], bank[3][:, P:P + FR], ACT.Copy).then_inc(s["params_copied"], 1)
                A(ffp[:, FR:2 * FR], bank[3][:, 2 * P:2 * P + FR], ACT.Copy).then_inc(s["params_copied"], 1)
                A(dcol[:], bank[3][:, 3 * P:3 * P + 4], ACT.Copy).then_inc(s["params_copied"], 1)
                for n in range(2):
                    split_pre(act, n)
                for k in range(KT):
                    norm_squares(1, k)
                norm_apply(1)
                silu_due = [None]

                def silu_of(j):
                    act.wait_ge(s[f"pair_free{j % 2}"], (T_XBC + j) // 2 + 1)
                    A(xbc[:, j, :], xbc[:, j, :], ACT.Silu).then_inc(s["xbc_act"], 1)

                for n in range(N_WIN):
                    if n + 2 < N_WIN:
                        split_pre(act, n + 2)
                    m = n
                    if m == 12:
                        act.wait_ge(s["dt_ready"], 1)
                        for k, src in enumerate((cq[:, 0, :], cq[:, 1, :], ckv[:])):
                            A(nt[k][:], src, ACT.Square).then_inc(s["mn_sq"], 1)
                    if m == 15:
                        root(half(2, 0)[:, 0:NB], rst[:, 0:NB], MLA_QR, "mn_sum", "mn_rstd")
                        root(half(2, 0)[:, NB:2 * NB], rst[:, NB:2 * NB], MLA_KVR, "mn_sum", "mn_rstd")
                    if m == 19:
                        act.wait_ge(s["sw_vt"], 1)
                        A(svt[:], bank[3][:].rearrange("p (b d) -> p b d", b=NB), ACT.Copy).then_inc(s["sw_vcopied"], 1)
                    act.wait_ge(s["pack_used"], n + 1)
                    ps, free = bank[m % 2][:], s[f"pair_free{m % 2}"]
                    if m < T_XBC:
                        dst = ([sq[:, 0, :], sq[:, 1, :], sk[:], sv[:], misc[:], cq[:, 0, :], cq[:, 1, :], ckv[:]])[m]
                        A(dst, ps, ACT.Copy).then_inc(free, 1)
                        if m == T_MISC + 1:
                            act.wait_ge(s["pair_free0"], 3)
                            act.wait_ge(s["ada_part"], 2)
                            A(nt[0][0:8, :], misc[0:8, :], ACT.Abs, bias=hp[:, 0:1]).then_inc(s["dt_abs"], 1)
                            act.wait_ge(s["dt_abs"], 1)
                            A(nt[1][0:8, :], nt[0][0:8, :], ACT.Exp, scale=-1.0).then_inc(s["dt_exp"], 1)
                            A(hp[:, 1:2], hp[:, 1:2], ACT.Exp).then_inc(s["dt_exp"], 1)
                            act.wait_ge(s["dt_sum"], 1)
                            A(nt[3][0:8, :], nt[2][0:8, :], ACT.Ln).then_inc(s["dt_ln"], 1)
                    elif m < T_Z:
                        j = m - T_XBC
                        A(xbc[:, j, :], ps, ACT.Identity, bias=prm[:, R_CB + j:R_CB + j + 1],
                          scale=prm[:, R_CW + 24 + j:R_CW + 25 + j]).then_inc(s["conv_base"], 1)
                        if j >= 1:
                            silu_of(j - 1)
                    else:
                        if m == T_Z:
                            silu_of(7)
                            act.wait_ge(s["tail_saved"], 16)
                        A(zs[:, m - T_Z, :], ps, ACT.Silu).then_inc(free, 1)

                for h in range(MLA_H):
                    act.wait_ge(s["mp_full"], h + 1)
                    A(qh[h][0:64, :], bank[h][0:64, :], ACT.Copy).then_inc(s["mp_kv"], 1)
                for h in range(MLA_H):
                    act.wait_ge(s["mp_full"], 5 + h)
                    A(kh[h][0:64, :], bank[h][0:64, :], ACT.Copy).then_inc(s["mp_kv"], 1)
                for u in range(2):
                    act.wait_ge(s["mp_full"], 9 + u)
                    A(vt[:, 4 * u:4 * u + 4, :], bank[2 + u][:].rearrange("p (b d) -> p b d", b=4), ACT.Copy).then_inc(s["mp_kv"], 1)

                def y_hi(i, y_sem, hi_sem, dst):
                    act.wait_ge(s[y_sem], i + 1)
                    A(dst[:, :, i * BLK:(i + 1) * BLK], half(3, 1)[:, 0:256].rearrange("p (k t) -> p k t", k=2), ACT.Copy).then_inc(s[hi_sem], 1)

                def sw_exp(i):
                    act.wait_ge(s["sw_n"], i + 1)
                    st_ = stat[:, i % 3]
                    for h in range(SWA_H):
                        a = pr[i % 2][:, h * 256 + (0 if i else BLK):(h + 1) * 256]
                        A(a, a, ACT.Exp, bias=st_[:, 1, h:h + 1], accum_out=st_[:, 2, h:h + 1])
                    A(st_[:, 4, :], st_[:, 3, :], ACT.Exp).then_inc(s["sw_e"], 1)

                sw_exp(0)
                act.wait_ge(s["rope_dve"], 6)
                for i in range(NB):
                    if i + 1 < NB:
                        sw_exp(i + 1)
                    act.wait_ge(s["sw_t"], i + 1)
                    if i >= 2:
                        act.wait_ge(s["sw_o"], i - 1)
                    lo = 0 if i else 1
                    view = lambda t: t.rearrange("p (h b k) -> p h b k", h=2, b=2)[:, :, lo:2, :]
                    A(view(pt[i % 2][:, 0:HALF]), view(half(2, 0)), ACT.Copy).then_inc(s["sw_ca"], 1)
                    if i >= 2:
                        y_hi(i - 2, "sw_y", "sw_hi", sHi)
                y_hi(NB - 2, "sw_y", "sw_hi", sHi)
                y_hi(NB - 1, "sw_y", "sw_hi", sHi)

                def ml_exp(u):
                    i, h = divmod(u, MLA_H)
                    n = (i + 1) * BLK
                    act.wait_ge(s["ml_n"], u + 1)
                    if u < 2:
                        act.wait_ge(s["sw_t"], NB)
                    else:
                        act.wait_ge(s["ml_t"], u - 1)
                    A(pr[u % 2][:, 0:n], bank[u % 2][:, 0:n], ACT.Exp, bias=stat[:, i % 3, 1, h:h + 1],
                      scale=MLA_SCALE, accum_out=stat[:, i % 3, 2, h:h + 1]).then_inc(s["ml_e"], 1)

                ml_exp(0)
                for u in range(4 * NB):
                    if u + 1 < 4 * NB:
                        ml_exp(u + 1)
                    ml_copy(act, u, "a", "ml_ca")
                    if u % 4 == 3 and u > 4:
                        y_hi(u // 4 - 1, "ml_y", "ml_hi", mHi)
                y_hi(NB - 1, "ml_y", "ml_hi", mHi)

                def chunk_square(ch):
                    act.wait_ge(s["sd_y"], ch + 1)
                    if ch >= 2:
                        act.wait_ge(s["sd_ss"], ch - 1)
                    A(sqc[ch % 2][:], xbc[:, 0:4, ch * BLK:(ch + 1) * BLK], ACT.Square).then_inc(s["sd_sq"], 1)

                act.wait_ge(s["sd_t"], 1)
                A(adt[:], half(3, 0)[:, 0:320].rearrange("p (b r) -> p b r", b=NB), ACT.Copy).then_inc(s["sd_c"], 1)
                act.wait_ge(s["sd_t"], 2)
                A(aend[:], half(3, 1)[:, 0:64].rearrange("p (b r) -> p b r", b=NB), ACT.Copy).then_inc(s["sd_c"], 1)
                act.wait_ge(s["sd_c"], 2)
                A(dec[:], aend[:], ACT.Exp).then_inc(s["sd_c"], 1)
                act.wait_ge(s["sd_xe0"], 1)
                A(dte[:], dte[:], ACT.Exp).then_inc(s["sd_c"], 1)
                for g in range(2):
                    act.wait_ge(s["sd_xt"], 5 + g)
                    A(bt[g][:], bank[g][:].rearrange("p (b n) -> p b n", b=NB), ACT.Copy).then_inc(s["sd_bt"], 1)
                for v in range(2 * NB):
                    ch, g = divmod(v, 2)
                    act.wait_ge(s["sd_bc"], v + 1)
                    if v >= 2:
                        act.wait_ge(s["sd_yd"], v - 1)
                    for q in range(4):
                        h = 4 * g + q
                        last = A(Mt[v % 2][:, q, :], half(v % 2, 0)[:, q * P:(q + 1) * P], ACT.Relu, bias=adt[:, ch, h:h + 1], scale=-1.0)
                    last.then_inc(s["sd_seg"], 1)
                    A(Cs[v % 2][:], half(v % 2, 0).rearrange("p (q l) -> p q l", q=4), ACT.Exp).then_inc(s["sd_eb"], 1)
                    act.wait_ge(s["sd_seg"], v + 1)
                    A(Mt[v % 2][:], Mt[v % 2][:], ACT.Exp, scale=-1.0).then_inc(s["sd_dec"], 1)
                    if g and ch >= 2:
                        chunk_square(ch - 2)
                for n in range(2):
                    split_pre(act, N_OUT0 + n)
                for ch in (NB - 2, NB - 1):
                    chunk_square(ch)
                root(half(2, 1)[:, 256:256 + 2 * NB], rst[:], SSD_INNER // 2, "sd_ss", "sd_rstd", NB)
                for j in range(4):
                    act.wait_ge(s["sd_rd"], j + 1)
                    A(yHi[:, j, :], xbc[:, j, :], ACT.Copy).then_inc(s["sd_hi"], 1)

                for m in range(KT):
                    if m + 2 < KT:
                        split_pre(act, N_OUT0 + m + 2)
                    else:
                        split_up(act, 0, m + 2 - KT)
                    norm_squares(2, m)
                norm_apply(2)

                def after_up(G, par, j):
                    c, is_b = divmod(j, 2)
                    act.wait_ge(s["pack_used"], N_PRE + 4 * G + j + 1)
                    first = type(G) is int and G == 0
                    if not first:
                        act.wait_ge(s["up_mul" if is_b else "up_lo"], 2 * G - 1 + c)
                    col = 2 * G + c + is_b * FT
                    A((ub if is_b else ua)[c][:], bank[is_b][:], ACT.Identity, bias=ffp[:, bass.ds(col + 3 * 2 * FT, 1)],
                      scale=ffp[:, bass.ds(col + 2 * 2 * FT, 1)]).then_inc(s["up_base"], 1)
                    if is_b:
                        act.wait_ge(s["up_tap"], 8 * G + 4 * c + 2)
                        A(ua[c][:], ua[c][:], ACT.Silu).then_inc(s["up_silu"], 1)
                    if j == 2:
                        g_hi(G, par, 0)

                def g_hi(G, par, c):
                    act.wait_ge(s["up_mul"], 2 * G + c + 1)
                    if not (type(G) is int and G < 2):
                        act.wait_ge(s["down_full"], 8 * (G - 1))
                    A(gHi[par][c][:], ua[c][:], ACT.Copy).then_inc(s["up_hi"], 1)

                run_splitter(act, after_up, lambda G, par: g_hi(G, par, 1))

            @block.vector
            def _(dve):
                step = [0]

                def link(ins):
                    step[0] += 1
                    ins.then_inc(s["dve_step"], 1)
                    dve.wait_ge(s["dve_step"], step[0])

                def norm_adds(i, k):
                    dve.wait_ge(s[f"n{i}_sq"], k + 1)
                    if k >= 2:
                        dve.wait_ge(s[f"n{i}_acc"], k - 1)
                    dve.tensor_tensor(nt[2][:], nt[2][:], nt[k % 2][:], ALU.add).then_inc(s[f"n{i}_acc"], 1)

                def inverse(dst, sem):
                    dve.wait_ge(s[sem], 1)
                    dve.reciprocal(dst, dst).then_inc(s[sem], 1)

                def norm_apply(i):
                    inverse(rst[:, 0:NB], f"n{i}_rstd")
                    dve.wait_ge(s[f"n{i}_spread"], 1)
                    shift = (i - 1) * 3 * KT

                    def scaled(k):
                        if k >= 2:
                            dve.wait_ge(s[f"n{i}_lo"], k - 1)
                        dve.scalar_tensor_tensor(out=nt[k % 2][:], in0=xT[:, k, :], scalar=scl[:, i - 1, k:k + 1], in1=bank[2][:],
                                                 op0=ALU.mult, op1=ALU.mult).then_inc(s[f"n{i}_scaled"], 1)

                    scaled(0)
                    for k in range(KT):
                        if k + 1 < KT:
                            scaled(k + 1)
                        dve.wait_ge(s[f"n{i}_hi"], k + 1)
                        dve.scalar_tensor_tensor(out=hLo[:, k, :], in0=nt[k % 2][:], scalar=mod[:, shift + k:shift + k + 1],
                                                 in1=fview(hHi[:, k, :]), op0=ALU.add, op1=ALU.subtract).then_inc(s[f"n{i}_lo"], 1)

                for k in range(1, KT):
                    norm_adds(1, k)
                dve.wait_ge(s["params_copied"], 4)
                dve.tensor_tensor(mod[:, 0:ADA_FIRST], mod[:, 0:ADA_FIRST], prm[:, R_ADAB:R_ADAB + ADA_FIRST], ALU.add).then_inc(s["mod_first"], 1)
                dve.wait_ge(s["mod_first"], 1)
                link(dve.scalar_tensor_tensor(out=scl[:, 0, :], in0=mod[:, KT:2 * KT], scalar=1.0, in1=prm[:, R_N1:R_N1 + KT],
                                              op0=ALU.add, op1=ALU.mult))
                norm_apply(1)

                def dt_work():
                    dve.wait_ge(s["pair_free0"], 3)
                    n0, n1, n2, n3 = (t[0:8, :] for t in nt)
                    raw_dt = misc[0:8, :]
                    dve.wait_ge(s["dt_exp"], 2)
                    link(dve.tensor_scalar(hp[:, 1:2], hp[:, 1:2], -1.0, None, ALU.mult))
                    dve.tensor_scalar(n2, n1, 1.0, None, ALU.add).then_inc(s["dt_sum"], 1)
                    dve.wait_ge(s["dt_ln"], 1)
                    link(dve.tensor_scalar(n2, n2, -1.0, None, ALU.add))
                    link(dve.tensor_scalar(n0, n2, 0.0, None, ALU.is_equal))
                    link(dve.tensor_tensor(n2, n2, n0, ALU.add))
                    link(dve.reciprocal(n2, n2))
                    link(dve.tensor_tensor(n3, n3, n1, ALU.mult))
                    link(dve.tensor_tensor(n3, n3, n2, ALU.mult))
                    link(dve.tensor_tensor(n1, n1, n0, ALU.mult))
                    link(dve.tensor_tensor(n3, n3, n1, ALU.add))
                    link(dve.tensor_scalar(n0, raw_dt, hp[:, 0:1], 0.0, ALU.add, ALU.max))
                    link(dve.tensor_tensor(n2, n0, n3, ALU.add))
                    link(dve.tensor_copy(cs[32:40, :], n2))
                    link(dve.tensor_scalar(n1, n2, hp[:, 1:2], None, ALU.mult))
                    link(dve.tensor_scalar(n0, n2, 0.0, 1.0, ALU.mult, ALU.add))
                    for b in range(NB):
                        c0 = slice(b * BLK, (b + 1) * BLK)
                        last = dve.tensor_tensor_scan(cs[0:8, c0], n0[:, c0], n1[:, c0], 0.0, ALU.mult, ALU.add)
                    last.then_inc(s["dt_ready"], 1)

                for r in range(2 * KT):
                    j, k = divmod(r, KT)
                    acc = nt[2 + j]
                    if k == 0:
                        dve.wait_ge(s[f"ada_early_loaded{j}"], 16 * KT)
                        ins = dve.tensor_scalar(acc[:], adaE[k][:], cact[:, 0:1], None, ALU.mult)
                    else:
                        dve.wait_ge(s["ada_early"], r)
                        ins = dve.scalar_tensor_tensor(out=acc[:], in0=adaE[k][:], scalar=cact[:, k:k + 1], in1=acc[:],
                                                       op0=ALU.mult, op1=ALU.add)
                    ins.then_inc(s["ada_early"], 1)
                dve.wait_ge(s["ada_part"], 2)
                dve.tensor_tensor(mod[:, 2 * KT:4 * KT], half(3, 1)[:, 256:256 + 2 * KT], prm[:, R_ADAB + 2 * KT:R_ADAB + 4 * KT],
                                  ALU.add).then_inc(s["mod_rest"], 1)
                dt_work()
                for j in range(8):
                    if j == 7:
                        dve.wait_ge(s["mn_rstd"], 2)
                        dve.reciprocal(rst[:], rst[:]).then_inc(s["mn_rstd"], 1)
                    m = T_XBC + j
                    ps = bank[m % 2]
                    dve.wait_ge(s["conv_base"], j + 1)
                    for d in (1, 2, 3):
                        if d > 1:
                            dve.wait_ge(s["conv_tap"], 2 * j + d - 1)
                        col = R_CW + (3 - d) * 8 + j
                        ins = dve.scalar_tensor_tensor(out=xbc[:, j, d:T], in0=ps[:, 0:T - d], scalar=prm[:, col:col + 1],
                                                       in1=xbc[:, j, d:T], op0=ALU.mult, op1=ALU.add)
                        ins.then_inc(s["conv_tap"] if d < 3 else s[f"pair_free{m % 2}"], 1)

                dve.wait_ge(s["mn_sum"], 2)
                for k in range(2):
                    dve.scalar_tensor_tensor(out=cq[:, k, :], in0=cq[:, k, :], scalar=prm[:, R_QN + k:R_QN + k + 1], in1=bank[2][:],
                                             op0=ALU.mult, op1=ALU.mult).then_inc(s["mn_dve"], 1)
                dve.scalar_tensor_tensor(out=ckv[:], in0=ckv[:], scalar=prm[:, R_KN:R_KN + 1], in1=bank[3][:],
                                         op0=ALU.mult, op1=ALU.mult).then_inc(s["mn_dve"], 1)
                a, b = slice(64, 96), slice(96, 128)

                def rope(ins, n):
                    ins.then_inc(s["rope_dve"], 1)
                    dve.wait_ge(s["rope_dve"], n)

                rope(dve.tensor_tensor(misc[b, :], misc[b, :], cs[b, :], ALU.mult), 1)
                rope(dve.tensor_tensor(misc[a, :], misc[a, :], cs[a, :], ALU.mult), 2)
                dve.wait_ge(s["pack_used"], N_WIN)
                for h in range(MLA_H):
                    rope(dve.tensor_tensor(kh[h][a, :], misc[a, :], misc[b, :], ALU.add), 3 + h)
                for h in range(MLA_H):
                    dve.wait_ge(s["mp_full"], h + 1)
                    ps = bank[h]
                    if h:
                        dve.wait_ge(s["mp_q"], 3 * h)
                    dve.tensor_tensor(rt[a, :], ps[b, :], cs[b, :], ALU.mult).then_inc(s["mp_q"], 1)
                    dve.tensor_tensor(qh[h][a, :], ps[a, :], cs[a, :], ALU.mult).then_inc(s["mp_q"], 1)
                    dve.wait_ge(s["mp_q"], 3 * h + 2)
                    dve.tensor_tensor(qh[h][a, :], qh[h][a, :], rt[a, :], ALU.add).then_inc(s["mp_q"], 1)

                def sw_max(i):
                    dve.wait_ge(s["sw_s"], i + 1)
                    if i >= 2:
                        dve.wait_ge(s["sw_t"], i - 1)
                    lo = 0 if i else 1
                    p4 = pr[i % 2][:].rearrange("p (h b k) -> p h b k", h=4, b=2)
                    s4 = bank[i % 2][:].rearrange("p (h b k) -> p h b k", h=4, b=2)
                    st_ = stat[:, i % 3]
                    if i:
                        dve.scalar_tensor_tensor(out=p4.rearrange("p h b k -> p h (b k)"), in0=s4.rearrange("p h b k -> p h (b k)"), scalar=SWA_SCALE,
                                                 in1=band[:].rearrange("p b k -> p (b k)").unsqueeze(1).to_broadcast([P, 4, 2 * P]),
                                                 op0=ALU.mult, op1=ALU.add).then_inc(s["sw_m"], 1)
                    else:
                        dve.scalar_tensor_tensor(out=p4[:, :, 1, :], in0=s4[:, :, 1, :], scalar=SWA_SCALE,
                                                 in1=band[:, 1, :].unsqueeze(1).to_broadcast([P, 4, P]),
                                                 op0=ALU.mult, op1=ALU.add).then_inc(s["sw_m"], 1)
                    dve.wait_ge(s["sw_m"], i + 1)
                    src = p4.rearrange("p h b k -> p h (b k)") if i else p4[:, :, 1, :]
                    link(dve.tensor_reduce(st_[:, 0, :], src, AX.X, ALU.max))
                    link(dve.tensor_tensor(st_[:, 0, :], st_[:, 0, :], sink[:], ALU.max))
                    link(dve.tensor_scalar(st_[:, 1, :], st_[:, 0, :], -1.0, None, ALU.mult))
                    dve.tensor_tensor(st_[:, 3, :], st_[:, 1, :], sink[:], ALU.add).then_inc(s["sw_n"], 1)

                def sw_norm(i):
                    st_ = stat[:, i % 3]
                    dve.wait_ge(s["sw_e"], i + 1)
                    link(dve.tensor_tensor(st_[:, 5, :], st_[:, 2, :], st_[:, 4, :], ALU.add))
                    link(dve.reciprocal(st_[:, 5, :], st_[:, 5, :]))
                    normalise(i, "sw_o", i + 1, "sw_y", "sw_x")

                def normalise(i, o_sem, o_val, y_sem, x_sem):
                    dve.wait_ge(s[o_sem], o_val)
                    if i >= 2:
                        dve.wait_ge(s[y_sem], i - 1)
                    dve.tensor_tensor(otok[i % 2][:].rearrange("p (h d) -> p h d", h=4),
                                      half(3, 0)[:, 0:256].rearrange("p (h d) -> p h d", h=4),
                                      stat[:, i % 3, 5, :].unsqueeze(2).to_broadcast([P, 4, 64]), ALU.mult).then_inc(s[x_sem], 1)

                def y_lo(i, hi_sem, lo_sem, hi, lo):
                    dve.wait_ge(s[hi_sem], i + 1)
                    blk = slice(i * BLK, (i + 1) * BLK)
                    dve.tensor_tensor(lo[:, :, blk], half(3, 1)[:, 0:256].rearrange("p (k t) -> p k t", k=2),
                                      fview(hi[:, :, blk]), ALU.subtract).then_inc(s[lo_sem], 1)

                sw_max(0)
                for i in range(NB):
                    if i + 1 < NB:
                        sw_max(i + 1)
                    dve.wait_ge(s["sw_t"], i + 1)
                    if i >= 2:
                        dve.wait_ge(s["sw_o"], i - 1)
                    lo = 0 if i else 1
                    view = lambda t: t.rearrange("p (h b k) -> p h b k", h=2, b=2)[:, :, lo:2, :]
                    dve.tensor_copy(view(pt[i % 2][:, HALF:T]), view(half(2, 1))).then_inc(s["sw_cd"], 1)
                    if i >= 1:
                        sw_norm(i - 1)
                    if i >= 2:
                        y_lo(i - 2, "sw_hi", "sw_lo", sHi, sLo)
                sw_norm(NB - 1)
                y_lo(NB - 2, "sw_hi", "sw_lo", sHi, sLo)
                y_lo(NB - 1, "sw_hi", "sw_lo", sHi, sLo)

                def ml_max(u):
                    i, h = divmod(u, MLA_H)
                    n = (i + 1) * BLK
                    dve.wait_ge(s["ml_s"], u + 1)
                    diag = bank[u % 2][:, i * BLK:n]
                    link(dve.tensor_tensor(diag, diag, band[:, 1, :], ALU.add))
                    link(dve.tensor_reduce(stat[:, i % 3, 0, h:h + 1], bank[u % 2][:, 0:n], AX.X, ALU.max))
                    dve.tensor_scalar(stat[:, i % 3, 1, h:h + 1], stat[:, i % 3, 0, h:h + 1], -MLA_SCALE, None, ALU.mult).then_inc(s["ml_n"], 1)

                def ml_norm(i):
                    dve.wait_ge(s["ml_e"], 4 * i + 4)
                    link(dve.reciprocal(stat[:, i % 3, 5, :], stat[:, i % 3, 2, :]))
                    normalise(i, "ml_o", 4 * i + 4, "ml_y", "ml_x")

                ml_max(0)
                for u in range(4 * NB):
                    if u + 1 < 4 * NB:
                        ml_max(u + 1)
                    ml_copy(dve, u, "d", "ml_cd")
                    if u % 4 == 0 and u:
                        ml_norm(u // 4 - 1)
                    if u % 4 == 3 and u > 4:
                        y_lo(u // 4 - 1, "ml_hi", "ml_lo", mHi, mLo)
                ml_norm(NB - 1)
                dve.wait_ge(s["ada_part"], 6)
                dve.tensor_tensor(mod[:, 4 * KT:6 * KT], half(3, 0)[:, 256 + 2 * KT:256 + 4 * KT], prm[:, R_ADAB + 4 * KT:R_ADAB + 6 * KT],
                                  ALU.add).then_inc(s["mod_rest"], 1)
                dve.tensor_copy(mod[:, 0:2 * KT], half(3, 0)[:, 256 + 4 * KT:256 + 6 * KT]).then_inc(s["mod_rest"], 1)
                dve.wait_ge(s["mod_rest"], 3)
                link(dve.scalar_tensor_tensor(out=scl[:, 1, :], in0=mod[:, 4 * KT:5 * KT], scalar=1.0, in1=prm[:, R_N2:R_N2 + KT],
                                              op0=ALU.add, op1=ALU.mult))
                y_lo(NB - 1, "ml_hi", "ml_lo", mHi, mLo)

                dve.wait_ge(s["sd_c"], 2)
                dve.tensor_tensor(dte[:], aend[:], adt[:, :, 0:8], ALU.subtract).then_inc(s["sd_xe0"], 1)
                dve.memset(hst[0][:], 0.0).then_inc(s["sd_h"], 1)

                def x_end(j):
                    if j == 0:
                        dve.wait_ge(s["sd_c"], 4)
                    dve.wait_ge(s["sd_xd"], j + 1)
                    o = slice(2 * j, 2 * j + 2)
                    dve.tensor_tensor(xe[:, :, o, :], xd[:, :, o, :], dte[:, :, o].unsqueeze(3).to_broadcast([P, NB, 2, 64]), ALU.mult).then_inc(s["sd_xe"], 1)

                for j in range(4):
                    dve.wait_ge(s["sd_xt"], j + 1)
                    o = slice(2 * j, 2 * j + 2)
                    dve.tensor_tensor(xd[:, :, o, :], bank[j % 2][:].rearrange("p (b h d) -> p b h d", b=NB, h=2),
                                      adt[:, :, 32 + 2 * j:34 + 2 * j].unsqueeze(3).to_broadcast([P, NB, 2, 64]), ALU.mult).then_inc(s["sd_xd"], 1)
                    if j >= 1:
                        x_end(j - 1)
                x_end(3)

                def mix(v):
                    ch, g = divmod(v, 2)
                    dve.wait_ge(s["sd_cb"], v + 1)
                    link(dve.tensor_tensor(cbm[v % 2][:], half(2, v % 2)[:, 0:P], caus01[:], ALU.mult))
                    dve.wait_ge(s["sd_eb"], v + 1)
                    dve.tensor_tensor(Cs[v % 2][:], Cs[v % 2][:], xbc[:, 6 + g, ch * BLK:(ch + 1) * BLK].unsqueeze(1).to_broadcast([P, 4, P]),
                                      ALU.mult).then_inc(s["sd_cs"], 1)
                    dve.wait_ge(s["sd_dec"], v + 1)
                    dve.tensor_tensor(Mt[v % 2][:], Mt[v % 2][:], cbm[v % 2][:].unsqueeze(1).to_broadcast([P, 4, P]), ALU.mult).then_inc(s["sd_M"], 1)

                def next_state(ch):
                    old, new = hst[ch % 2], hst[(ch + 1) % 2]
                    if ch:
                        dve.wait_ge(s["sd_yd"], 2 * ch)
                    dve.wait_ge(s["sd_c"], 3)
                    dve.tensor_tensor(new[:], old[:], dec[:, ch, :].unsqueeze(2).to_broadcast([P, 8, 64]), ALU.mult).then_inc(s["sd_h"], 1)
                    dve.wait_ge(s["sd_h"], 2 + 2 * ch)
                    dve.wait_ge(s["sd_st"], 2 * ch + 2)
                    dve.tensor_tensor(new[:], new[:], half(ch % 2, 1).rearrange("p (h d) -> p h d", h=8), ALU.add).then_inc(s["sd_h"], 1)

                def chunk_out(ch):
                    c0 = slice(ch * BLK, (ch + 1) * BLK)
                    dve.wait_ge(s["sd_yd"], 2 * ch + 2)
                    for j in range(4):
                        last = dve.scalar_tensor_tensor(out=xbc[:, j, c0], in0=xbc[:, j, c0], scalar=dcol[:, j:j + 1],
                                                        in1=half(3, ch % 2)[:, j * P:(j + 1) * P], op0=ALU.mult, op1=ALU.add)
                    link(last)
                    dve.tensor_tensor(xbc[:, 0:4, c0], xbc[:, 0:4, c0], zs[:, :, c0], ALU.mult).then_inc(s["sd_y"], 1)

                for v in range(2 * NB):
                    mix(v)
                    if v % 2:
                        if v // 2 < NB - 1:
                            next_state(v // 2)
                        if v > 1:
                            chunk_out(v // 2 - 1)
                chunk_out(NB - 1)
                inverse(rst[:], "sd_rstd")
                dve.wait_ge(s["sd_spread"], 1)
                def ssd_scaled(j):
                    dve.scalar_tensor_tensor(out=xbc[:, j, :], in0=xbc[:, j, :], scalar=prm[:, R_SN + j:R_SN + j + 1],
                                             in1=bank[2 + j // 2][:], op0=ALU.mult, op1=ALU.mult).then_inc(s["sd_rd"], 1)

                ssd_scaled(0)
                for j in range(4):
                    if j < 3:
                        ssd_scaled(j + 1)
                    dve.wait_ge(s["sd_hi"], j + 1)
                    dve.tensor_tensor(yLo[:, j, :], xbc[:, j, :], fview(yHi[:, j, :]), ALU.subtract).then_inc(s["sd_lo"], 1)

                for m in range(KT):
                    dve.wait_ge(s["pack_used"], N_OUT0 + m + 1)
                    if m == 4:
                        dve.wait_ge(s["tail_loaded"], 16)
                    dve.scalar_tensor_tensor(out=xT[:, m, :], in0=bank[m % 2][:], scalar=mod[:, 2 * KT + m:2 * KT + m + 1],
                                             in1=xT[:, m, :], op0=ALU.mult, op1=ALU.add).then_inc(s["x_updated"], 1)
                    if m >= 2:
                        norm_adds(2, m - 1)
                norm_adds(2, KT - 1)
                norm_apply(2)

                due = []

                def tap(G, j, d):
                    c, is_b = divmod(j, 2)
                    y = (ub if is_b else ua)[c]
                    if d == 2:
                        dve.wait_ge(s["up_tap"], 8 * G + 2 * j + 1)
                    col = 2 * G + c + is_b * FT + (2 - d) * 2 * FT
                    dve.scalar_tensor_tensor(out=y[:, d:T], in0=bank[is_b][:, 0:T - d], scalar=ffp[:, bass.ds(col, 1)],
                                             in1=y[:, d:T], op0=ALU.mult, op1=ALU.add).then_inc(s["up_tap"], 1)

                def gate(G, c):
                    dve.wait_ge(s["up_silu"], 2 * G + c + 1)
                    dve.wait_ge(s["up_tap"], 8 * G + 4 * c + 4)
                    dve.tensor_tensor(ua[c][:], ua[c][:], ub[c][:], ALU.mult).then_inc(s["up_mul"], 1)

                def up(G, par, nxt):
                    for j in range(4):
                        dve.wait_ge(s["up_base"], 4 * G + j + 1)
                        tap(G, j, 1)
                        if j == 3 and nxt[0] == "down":
                            due.append(G)
                            continue
                        tap(G, j, 2)
                        if j % 2:
                            gate(G, j // 2)

                def down(G, par, nxt):
                    for m in range(KT):
                        dve.wait_ge(s["down_full"], 8 * G + m + 1)
                        if not (type(G) is int and G == 0):
                            dve.wait_ge(s[f"down_free{m % 2}"], 4 * (G - 1) + m // 2 + 1)
                        dve.scalar_tensor_tensor(out=xT[:, m, :], in0=bank[2 + m % 2][:], scalar=mod[:, 5 * KT + m:5 * KT + m + 1],
                                                 in1=xT[:, m, :], op0=ALU.mult, op1=ALU.add).then_inc(s[f"down_free{m % 2}"], 1)
                        if due and m == 0:
                            tap(due[0], 3, 2)
                        elif due and m == 1:
                            gate(due.pop(), 1)

                run_mlp(dve, up, nothing, down)

        with nc.Block() as block:
            @block.sync
            def _(sp):
                for name in names:
                    sp.sem_clear(s[name])

    xout = [place(f"xout{i}", [P, D], F32, E[i]) for i in range(4)]
    with ExitStack() as st:
        s = sems(st, ["sq", "acc", "sum", "sqrt", "recip", "normed", "transposed", "copied_act", "copied_dve", "out_written"])
        with nc.Block() as block:
            def copy_out(eng, t, sem):
                eng.wait_ge(s["transposed"], t + 1)
                if t >= 4:
                    eng.wait_ge(s["out_written"], 16 * (t - 3))
                src, dst = bank[t % 4][:], xout[t % 4][:]
                (eng.activation(dst, src, ACT.Copy) if sem == "copied_act" else eng.tensor_copy(dst, src)).then_inc(s[sem], 1)

            @block.scalar
            def _(act):
                for k in range(KT):
                    if k >= 3:
                        act.wait_ge(s["acc"], k - 2)
                    act.activation(nt[2 if k == 0 else k % 2][:], xT[:, k, :], ACT.Square).then_inc(s["sq"], 1)
                act.wait_ge(s["sum"], 1)
                act.activation(nt[3][:], bank[1][:], ACT.Sqrt, bias=eps[:], scale=1.0 / D).then_inc(s["sqrt"], 1)
                for t in range(0, NB, 2):
                    copy_out(act, t, "copied_act")

            @block.vector
            def _(dve):
                for k in range(1, KT):
                    dve.wait_ge(s["sq"], k + 1)
                    if k >= 2:
                        dve.wait_ge(s["acc"], k - 1)
                    dve.tensor_tensor(nt[2][:], nt[2][:], nt[k % 2][:], ALU.add).then_inc(s["acc"], 1)
                dve.wait_ge(s["sqrt"], 1)
                dve.reciprocal(nt[3][:], nt[3][:]).then_inc(s["recip"], 1)
                dve.wait_ge(s["recip"], 1)
                for k in range(KT):
                    dve.scalar_tensor_tensor(out=xT[:, k, :], in0=xT[:, k, :], scalar=fng[:, k:k + 1], in1=nt[3][:],
                                             op0=ALU.mult, op1=ALU.mult).then_inc(s["normed"], 1)
                for t in range(1, NB, 2):
                    copy_out(dve, t, "copied_dve")

            @block.tensor
            def _(pe):
                pe.wait_ge(s["acc"], KT - 1)
                for hf in range(2):
                    last = pe.matmul(half(1, hf), caus01[:, P - 1:P].to_broadcast([P, P]), nt[2][:, HALF * hf:HALF * (hf + 1)], start=True, stop=True)
                last.then_inc(s["sum"], 1)
                pe.wait_ge(s["sqrt"], 1)
                for t in range(NB):
                    if t >= 4:
                        pe.wait_ge(s["copied_act" if t % 2 == 0 else "copied_dve"], (t - 4) // 2 + 1)
                    for k in range(KT):
                        if t == 0:
                            pe.wait_ge(s["normed"], k + 1)
                        last = pe.transpose(bank[t % 4][:, k * P:(k + 1) * P], xT[:, k, t * P:(t + 1) * P], ident[:])
                    last.then_inc(s["transposed"], 1)

            @block.sync
            def _(sp):
                for t in range(NB):
                    sp.wait_ge(s["copied_act" if t % 2 == 0 else "copied_dve"], t // 2 + 1)
                    if t:
                        sp.wait_ge(s["out_written"], 16 * t)
                    sp.dma_start(out[0, t * P:(t + 1) * P, :], xout[t % 4][:]).then_inc(s["out_written"], 16)
                sp.wait_ge(s["out_written"], 16 * NB)


_INS = ["x", "c", "positions", "ada_w", "ada_b", "norm1_g", "norm2_g", "w_in", "ssd_conv_w", "ssd_conv_b",
        "ssd_dt_bias", "ssd_a_log", "ssd_d", "ssd_norm_g", "mla_q_norm_g", "mla_w_uq", "mla_kv_norm_g",
        "mla_w_ukv", "swa_sinks", "w_out", "ffn_w_up", "ffn_conv_w", "ffn_conv_b", "ffn_w_down", "final_norm_g"]


def rope_constants():
    k = np.zeros((P, 4), np.float32)
    inv = np.float32(10000.0) ** (-np.arange(0, MLA_ROPE, 2, dtype=np.float32) / np.float32(MLA_ROPE))
    k[64:, 0] = np.tile(inv, 4)
    k[64:96, 1], k[64:96, 2] = 0.25, np.pi / 2
    k[:, 3] = 1.0
    k[96:112, 3] = -1.0
    return k


def kernel(**inputs):
    import numpy as _np
    import concourse.bacc as _bacc
    from concourse import mybir as _mybir
    from concourse.bass_utils import run_bass_kernel_spmd as _run

    nc = _bacc.Bacc("TRN2", target_bir_lowering=False, num_devices=1)
    arrays, args = {}, []
    held = [(n, inputs[n]) for n in _INS] + [("rope_consts", rope_constants())]
    for name, a in held:
        a = _np.ascontiguousarray(a)
        arrays[f"in_{name}_dram"] = a
        args.append(nc.dram_tensor(f"in_{name}_dram", a.shape, _mybir.dt.from_np(a.dtype), kind="ExternalInput").ap())
    args.append(nc.dram_tensor("out_0_dram", (1, T, D), F32, kind="ExternalOutput").ap())
    build(nc, *args)
    r = _run(nc, [arrays], core_ids=[0])
    return r.results[0]["out_0_dram"]
```

```python
from contextlib import ExitStack

import numpy as np
import concourse.bass as bass
from concourse import mybir

F32 = mybir.dt.float32
F32R = mybir.dt.float32r
I32 = mybir.dt.int32
ALU = mybir.AluOpType
ACT = mybir.ActivationFunctionType
AX = mybir.AxisListType

P = 128
T = 1024
D = 1024
KT = D // P
DEPTH = 2
EPS = 1e-6
HALF = 512
BLK = 128
NB = T // BLK

SSD_HEADS, SSD_INNER, SSD_XBC = 8, 512, 1024
MLA_H, MLA_NOPE, MLA_ROPE, MLA_V = 4, 64, 32, 64
MLA_QR, MLA_KVR = 256, 128
SWA_H, SWA_D = 4, 64
COL_Z, COL_XBC = 0, SSD_INNER
COL_DT = COL_XBC + SSD_XBC
COL_CQ = COL_DT + SSD_HEADS
COL_CKV = COL_CQ + MLA_QR
COL_KR = COL_CKV + MLA_KVR
COL_SQ = COL_KR + MLA_ROPE
COL_SK = COL_SQ + SWA_H * SWA_D
COL_SV = COL_SK + 2 * SWA_D
D_FF = 2816
FT = D_FF // P
NG = FT // 2
MLA_SCALE = float((MLA_NOPE + MLA_ROPE) ** -0.5)
SWA_SCALE = float(SWA_D ** -0.5)
NEG = -1.0e30

N_WIN = 20
ADA_AT = (1, 6, 7)
PACKS = [("win", t) for t in range(N_WIN)] + [("out", m) for m in range(KT)]
N_PRE = len(PACKS)
N_ALL = N_PRE + 6 * NG
N_OUT0 = N_PRE - KT
WIN_AT = {PACKS[n][1]: n for n in range(N_PRE) if PACKS[n][0] == "win"}
ADA_FIRST = 2 * KT
ADA_TILES = 6 * KT
ADA_PACKS = 4 * KT
WIN_COLS = (
    [[(0, COL_SQ, 64), (64, COL_SQ + 128, 64)], [(0, COL_SQ + 64, 64), (64, COL_SQ + 192, 64)],
     [(0, COL_SK, 128)], [(0, COL_SV, 128)],
     [(0, COL_DT, 8), (64, COL_KR, 32), (96, COL_KR + 16, 16), (112, COL_KR, 16)]]
    + [[(0, COL_CQ + 128 * j, 128)] for j in range(2)] + [[(0, COL_CKV, 128)]]
    + [[(0, COL_XBC + 128 * j, 128)] for j in range(8)]
    + [[(0, COL_Z + 128 * j, 128)] for j in range(4)])
T_MISC, T_XBC, T_Z = 4, 8, 16


def pack_dmas(n):
    return len(WIN_COLS[PACKS[n][1]]) if PACKS[n][0] == "win" else 1


AHEAD = 2


def loaded(n):
    return 16 * sum(pack_dmas(m) for m in range(AHEAD + n % 2, n + 1, 2))


def splits(n):
    return n + 1 - AHEAD


UNITS = [(i, hs) for i in range(NB) for hs in (((0, 1), (2, 3)) if (i + 1) * BLK <= HALF else ((0,), (1,), (2,), (3,)))]
NU = len(UNITS)
UNIT_END = [1 + max(u for u in range(NU) if UNITS[u][0] == i) for i in range(NB)]
UNIT_FIRST = [0] + UNIT_END[:-1]

R_N1, R_N2, R_ADAB, R_CW, R_CB, R_SN, R_QN, R_KN, R_END = 0, 8, 16, 64, 96, 104, 108, 110, 111
FR = 88


def build(nc, x, c, positions, ada_w, ada_b, norm1_g, norm2_g, w_in, ssd_conv_w, ssd_conv_b,
          ssd_dt_bias, ssd_a_log, ssd_d, ssd_norm_g, mla_q_norm_g, mla_w_uq, mla_kv_norm_g,
          mla_w_ukv, swa_sinks, w_out, ffn_w_up, ffn_conv_w, ffn_conv_b, ffn_w_down,
          final_norm_g, rope_consts, out):
    K = 1024
    base = 16512
    at = {"x": base, "h": base + 32 * K, "hl": base + 96 * K, "raw": base + 112 * K,
          "e": base + 120 * K, "f": base + 184 * K}

    def place(name, shape, dt, offset):
        return nc.alloc_sbuf_tensor_at(name, shape, dt, offset=offset)

    small_at = [at["f"] + 20 * K]

    def small(name, shape, dt=F32):
        n = int(np.prod(shape[1:])) * 4
        t = place(name, shape, dt, small_at[0])
        small_at[0] += (n + 31) // 32 * 32
        assert small_at[0] <= 229368, name
        return t

    xT = place("xT", [P, KT, T], F32, at["x"])
    hHi = place("hHi", [P, KT, T], F32R, at["h"])
    hLo = place("hLo", [P, KT, T], F32R, at["h"] + 32 * K)
    raw = [place(f"raw{s}", [P, 1024], F32, at["raw"] + 4 * K * s) for s in range(2)]
    wHi = [place(f"wHi{s}", [P, 1024], F32R, at["hl"] + 8 * K * s) for s in range(2)]
    wLo = [place(f"wLo{s}", [P, 1024], F32R, at["hl"] + 8 * K * s + 4 * K) for s in range(2)]
    nt = [place(f"nt{i}", [P, T], F32, at["f"] + 4 * K * i) for i in range(4)]
    cs = place("cs", [P, T], F32, at["f"] + 16 * K)
    E = [at["e"] + 4 * K * i for i in range(16)]
    X4 = at["x"] + 16 * K
    sq = place("swaQ", [P, 2, T], F32, E[0])
    sk = place("swaK", [P, T], F32, E[2])
    sv = place("swaV", [P, T], F32, E[3])
    misc = place("misc", [P, T], F32, E[4])
    cq = place("cq", [P, 2, T], F32, E[5])
    ckv = place("ckv", [P, T], F32, E[7])
    xbc = place("xbc", [P, 8, T], F32, E[8])
    zs = place("zs", [P, 4, T], F32, X4)
    sHi = place("swaHi", [P, 2, T], F32R, E[4])
    sLo = place("swaLo", [P, 2, T], F32R, E[6])
    mHi = place("mlaHi", [P, 2, T], F32R, E[0])
    mLo = place("mlaLo", [P, 2, T], F32R, E[2])
    yHi = place("ssdHi", [P, 4, T], F32R, E[12])
    yLo = place("ssdLo", [P, 4, T], F32R, E[8])
    adaE = [place(f"adaE{k}", [P, D], F32, E[8 + k]) for k in range(KT)]
    R = [at["h"] + 4 * K * i for i in range(16)]
    qh = [place(f"mlaQ{h}", [P, T], F32, R[h]) for h in range(4)]
    kh = [place(f"mlaK{h}", [P, T], F32, R[4 + h]) for h in range(4)]
    vt = place("mlaV", [P, NB, 256], F32, R[8])
    svt = place("swaVtok", [P, NB, P], F32, E[3])
    rt = place("ropeTmp", [P, T], F32, R[11])
    wuq = place("wuq", [P, 2, MLA_H, P], F32, at["f"] + 12 * K)
    wukv = place("wukv", [P, MLA_H, P], F32, at["f"] + 8 * K)
    otok = [place(f"otok{i}", [P, 256], F32, R[14] + K * i) for i in range(2)]
    stat = place("stat", [P, 3, 6, 4], F32, R[15])
    pr = [place(f"prob{i}", [P, T], F32, at["hl"] + 4 * K * i) for i in range(2)]
    pt = [place(f"probT{i}", [P, T], F32, at["hl"] + 8 * K + 4 * K * i) for i in range(2)]
    xd = place("xdt", [P, NB, 8, 64], F32, R[0])
    xe = place("xdtEnd", [P, NB, 8, 64], F32, R[4])
    bt = [place(f"Btok{g}", [P, NB, P], F32, R[8 + g]) for g in range(2)]
    Mt = [place(f"Mt{i}", [P, 4, P], F32, R[10] + 2 * K * i) for i in range(2)]
    Cs = [place(f"Cdec{i}", [P, 4, P], F32, R[11] + 2 * K * i) for i in range(2)]
    hst = [place(f"hstate{i}", [P, 8, 64], F32, R[12] + 2 * K * i) for i in range(2)]
    cbm = [place(f"cbm{i}", [P, P], F32, R[13] + 512 * i) for i in range(2)]
    sqc = [place(f"sqc{i}", [P, 4, P], F32, R[15] + 2 * K * i) for i in range(2)]
    adt = place("adt", [P, NB, 40], F32, R[14])
    aend = place("aend", [P, NB, 8], F32, R[14] + 1280)
    dec = place("dec", [P, NB, 8], F32, R[14] + 1280 + 256)
    dte = place("dte", [P, NB, 8], F32, R[14] + 1280 + 512)
    gHi = [[place(f"gHi{q}{k}", [P, T], F32R, E[4 * q + 2 * k]) for k in range(2)] for q in range(2)]
    gLo = [[place(f"gLo{q}{k}", [P, T], F32R, E[4 * q + 2 * k + 1]) for k in range(2)] for q in range(2)]
    ua = [place(f"ua{k}", [P, T], F32, E[8 + 2 * k]) for k in range(2)]
    ub = [place(f"ub{k}", [P, T], F32, E[9 + 2 * k]) for k in range(2)]
    ident = small("ident", [P, P])
    band = small("band", [P, 2, P])
    caus01 = small("caus01", [P, P])
    prm = small("prm", [P, R_END + 1])
    ffp = small("ffp", [P, 2 * FR])
    mod = small("mod", [P, ADA_TILES])
    scl = small("scl", [P, 2, KT])
    cact = small("cact", [P, KT])
    dcol = small("dcol", [P, 4])
    ropec = small("ropec", [P, 4])
    hp = small("hp", [8, 3])
    sink = small("sink", [P, SWA_H])
    eps = small("eps", [P, 1])
    rst = small("rst", [P, 16])

    bank = [nc.alloc_psum_tensor(f"bank{i}", [P, 1024], F32) for i in range(4)]

    def half(pair, i):
        return bank[pair][:, HALF * i:HALF * (i + 1)]

    xtail = nc.dram_tensor("xtail", [P, 4, T], F32, kind="Internal").ap()

    def sems(stack, names):
        return {n: stack.enter_context(nc.semaphore(n)) for n in names}

    def fview(t):
        return t.bitcast(F32)

    prow = place("paramRows", [P, 3 * P], F32, E[14])

    def load_params(sp, of_layer):
        rows = [(norm1_g, R_N1, 8), (norm2_g, R_N2, 8), (ada_b, R_ADAB, 48), (ssd_conv_w, R_CW, 32),
                (ssd_conv_b, R_CB, 8), (ssd_norm_g, R_SN, 4), (mla_q_norm_g, R_QN, 2), (mla_kv_norm_g, R_KN, 1)]
        load = lambda dst, src: sp.dma_start(dst, src).then_inc(s["params_loaded"], 16)
        for w, r, n in rows:
            src = of_layer(w)
            src = src.rearrange("o a (k p) -> (o a k) p", p=P) if len(w.shape) == 3 else src.rearrange("o (k p) -> (o k) p", p=P)
            load(prow[r:r + n, 0:P], src)
        taps = of_layer(ffn_conv_w).rearrange("o a (k p) -> (o a k) p", p=P)
        load(prow[0:FR, P:2 * P], taps[0:FR])
        load(prow[0:132 - FR, 2 * P:3 * P], taps[FR:132])
        load(prow[132 - FR:FR, 2 * P:3 * P], of_layer(ffn_conv_b).rearrange("o (k p) -> (o k) p", p=P))
        for i, w in enumerate((ssd_dt_bias, ssd_a_log, ssd_d)):
            load(hp[:, i:i + 1], of_layer(w).rearrange("o h -> h o"))
        load(sink[:], of_layer(swa_sinks).to_broadcast([P, SWA_H]))

    def transpose_params(pe):
        pe.wait_ge(s["params_loaded"], 16 * 15)
        pe.transpose(bank[1][:, 0:R_END], prow[0:R_END, 0:P], ident[0:R_END, 0:R_END])
        pe.transpose(bank[1][:, P:P + FR], prow[0:FR, P:2 * P], ident[0:FR, 0:FR])
        pe.transpose(bank[1][:, 2 * P:2 * P + FR], prow[0:FR, 2 * P:3 * P], ident[0:FR, 0:FR])
        for h in range(SSD_HEADS):
            last = pe.matmul(bank[1][64 * (h % 2):64 * (h % 2) + 64, 3 * P + h // 2:3 * P + h // 2 + 1],
                             ident[0:8, h:h + 1].to_broadcast([8, 64]), hp[:, 2:3], start=True, stop=True)
        last.then_inc(s["params_transposed"], 1)

    def copy_params(act):
        act.wait_ge(s["params_transposed"], 1)
        act.activation(prm[:, 0:R_END], bank[1][:, 0:R_END], ACT.Copy).then_inc(s["params_copied"], 1)
        act.activation(ffp[:, 0:FR], bank[1][:, P:P + FR], ACT.Copy).then_inc(s["params_copied"], 1)
        act.activation(ffp[:, FR:2 * FR], bank[1][:, 2 * P:2 * P + FR], ACT.Copy).then_inc(s["params_copied"], 1)
        act.activation(dcol[:], bank[1][:, 3 * P:3 * P + 4], ACT.Copy).then_inc(s["params_copied"], 1)

    def first_modulation(dve):
        dve.wait_ge(s["params_copied"], 4)
        dve.tensor_tensor(mod[:, 0:ADA_FIRST], mod[:, 0:ADA_FIRST], prm[:, R_ADAB:R_ADAB + ADA_FIRST], ALU.add).then_inc(s["mod_first"], 1)
        dve.wait_ge(s["mod_first"], 1)
        dve.scalar_tensor_tensor(out=scl[:, 0, :], in0=mod[:, KT:2 * KT], scalar=1.0, in1=prm[:, R_N1:R_N1 + KT],
                                 op0=ALU.add, op1=ALU.mult).then_inc(s["mod_first"], 1)

    def load_win(sp, w_l, slot, m, sem):
        w = w_l.rearrange("o (k p) m -> p (o k) m", p=P)
        for a, b, width in WIN_COLS[m]:
            sp.dma_start(raw[slot][:].rearrange("p (k m) -> p k m", k=KT)[:, :, a:a + width], w[:, :, b:b + width]).then_inc(sem, 16)

    def split_ahead(eng, n):
        if eng is nc.gpsimd:
            eng.wait_ge(s["next_hi"], n + 1)
            eng.tensor_tensor(wLo[n][:], raw[n][:], fview(wHi[n][:]), ALU.subtract).then_inc(s["next_lo"], 1)
        else:
            eng.wait_ge(s[f"next_loaded{n}"], 16 * len(WIN_COLS[n]))
            eng.activation(wHi[n][:], raw[n][:], ACT.Copy).then_inc(s["next_hi"], 1)

    def spread(pe, out_, column):
        return pe.matmul(out_, column.to_broadcast([P, P]), ident[:], start=True, stop=True)

    def spread_rms(pe, sem):
        pe.wait_ge(s[f"{sem}_rstd"], 2)
        for b in range(NB):
            last = spread(pe, bank[2][:, b * P:(b + 1) * P], rst[:, b:b + 1])
        last.then_inc(s[f"{sem}_spread"], 1)

    xin = [place(f"xin{i}", [P, D], F32, E[i]) for i in range(NB)]
    crow = place("crow", [8, P], F32, E[8])
    posi = place("posi", [P, T], I32, E[10])
    adaw = [place(f"adaw{i}", [P, D], F32, at["h"] + 4 * K * i) for i in range(2 * KT)]
    adas = [place(f"adas{g}", [P, D], F32, E[(12, 13, 15)[g]]) for g in range(3)]
    two_pi = 6.283185307179586
    parts, rest = [], two_pi
    for bits in (5, 13, 21):
        q = float(np.floor(rest * 2.0 ** bits) / 2.0 ** bits)
        parts.append(q)
        rest -= q
    parts.append(float(np.float32(rest)))
    with ExitStack() as st:
        s = sems(st, ["x_loaded", "small_loaded", "ident_ready", "pool_step", "x_transposed",
                      "x_copied_act", "x_copied_dve", "c_transposed", "c_act", "angle", "rope_sin",
                      "ada_loaded0", "ada_loaded1", "ada_loaded2", "ada_loaded3", "ada_done", "ada_sum", "dve_step", "params_loaded", "params_transposed", "params_copied", "mod_first",
                      "next_loaded0", "next_loaded1", "next_hi", "next_lo", "n1_sq", "n1_rstd", "n1_spread"])
        with nc.Block() as block:

            @block.sync
            def _(sp):
                sp.dma_start(crow[:], c.rearrange("b (k p) -> (b k) p", p=P)).then_inc(s["small_loaded"], 16)
                sp.dma_start(ropec[:], rope_consts).then_inc(s["small_loaded"], 16)
                sp.dma_start(posi[64:128, :], positions.to_broadcast([64, T])).then_inc(s["small_loaded"], 16)
                def load_adaw(i):
                    g, k = divmod(i, KT)
                    sp.dma_start(adaw[i][:], ada_w[0, k * P:(k + 1) * P, g * D:(g + 1) * D]).then_inc(s[f"ada_loaded{i // 4}"], 16)

                for i in range(4):
                    load_adaw(i)
                for t in range(NB):
                    sp.dma_start(xin[t][:], x[0, t * P:(t + 1) * P, :]).then_inc(s["x_loaded"], 16)
                load_params(sp, lambda w: w[0:1])
                for i in range(4, 2 * KT):
                    load_adaw(i)
                for n in range(AHEAD):
                    load_win(sp, w_in[0:1], n, n, s[f"next_loaded{n}"])


            @block.gpsimd
            def _(pool):
                pool.memset(ident[:], 0.0).then_inc(s["pool_step"], 1)
                pool.memset(band[:], 0.0).then_inc(s["pool_step"], 1)
                pool.memset(caus01[:], 1.0).then_inc(s["pool_step"], 1)
                pool.memset(cs[0:64, :], 0.0).then_inc(s["pool_step"], 1)
                pool.memset(eps[:], EPS).then_inc(s["pool_step"], 1)
                pool.wait_ge(s["pool_step"], 5)
                pool.affine_select(out=ident[:], in_=ident[:], compare_op=ALU.not_equal, fill=1.0, base=0,
                                   pattern=[[-1, P]], channel_multiplier=1).then_inc(s["ident_ready"], 1)
                pool.affine_select(out=band[:, 0, :], in_=band[:, 0, :], compare_op=ALU.is_gt, fill=NEG, base=0,
                                   pattern=[[1, P]], channel_multiplier=-1).then_inc(s["ident_ready"], 1)
                pool.affine_select(out=band[:, 1, :], in_=band[:, 1, :], compare_op=ALU.is_ge, fill=NEG, base=0,
                                   pattern=[[-1, P]], channel_multiplier=1).then_inc(s["ident_ready"], 1)
                pool.affine_select(out=caus01[:], in_=caus01[:], compare_op=ALU.is_ge, fill=0.0, base=0,
                                   pattern=[[1, P]], channel_multiplier=-1).then_inc(s["ident_ready"], 1)
                pool.wait_ge(s["c_act"], 1)
                pool.wait_ge(s["ada_loaded0"], 16 * 4)
                acc = adas[2][:]
                for k in range(4):
                    w, ck = adaw[k][:], cact[:, k:k + 1].to_broadcast([P, D])
                    pool.tensor_tensor(w if k else acc, w, ck, ALU.mult).then_inc(s["pool_step"], 1)
                    if k:
                        pool.wait_ge(s["pool_step"], 5 + 2 * k)
                        pool.tensor_tensor(acc, acc, w, ALU.add).then_inc(s["pool_step"], 1)
                for n in range(AHEAD):
                    split_ahead(pool, n)

            @block.tensor
            def _(pe):
                pe.wait_ge(s["ident_ready"], 4)
                pe.wait_ge(s["small_loaded"], 48)
                pe.transpose(bank[3][:, 0:8], crow[:], ident[0:8, 0:8]).then_inc(s["c_transposed"], 1)
                pe.wait_ge(s["x_loaded"], 16 * NB)
                for t in range(NB):
                    if t >= 2:
                        pe.wait_ge(s["x_copied_act" if t % 2 == 0 else "x_copied_dve"], t // 2)
                    for k in range(KT):
                        mm = pe.transpose(bank[t % 2][:, k * P:(k + 1) * P], xin[t][:, k * P:(k + 1) * P], ident[:])
                    mm.then_inc(s["x_transposed"], 1)
                pe.wait_ge(s["x_copied_dve"], 4)
                transpose_params(pe)
                pe.wait_ge(s["pool_step"], 5 + 7)
                pe.wait_ge(s["ada_done"], 4)
                for g in range(2):
                    if g:
                        pe.wait_ge(s["ada_done"], 12)
                    parts_ = (adas[2], adas[0]) if g == 0 else (adas[1],)
                    for m in range(KT):
                        for n, a in enumerate(parts_):
                            mm = pe.matmul(bank[3][:, 16 + g * KT + m:17 + g * KT + m], a[:, m * P:(m + 1) * P], caus01[:, P - 1:P],
                                           start=n == 0, stop=n == len(parts_) - 1)
                mm.then_inc(s["ada_sum"], 1)
                spread_rms(pe, "n1")

            def copy_x(eng, t, sem):
                eng.wait_ge(s["x_transposed"], t + 1)
                src = bank[t % 2][:].rearrange("p (k t) -> p k t", k=KT)
                dst = xT[:, :, t * P:(t + 1) * P]
                (eng.activation(dst, src, ACT.Copy) if sem == "x_copied_act" else eng.tensor_copy(dst, src)).then_inc(s[sem], 1)

            @block.scalar
            def _(act):
                act.wait_ge(s["c_transposed"], 1)
                act.activation(cact[:], bank[3][:, 0:8], ACT.Silu).then_inc(s["c_act"], 1)
                act.wait_ge(s["angle"], 1)
                act.activation(nt[1][64:128, :], nt[0][64:128, :], ACT.Sin).then_inc(s["rope_sin"], 1)
                for t in range(0, NB, 2):
                    copy_x(act, t, "x_copied_act")
                for t in range(NB):
                    if t:
                        act.wait_ge(s["n1_sq"], t)
                    act.activation(nt[3][:], xin[t][:], ACT.Square, accum_out=rst[:, t:t + 1]).then_inc(s["n1_sq"], 1)
                act.wait_ge(s["n1_sq"], NB)
                act.activation(rst[:, 0:NB], rst[:, 0:NB], ACT.Sqrt, bias=eps[:], scale=1.0 / D).then_inc(s["n1_rstd"], 1)
                copy_params(act)
                for n in range(AHEAD):
                    split_ahead(act, n)

            @block.vector
            def _(dve):
                step = [0]

                def link(ins):
                    step[0] += 1
                    ins.then_inc(s["dve_step"], 1)
                    dve.wait_ge(s["dve_step"], step[0])

                lo, ang, k = slice(64, 128), nt[0], nt[1]
                dve.wait_ge(s["small_loaded"], 48)
                dve.wait_ge(s["ident_ready"], 4)
                link(dve.tensor_copy(nt[2][lo, :], posi[lo, :]))
                link(dve.tensor_scalar(ang[lo, :], nt[2][lo, :], ropec[lo, 0:1], None, ALU.mult))
                link(dve.tensor_scalar(k[lo, :], ang[lo, :], 1.0 / two_pi, ropec[lo, 1:2], ALU.mult, ALU.add))
                link(dve.tensor_scalar(k[lo, :], k[lo, :], 12582912.0, None, ALU.add))
                link(dve.tensor_scalar(k[lo, :], k[lo, :], -12582912.0, None, ALU.add))
                for q in parts:
                    link(dve.scalar_tensor_tensor(out=ang[lo, :], in0=k[lo, :], scalar=-q, in1=ang[lo, :],
                                                  op0=ALU.mult, op1=ALU.add))
                link(dve.tensor_scalar(ang[lo, :], ang[lo, :], ropec[lo, 2:3], None, ALU.add))
                dve.tensor_scalar(ang[lo, :], ang[lo, :], 3.1415925, -3.1415925, ALU.min, ALU.max).then_inc(s["angle"], 1)
                dve.wait_ge(s["rope_sin"], 1)
                dve.tensor_scalar(cs[lo, :], nt[1][lo, :], ropec[lo, 3:4], None, ALU.mult)
                for t in range(1, NB, 2):
                    copy_x(dve, t, "x_copied_dve")
                dve.wait_ge(s["c_act"], 1)
                for n, i in enumerate(range(4, 2 * KT)):
                    g, k = divmod(i, KT)
                    if i % 4 == 0:
                        dve.wait_ge(s[f"ada_loaded{i // 4}"], 16 * 4)
                    if k in (0, 4) and i != 12:
                        ins = dve.tensor_scalar(adas[g][:], adaw[i][:], cact[:, k:k + 1], None, ALU.mult)
                    else:
                        dve.wait_ge(s["ada_done"], n)
                        ins = dve.scalar_tensor_tensor(out=adas[g][:], in0=adaw[i][:], scalar=cact[:, k:k + 1], in1=adas[g][:],
                                                       op0=ALU.mult, op1=ALU.add)
                    ins.then_inc(s["ada_done"], 1)
                dve.wait_ge(s["n1_rstd"], 1)
                dve.reciprocal(rst[:, 0:NB], rst[:, 0:NB]).then_inc(s["n1_rstd"], 1)
                dve.wait_ge(s["ada_sum"], 1)
                link(dve.tensor_copy(mod[:, 0:ADA_FIRST], bank[3][:, 16:16 + ADA_FIRST]))
                first_modulation(dve)

    names = """next_loaded0 next_loaded1 next_hi next_lo raw_loaded0 raw_loaded1 split_hi split_lo pack_used params_loaded uproj_loaded
        tail_saved tail_loaded params_transposed params_copied mod_first mod_rest ada_loaded0 ada_loaded1 ada_early ada_early_loaded0 ada_early_loaded1 ada_part ada_used ada_prod dve_step
        n1_sq n1_acc n1_sum n1_rstd n1_spread n1_scaled n1_hi n1_lo
        n2_sq n2_acc n2_sum n2_rstd n2_spread n2_scaled n2_hi n2_lo
        pair_free0 pair_free1 conv_base conv_tap xbc_act
        misc_clear dt_abs dt_exp dt_sum dt_ln dt_ready
        mn_sq mn_sum mn_rstd mn_dve mp_full mp_q mp_kv rope_dve
        sw_vt sw_vcopied sw_s sw_m sw_n sw_e sw_t sw_ca sw_cd sw_o sw_x sw_y sw_hi sw_lo
        ml_s ml_n ml_e ml_t ml_ca ml_cd ml_o ml_x ml_y ml_hi ml_lo
        sd_xe sd_xe0 sd_t sd_c sd_xt sd_xd sd_bt sd_bc sd_cb sd_seg sd_dec sd_M sd_yd sd_yd_read sd_eb sd_cs sd_st sd_y
        sd_h sd_sq sd_ss sd_rstd sd_spread sd_rd sd_hi sd_lo
        x_updated down_full down_free0 down_free1 up_base up_tap up_silu up_mul up_hi up_lo""".split()
    with nc.Fori(0, DEPTH) as layer, ExitStack() as st:
        s = sems(st, names)

        def of_layer(w):
            return w[bass.ds(layer, 1)]

        def of_next(w):
            return w[bass.ds(1 - layer, 1)]

        w_in_l, ada_l, out_l = of_layer(w_in), of_layer(ada_w), of_layer(w_out)
        assert DEPTH == 2
        ada_next = of_next(ada_w)
        up_l, down_l = of_layer(ffn_w_up), of_layer(ffn_w_down)

        def up_pack(G):
            return N_PRE if type(G) is int and G == 0 else N_PRE - 2 + 6 * G

        def down_pack(G):
            return N_PRE + 4 + 6 * G if type(G) is int and G == NG - 1 else N_PRE + 8 + 6 * G

        def run_mlp(eng, up, finish, down):
            up(0, 0, ("up", 1))
            finish(0, 0)
            up(1, 1, ("down", 0))
            finish(1, 1)
            down(0, 0, ("up", 2))
            up(2, 0, ("down", 1))
            finish(2, 0)
            down(1, 1, ("up", 3))
            with eng.Fori(0, (NG - 5) // 2) as i:
                for q in range(2):
                    G = 2 * i + (3 + q)
                    up(G, 1 - q, ("down", G - 1))
                    finish(G, 1 - q)
                    down(G - 1, q, ("up", G + 1))
            up(NG - 2, 1, ("down", NG - 3))
            finish(NG - 2, 1)
            down(NG - 3, 0, ("up", NG - 1))
            up(NG - 1, 0, ("down", NG - 2))
            finish(NG - 1, 0)
            down(NG - 2, 1, ("down", NG - 1))
            down(NG - 1, 0, None)

        def ada_at(j):
            return (half(3, 1) if j < 2 else half(3, 0))[:, 256 + KT * j:256 + KT * (j + 1)]

        def norm_sums(i):
            return half(0 if i == 1 else 3, 1)[:, 0:NB]

        def nothing(G, par):
            pass

        def ml_copy(eng, u, who, sem):
            i, hs = UNITS[u]
            n = i + 1
            if who == "a":
                a, b = 0, min(n, 4)
            else:
                a, b = 4, 4 + n if len(hs) == 2 else n
            eng.wait_ge(s["ml_t"], u + 1)
            if u >= 2:
                eng.wait_ge(s["ml_o"], u - 1)
            else:
                eng.wait_ge(s["sw_o"], NB)
            src, dst = bank[2][:, a * P:b * P], pt[u % 2][:, a * P:b * P]
            (eng.activation(dst, src, ACT.Copy) if who == "a" else eng.tensor_copy(dst, src)).then_inc(s[sem], 1)

        with nc.Block() as block:
            @block.sync
            def _(sp):
                def load_pack(n, kind, m):
                    if n >= AHEAD + 2:
                        sp.wait_ge(s["split_hi"], splits(n - 2))
                        sp.wait_ge(s["split_lo"], splits(n - 2))
                    sem = s[f"raw_loaded{n % 2}"]
                    if kind == "win":
                        load_win(sp, w_in_l, n % 2, m, sem)
                    else:
                        w = out_l.rearrange("o (k p) m -> p (o k) m", p=P)
                        sp.dma_start(raw[n % 2][:].rearrange("p (k m) -> p k m", k=KT), w[:, :, m * P:(m + 1) * P]).then_inc(sem, 16)

                def load_ada():
                    for r in range(ADA_PACKS):
                        j, k = 2 + r // KT, r % KT
                        if r < 2:
                            sp.wait_ge(s["split_hi"], splits(N_WIN - 2 + r))
                            sp.wait_ge(s["split_lo"], splits(N_WIN - 2 + r))
                        else:
                            sp.wait_ge(s["ada_used"], r - 1)
                        w, col = (ada_l, (j + 2) * D) if j < 4 else (ada_next, (j - 4) * D)
                        sp.dma_start(raw[r % 2][:], w[:, k * P:(k + 1) * P, col:col + D].rearrange("o p m -> (o p) m")).then_inc(s[f"ada_loaded{r % 2}"], 16)

                def load_early(j):
                    for k in range(KT):
                        if j:
                            sp.wait_ge(s["ada_early"], k + 1)
                        sp.dma_start(adaE[k][:], ada_l[:, k * P:(k + 1) * P, (j + 2) * D:(j + 3) * D].rearrange("o p m -> (o p) m")).then_inc(s[f"ada_early_loaded{j}"], 16)

                for n, (kind, m) in enumerate(PACKS):
                    if kind == "win" and m in (2, 4):
                        load_early(m // 2 - 1)
                    if kind == "win" and m == N_WIN - 2:
                        sp.wait_ge(s["dt_ready"], 1)
                        sp.wait_ge(s["mn_sum"], 1)
                        for k in range(2):
                            wq = of_layer(mla_w_uq)[:, k * P:(k + 1) * P, :].rearrange("o p (h d) -> p (o h) d", h=MLA_H)
                            sp.dma_start(wuq[:, k, :, 0:96], wq).then_inc(s["uproj_loaded"], 16)
                            sp.dma_start(wuq[:, k, :, 96:112], wq[:, :, 80:96]).then_inc(s["uproj_loaded"], 16)
                            sp.dma_start(wuq[:, k, :, 112:128], wq[:, :, 64:80]).then_inc(s["uproj_loaded"], 16)
                        sp.dma_start(wukv[:], of_layer(mla_w_ukv).rearrange("o p (h d) -> p (o h) d", h=MLA_H)).then_inc(s["uproj_loaded"], 16)
                    if kind == "win" and m == T_XBC:
                        sp.wait_ge(s["n1_lo"], KT)
                        sp.dma_start(xtail, xT[:, 4:8, :]).then_inc(s["tail_saved"], 16)
                    if n == N_OUT0:
                        load_ada()
                        sp.wait_ge(s["ada_used"], ADA_PACKS)
                    if n == N_OUT0 + 2:
                        sp.wait_ge(s["sd_y"], NB)
                        sp.dma_start(xT[:, 4:8, :], xtail).then_inc(s["tail_loaded"], 16)
                    if n >= AHEAD:
                        load_pack(n, kind, m)

                def raw_free(n):
                    sp.wait_ge(s["split_hi"], splits(n - 2))
                    sp.wait_ge(s["split_lo"], splits(n - 2))

                def load_up(G, par, nxt):
                    if type(G) is int and G == 1:
                        sp.wait_ge(s["pack_used"], N_PRE)
                        load_params(sp, of_next)
                    for j in range(4):
                        raw_free(up_pack(G) + j)
                        col = ((j // 2) + (j % 2) * FT) * P + G * 2 * P
                        w = up_l.rearrange("o (k p) m -> p (o k) m", p=P)[:, :, bass.ds(col, P)]
                        sp.dma_start(raw[j % 2][:].rearrange("p (k m) -> p k m", k=KT), w).then_inc(s[f"raw_loaded{j % 2}"], 16)

                def load_down(G, par, nxt):
                    for j in range(2):
                        raw_free(down_pack(G) + j)
                        w = down_l[:, bass.ds(G * 2 * P, 2 * P), HALF * j:HALF * (j + 1)].rearrange("o (k p) m -> p (o k) m", p=P)
                        sp.dma_start(raw[j][:].rearrange("p (k m) -> p k m", k=2), w).then_inc(s[f"raw_loaded{j}"], 16)

                run_mlp(sp, load_up, nothing, load_down)
                for n in range(AHEAD):
                    raw_free(N_ALL + n)
                    load_win(sp, of_next(w_in), n, n, s[f"next_loaded{n}"])

            def split(eng, slot, n, landed, *slot_free):
                if eng is nc.gpsimd:
                    eng.wait_ge(s["split_hi"], splits(n))
                eng.wait_ge(s[f"raw_loaded{slot}"], landed)
                for sem, v in slot_free:
                    eng.wait_ge(s[sem], v)
                if eng is nc.gpsimd:
                    eng.tensor_tensor(wLo[slot][:], raw[slot][:], fview(wHi[slot][:]), ALU.subtract).then_inc(s["split_lo"], 1)
                else:
                    eng.activation(wHi[slot][:], raw[slot][:], ACT.Copy).then_inc(s["split_hi"], 1)

            def split_pre(eng, n):
                if n == WIN_AT[T_MISC]:
                    eng.wait_ge(s["misc_clear"], 1)
                if n in (N_OUT0, N_OUT0 + 1):
                    split(eng, n % 2, n, loaded(n), ("ml_y", NB))
                else:
                    split(eng, n % 2, n, loaded(n), ("pack_used", n - 1))

            def split_up(eng, G, j):
                landed = loaded(N_PRE - 2 + j % 2) + 16 * (3 * G + j // 2 + (1 if type(G) is int and G == 0 else 0))
                if type(G) is int and G < 2 and j < 2 or j >= 2:
                    free = ("pack_used", N_PRE + 4 * G + j - 1)
                else:
                    free = ("down_full", 8 * (G - 2) + 4 * (j + 1))
                split(eng, j % 2, up_pack(G) + j, landed, free)

            def split_down(eng, G, j):
                final = type(G) is int and G == NG - 1
                landed = loaded(N_PRE - 2 + j) + 16 * (3 * G + (3 if final else 5))
                free = ("down_full", 8 * (NG - 2) + 4 * (j + 1)) if final else ("pack_used", N_PRE + 4 * (G + 1) + 3 + j)
                split(eng, j, down_pack(G) + j, landed, free)

            @block.tensor
            def _(pe):
                mm = pe.matmul
                ones = caus01[:, P - 1:P]

                def dense_step(pair, k, w_hi, w_lo, r_hi, r_lo, first, last_k):
                    for q, (w, r) in enumerate(((w_hi, r_hi), (w_hi, r_lo), (w_lo, r_hi))):
                        for hf in range(2):
                            last = mm(half(pair, hf), w(k), r(k)[:, HALF * hf:HALF * (hf + 1)],
                                      start=first and q == 0, stop=last_k and q == 2)
                    return last

                def dense(pair, w_hi, w_lo, r_hi, r_lo, kts):
                    for k in range(kts):
                        last = dense_step(pair, k, w_hi, w_lo, r_hi, r_lo, k == 0, k == kts - 1)
                    return last

                TWO = ([(0, 0), (0, 1)] + [(t, k + 2 - 2 * t) for k in range(KT - 2) for t in (0, 1)] + [(1, KT - 2), (1, KT - 1)])

                def dense_two(n0, r_hi, r_lo, order, k_ready):
                    steps = [step for step in order if not callable(step)]
                    ks = [[k for t_, k in steps if t_ == t] for t in range(2)]
                    for step in order:
                        if callable(step):
                            step()
                            continue
                        t, k = step
                        if t == 0 and k in k_ready:
                            pe.wait_ge(s[k_ready[k][0]], k_ready[k][1])
                        if k == ks[t][0] and n0 >= AHEAD:
                            pe.wait_ge(s["split_lo"], splits(n0 + t))
                        last = dense_step(t, k, tile_of(t, wHi), tile_of(t, wLo), r_hi, r_lo, k == ks[t][0], k == ks[t][-1])
                        if k == ks[t][-1]:
                            last.then_inc(s["pack_used"], 1)

                def tile_of(n, w):
                    return lambda k: w[n % 2][:, k * P:(k + 1) * P]

                def h_hi(k):
                    return hHi[:, k, :]

                def h_lo(k):
                    return hLo[:, k, :]

                def norm_sum(i):
                    pe.wait_ge(s[f"n{i}_acc"], KT - 1)
                    for b in range(NB):
                        last = mm(norm_sums(i)[:, b:b + 1], nt[2][:, b * P:(b + 1) * P], ones, start=True, stop=True)
                    last.then_inc(s[f"n{i}_sum"], 1)
                    spread_rms(pe, f"n{i}")

                def ada_sum(j):
                    pe.wait_ge(s["ada_early" if j < 2 else "ada_used"], KT * (j % 2 + 1 if j < 2 else j - 1))
                    for m in range(KT):
                        last = mm(ada_at(j)[:, m:m + 1], nt[(2 if j < 2 else 0) + j % 2][:, m * P:(m + 1) * P],
                                  caus01[:, P - 1:P], start=True, stop=True)
                    last.then_inc(s["ada_part"], 1)

                dense_two(0, h_hi, h_lo, TWO, {k: ("n1_lo", k + 1) for k in range(KT)})
                for m in range(2, N_WIN):
                    pe.wait_ge(s["split_lo"], splits(m))
                    pe.wait_ge(s[f"pair_free{m % 2}"], m // 2)
                    dense(m % 2, tile_of(m, wHi), tile_of(m, wLo), h_hi, h_lo, KT).then_inc(s["pack_used"], 1)
                    if m == 4:
                        ada_sum(0)
                        ada_sum(1)
                    if m == 13:
                        pe.wait_ge(s["mn_sq"], 3)
                        for b in range(NB):
                            for k in range(2):
                                mm(half(2, 0)[:, b:b + 1], nt[k][:, b * P:(b + 1) * P], ones, start=k == 0, stop=k == 1)
                            last = mm(half(2, 0)[:, NB + b:NB + b + 1], nt[2][:, b * P:(b + 1) * P], ones, start=True, stop=True)
                        last.then_inc(s["mn_sum"], 1)
                    if m == 15:
                        pe.wait_ge(s["mod_rest"], 1)
                        pe.wait_ge(s["mn_rstd"], 3)
                        for b in range(2 * NB):
                            last = spread(pe, bank[2 + b // NB][:, (b % NB) * P:(b % NB + 1) * P], rst[:, b:b + 1])
                        last.then_inc(s["mn_sum"], 1)
                    if m == 17:
                        pe.wait_ge(s["mn_dve"], 3)
                        for b in range(NB):
                            last = pe.transpose(bank[3][:, b * P:(b + 1) * P], sv[:, b * P:(b + 1) * P], ident[:])
                        last.then_inc(s["sw_vt"], 1)
                pe.wait_ge(s["pair_free0"], 10)
                pe.wait_ge(s["pair_free1"], 10)

                pe.wait_ge(s["uproj_loaded"], 16 * 7)
                pe.wait_ge(s["sw_vcopied"], 1)
                for h in range(MLA_H):
                    for hf in range(2):
                        for k in range(2):
                            last = mm(half(h, hf), wuq[:, k, h, :], cq[:, k, HALF * hf:HALF * (hf + 1)], start=k == 0, stop=k == 1)
                    last.then_inc(s["mp_full"], 1)
                for h in range(MLA_H):
                    pe.wait_ge(s["mp_kv"], h + 1)
                    pe.wait_ge(s["mp_q"], 3 * (h + 1))
                    for hf in range(2):
                        last = mm(bank[h][0:64, HALF * hf:HALF * (hf + 1)], wukv[:, h, 0:64], ckv[:, HALF * hf:HALF * (hf + 1)], start=True, stop=True)
                    last.then_inc(s["mp_full"], 1)
                for u in range(2):
                    pe.wait_ge(s["mp_kv"], 7 + u)
                    for b in range(4 * u, 4 * u + 4):
                        last = mm(bank[2 + u][:, (b % 4) * 256:(b % 4 + 1) * 256], ckv[:, b * P:(b + 1) * P], wukv[:, :, 64:128],
                                  start=True, stop=True)
                    last.then_inc(s["mp_full"], 1)

                def sw_scores(i):
                    if i < 2:
                        pe.wait_ge(s["mp_kv"], 5 + i)
                    else:
                        pe.wait_ge(s["sw_m"], i - 1)
                    lo = max(i - 1, 0) * BLK
                    for h in range(SWA_H):
                        r = slice(64 * (h // 2), 64 * (h // 2) + 64)
                        o = bank[i % 2][:, h * 256 + (0 if i else BLK):(h + 1) * 256]
                        last = mm(o, sq[r, h % 2, i * BLK:(i + 1) * BLK], sk[r, lo:(i + 1) * BLK], start=True, stop=True)
                    last.then_inc(s["sw_s"], 1)

                def sw_transposes(i):
                    pe.wait_ge(s["sw_e"], i + 1)
                    if i == 0:
                        pe.wait_ge(s["mp_kv"], 10)
                    if i >= 1:
                        pe.wait_ge(s["sw_ca"], i)
                        pe.wait_ge(s["sw_cd"], i)
                    for h in range(SWA_H):
                        for b in range(0 if i else 1, 2):
                            q = (2 * h + b) * P
                            last = pe.transpose(bank[2][:, q:q + P], pr[i % 2][:, q:q + P], ident[:])
                    last.then_inc(s["sw_t"], 1)

                def sw_out(i):
                    pe.wait_ge(s["sw_ca"], i + 1)
                    pe.wait_ge(s["sw_cd"], i + 1)
                    if i >= 1:
                        pe.wait_ge(s["sw_x"], i)
                    if i == 4:
                        ada_sum(2)
                    for h in range(SWA_H):
                        for b in range(0 if i else 1, 2):
                            last = mm(half(3, 0)[:, h * 64:(h + 1) * 64], pt[i % 2][:, (2 * h + b) * P:(2 * h + b + 1) * P],
                                      svt[:, i - 1 + b, (h // 2) * 64:(h // 2) * 64 + 64], start=b == (0 if i else 1), stop=b == 1)
                    last.then_inc(s["sw_o"], 1)

                def to_features(i, x_sem, lo_sem, y_sem):
                    pe.wait_ge(s[x_sem], i + 1)
                    if i >= 1:
                        pe.wait_ge(s[lo_sem], i)
                    for k in range(2):
                        last = pe.transpose(half(3, 1)[:, k * P:(k + 1) * P], otok[i % 2][:, k * P:(k + 1) * P], ident[:])
                    last.then_inc(s[y_sem], 1)

                sw_scores(0)
                for i in range(NB):
                    if i + 1 < NB:
                        sw_scores(i + 1)
                    sw_transposes(i)
                    if i >= 1:
                        sw_out(i - 1)
                    if i >= 2:
                        to_features(i - 2, "sw_x", "sw_lo", "sw_y")
                sw_out(NB - 1)
                to_features(NB - 2, "sw_x", "sw_lo", "sw_y")
                to_features(NB - 1, "sw_x", "sw_lo", "sw_y")

                def ml_scores(u):
                    i, hs = UNITS[u]
                    if u < 2:
                        pe.wait_ge(s["sw_m"], NB - 1 + u)
                        pe.wait_ge(s["rope_dve"], 6)
                        pe.wait_ge(s["mp_q"], 12)
                    else:
                        pe.wait_ge(s["ml_e"], u - 1)
                    n = (i + 1) * BLK
                    for q, h in enumerate(hs):
                        for a in range(0, n, HALF):
                            b = min(a + HALF, n)
                            last = mm(bank[u % 2][:, q * HALF + a:q * HALF + b], qh[h][0:96, i * BLK:n], kh[h][0:96, a:b], start=True, stop=True)
                    last.then_inc(s["ml_s"], 1)

                def copies_done(u):
                    pe.wait_ge(s["ml_ca"], u + 1)
                    pe.wait_ge(s["ml_cd"], u + 1)

                def ml_transposes(u):
                    i, hs = UNITS[u]
                    pe.wait_ge(s["ml_e"], u + 1)
                    if u >= 1:
                        copies_done(u - 1)
                    else:
                        pe.wait_ge(s["sw_ca"], NB)
                        pe.wait_ge(s["sw_cd"], NB)
                    for q in range(len(hs)):
                        for b in range(i + 1):
                            c0 = slice(q * HALF + b * P, q * HALF + (b + 1) * P)
                            last = pe.transpose(bank[2][:, c0], pr[u % 2][:, c0], ident[:])
                    last.then_inc(s["ml_t"], 1)

                def ml_out(u):
                    i, hs = UNITS[u]
                    copies_done(u)
                    if hs[0] == 0:
                        pe.wait_ge(s["ml_x" if i else "sw_x"], i if i else NB)
                        if i in ADA_AT:
                            ada_sum(3 + ADA_AT.index(i))
                    for q, h in enumerate(hs):
                        for b in range(i + 1):
                            last = mm(half(3, 0)[:, h * 64:(h + 1) * 64], pt[u % 2][:, q * HALF + b * P:q * HALF + (b + 1) * P],
                                      vt[:, b, h * 64:(h + 1) * 64], start=b == 0, stop=b == i)
                    last.then_inc(s["ml_o"], 1)

                ml_scores(0)
                for u in range(NU):
                    if u + 1 < NU:
                        ml_scores(u + 1)
                    ml_transposes(u)
                    if u == 0:
                        pe.wait_ge(s["sw_lo"], NB)
                    else:
                        ml_out(u - 1)
                    i = UNITS[u][0]
                    if i and u == UNIT_FIRST[i] + (1 if i < 4 else 2):
                        to_features(i - 1, "ml_x", "ml_lo", "ml_y")
                ml_out(NU - 1)
                to_features(NB - 1, "ml_x", "ml_lo", "ml_y")

                pe.wait_ge(s["dt_ready"], 1)
                pe.wait_ge(s["mod_rest"], 3)
                for b in range(NB):
                    last = pe.transpose(half(3, 0)[:, b * 40:(b + 1) * 40], cs[0:40, b * P:(b + 1) * P], ident[0:40, 0:40])
                last.then_inc(s["sd_t"], 1)
                pe.wait_ge(s["sd_c"], 1)
                pe.wait_ge(s["ml_lo"], NB)
                mm(half(3, 1)[:, 0:64], ident[:, P - 1:P].to_broadcast([P, P]), adt[:, :, 0:8], start=True, stop=True).then_inc(s["sd_t"], 1)
                for j in range(4):
                    if j < 2:
                        pe.wait_ge(s["ml_e"], NU)
                    else:
                        pe.wait_ge(s["sd_xd"], j - 1)
                    pe.wait_ge(s["xbc_act"], j + 1)
                    for b in range(NB):
                        last = pe.transpose(bank[j % 2][:, b * P:(b + 1) * P], xbc[:, j, b * P:(b + 1) * P], ident[:])
                    last.then_inc(s["sd_xt"], 1)
                pe.wait_ge(s["xbc_act"], 8)
                for g in range(2):
                    pe.wait_ge(s["sd_xd"], 3 + g)
                    for b in range(NB):
                        last = pe.transpose(bank[g][:, b * P:(b + 1) * P], xbc[:, 4 + g, b * P:(b + 1) * P], ident[:])
                    last.then_inc(s["sd_xt"], 1)

                def square_sums(ch):
                    pe.wait_ge(s["sd_sq"], ch + 1)
                    for g in range(2):
                        for k in range(2):
                            last = mm(half(2, 1)[:, 256 + NB * g + ch:257 + NB * g + ch], sqc[ch % 2][:, 2 * g + k, :], ones, start=k == 0, stop=k == 1)
                    last.then_inc(s["sd_ss"], 1)

                def sd_front(v):
                    ch, g = divmod(v, 2)
                    c0 = slice(ch * BLK, (ch + 1) * BLK)
                    if v < 2:
                        pe.wait_ge(s["sd_bt"], 2)
                        pe.wait_ge(s["sd_xe"], 4)
                    else:
                        pe.wait_ge(s["sd_eb"], v - 1)
                    for q in range(4):
                        h = 4 * g + q
                        last = mm(half(v % 2, 0)[:, q * P:(q + 1) * P], ident[0:8, h:h + 1].to_broadcast([8, P]), cs[0:8, c0],
                                  start=True, stop=True)
                    last.then_inc(s["sd_bc"], 1)
                    if v >= 2:
                        pe.wait_ge(s["sd_M"], v - 1)
                    if v % 2 and ch >= 5:
                        square_sums(ch - 5)
                    mm(half(2, v % 2)[:, 0:P], xbc[:, 4 + g, c0], xbc[:, 6 + g, c0], start=True, stop=True).then_inc(s["sd_cb"], 1)
                    if ch == NB - 1:
                        return
                    if g == 0 and ch >= 2:
                        pe.wait_ge(s["sd_h"], 2 * ch - 1)
                    mm(half(ch % 2, 1)[:, g * 256:(g + 1) * 256], bt[g][:, ch, :], xe[:, ch, 4 * g:4 * g + 4, :], start=True, stop=True).then_inc(s["sd_st"], 1)

                def sd_back(v):
                    ch, g = divmod(v, 2)
                    if g == 0:
                        pe.wait_ge(s["sd_h"], 1 + 2 * ch)
                        if ch >= 2:
                            pe.wait_ge(s["sd_yd_read"], ch - 1)
                    pe.wait_ge(s["sd_M"], v + 1)
                    pe.wait_ge(s["sd_cs"], v + 1)
                    for q in range(4):
                        h = 4 * g + q
                        o = half(3, ch % 2)[64 * (h % 2):64 * (h % 2) + 64, (h // 2) * P:(h // 2 + 1) * P]
                        mm(o, xd[:, ch, h, :], Mt[v % 2][:, q, :], start=True, stop=False)
                        last = mm(o, hst[ch % 2][:, h, :], Cs[v % 2][:, q, :], start=False, stop=True)
                    last.then_inc(s["sd_yd"], 1)

                sd_front(0)
                sd_front(1)
                for v in range(2 * NB):
                    sd_back(v)
                    if v + 2 < 2 * NB:
                        sd_front(v + 2)
                pe.wait_ge(s["sd_M"], 2 * NB)
                for ch in range(NB - 5, NB):
                    square_sums(ch)
                y_hi = [yHi[:, j, :] for j in range(4)] + [mHi[:, j, :] for j in range(2)] + [sHi[:, j, :] for j in range(2)]
                y_lo = [yLo[:, j, :] for j in range(4)] + [mLo[:, j, :] for j in range(2)] + [sLo[:, j, :] for j in range(2)]

                def spread_ssd():
                    pe.wait_ge(s["sd_rstd"], 2)
                    for b in range(2 * NB):
                        last = spread(pe, bank[2 + b // NB][:, (b % NB) * P:(b % NB + 1) * P], rst[:, b:b + 1])
                    last.then_inc(s["sd_spread"], 1)

                pe.wait_ge(s["sd_h"], 2 * NB - 1)
                dense_two(N_OUT0, lambda k: y_hi[k], lambda k: y_lo[k],
                          [(0, 4), (0, 5), (1, 4), (1, 5), (0, 6), spread_ssd, (1, 6), (0, 7), (1, 7),
                           (0, 0), (0, 1), (1, 0), (0, 2), (1, 1), (0, 3), (1, 2), (1, 3)],
                          {k: ("sd_lo", k + 1) for k in range(4)})
                for m in range(2, KT):
                    n = N_OUT0 + m
                    pe.wait_ge(s["split_lo"], splits(n))
                    pe.wait_ge(s["x_updated"], m - 1)
                    dense(m % 2, tile_of(n, wHi), tile_of(n, wLo), lambda k: y_hi[k], lambda k: y_lo[k], KT).then_inc(s["pack_used"], 1)

                pe.wait_ge(s["x_updated"], KT)
                norm_sum(2)

                def up(G, par, nxt):
                    first = type(G) is int and G == 0
                    if first:
                        dense_two(N_PRE, h_hi, h_lo, TWO, {k: ("n2_lo", k + 1) for k in range(KT)})
                    for j in range(2 if first else 0, 4):
                        pe.wait_ge(s["split_lo"], splits(up_pack(G) + j))
                        pe.wait_ge(s["up_tap"], 8 * G + 2 * j - 2)
                        dense(j % 2, tile_of(j, wHi), tile_of(j, wLo), h_hi, h_lo, KT).then_inc(s["pack_used"], 1)

                def down(G, par, nxt):
                    if nxt is None:
                        pe.wait_ge(s["up_tap"], 8 * NG)
                        transpose_params(pe)
                    pe.wait_ge(s["up_lo"], 2 * G + 2)
                    for m in range(KT):
                        j, col = m // 4, (m % 4) * P
                        if m % 4 == 0:
                            pe.wait_ge(s["split_lo"], splits(down_pack(G) + j))
                        pe.wait_ge(s[f"down_free{m % 2}"], 4 * G + m // 2)
                        dense(2 + m % 2, lambda k: wHi[j][:, k * HALF + col:k * HALF + col + P],
                              lambda k: wLo[j][:, k * HALF + col:k * HALF + col + P],
                              lambda k: gHi[par][k][:], lambda k: gLo[par][k][:], 2).then_inc(s["down_full"], 1)

                run_mlp(pe, up, nothing, down)
                norm_sum(1)

            def run_splitter(eng, after_up, finish):
                def split_next(nxt, j):
                    if nxt is not None:
                        (split_up if nxt[0] == "up" else split_down)(eng, nxt[1], j)

                def up(G, par, nxt):
                    for j in range(4):
                        if j < 2:
                            split_up(eng, G, j + 2)
                        else:
                            split_next(nxt, j - 2)
                        after_up(G, par, j)

                def down(G, par, nxt):
                    for j in range(2):
                        split_next(nxt, j)

                run_mlp(eng, up, finish, down)

            @block.gpsimd
            def _(pool):
                def ada_products():
                    pool.wait_ge(s["mn_sum"], 1)
                    for r in range(ADA_PACKS):
                        j, k = divmod(r, KT)
                        acc, w = nt[j % 2][:], raw[r % 2][:]
                        pool.wait_ge(s[f"ada_loaded{r % 2}"], 16 * (r // 2 + 1))
                        ck = cact[:, k:k + 1].to_broadcast([P, D])
                        if k == 0:
                            if j >= 2:
                                pool.wait_ge(s["ada_part"], j + 1)
                            pool.tensor_tensor(acc, w, ck, ALU.mult).then_inc(s["ada_used"], 1)
                        else:
                            pool.tensor_tensor(w, w, ck, ALU.mult).then_inc(s["ada_prod"], 1)
                            pool.wait_ge(s["ada_prod"], r - j)
                            pool.wait_ge(s["ada_used"], r)
                            pool.tensor_tensor(acc, acc, w, ALU.add).then_inc(s["ada_used"], 1)

                def scan_products():
                    pool.wait_ge(s["sd_c"], 4)
                    for j in range(4):
                        pool.wait_ge(s["sd_xd"], j + 1)
                        if j == 0:
                            pool.wait_ge(s["ml_e"], NU)
                        o = slice(2 * j, 2 * j + 2)
                        pool.tensor_tensor(xe[:, :, o, :], xd[:, :, o, :], dte[:, :, o].unsqueeze(3).to_broadcast([P, NB, 2, 64]), ALU.mult).then_inc(s["sd_xe"], 1)

                    def gate(ch):
                        pool.wait_ge(s["sd_yd_read"], ch + 1)
                        c0 = slice(ch * BLK, (ch + 1) * BLK)
                        pool.tensor_tensor(xbc[:, 0:4, c0], xbc[:, 0:4, c0], zs[:, :, c0], ALU.mult).then_inc(s["sd_y"], 1)

                    for v in range(2 * NB):
                        ch, g = divmod(v, 2)
                        pool.wait_ge(s["sd_eb"], v + 1)
                        pool.tensor_tensor(Cs[v % 2][:], Cs[v % 2][:], xbc[:, 6 + g, ch * BLK:(ch + 1) * BLK].unsqueeze(1).to_broadcast([P, 4, P]),
                                           ALU.mult).then_inc(s["sd_cs"], 1)
                        if v % 2 == 0 and ch >= 2:
                            gate(ch - 2)
                        if v in (4, 6):
                            split_pre(pool, N_OUT0 + v // 2 - 2)
                    gate(NB - 2)
                    gate(NB - 1)

                for n in range(AHEAD, N_PRE):
                    if n == WIN_AT[T_MISC]:
                        pool.wait_ge(s["split_hi"], splits(n - 2))
                        pool.wait_ge(s["split_lo"], splits(n - 2))
                        pool.memset(raw[n % 2][:].rearrange("p (k m) -> p k m", k=KT)[:, :, 8:64], 0.0).then_inc(s["misc_clear"], 1)
                    if n == N_OUT0:
                        ada_products()
                        scan_products()
                    if n not in (N_OUT0, N_OUT0 + 1):
                        split_pre(pool, n)
                for j in range(2):
                    split_up(pool, 0, j)

                def g_lo(G, par, c):
                    pool.wait_ge(s["up_hi"], 2 * G + c + 1)
                    pool.tensor_tensor(gLo[par][c][:], ua[c][:], fview(gHi[par][c][:]), ALU.subtract).then_inc(s["up_lo"], 1)

                run_splitter(pool, lambda G, par, j: g_lo(G, par, 0) if j == 3 else None, lambda G, par: g_lo(G, par, 1))
                for n in range(AHEAD):
                    split_ahead(pool, n)

            @block.scalar
            def _(act):
                A = act.activation

                def root(sums, dst, n, sum_sem, sem, count=1):
                    act.wait_ge(s[sum_sem], count)
                    A(dst, sums, ACT.Sqrt, bias=eps[:], scale=1.0 / n).then_inc(s[sem], 1)

                def norm_squares(i, k):
                    if i == 2:
                        act.wait_ge(s["x_updated"], k + 1)
                    else:
                        act.wait_ge(s[f"down_free{k % 2}"], 4 * (NG - 1) + k // 2 + 1)
                    if k >= 3:
                        act.wait_ge(s[f"n{i}_acc"], k - 2)
                    A(nt[2 if k == 0 else k % 2][:], xT[:, k, :], ACT.Square).then_inc(s[f"n{i}_sq"], 1)

                def h_hi(i):
                    for k in range(KT):
                        act.wait_ge(s[f"n{i}_scaled"], k + 1)
                        A(hHi[:, k, :], nt[k % 2][:], ACT.Identity, bias=mod[:, (i - 1) * 3 * KT + k:(i - 1) * 3 * KT + k + 1]).then_inc(s[f"n{i}_hi"], 1)

                h_hi(1)

                def silu_of(j):
                    act.wait_ge(s[f"pair_free{j % 2}"], (T_XBC + j) // 2 + 1)
                    A(xbc[:, j, :], xbc[:, j, :], ACT.Silu).then_inc(s["xbc_act"], 1)

                for n in range(N_WIN):
                    if n + 2 < N_WIN:
                        split_pre(act, n + 2)
                    m = n
                    if m == 12:
                        act.wait_ge(s["dt_ready"], 1)
                        for k, src in enumerate((cq[:, 0, :], cq[:, 1, :], ckv[:])):
                            A(nt[k][:], src, ACT.Square).then_inc(s["mn_sq"], 1)
                    if m == 15:
                        root(half(2, 0)[:, 0:NB], rst[:, 0:NB], MLA_QR, "mn_sum", "mn_rstd")
                        root(half(2, 0)[:, NB:2 * NB], rst[:, NB:2 * NB], MLA_KVR, "mn_sum", "mn_rstd")
                    if m == 19:
                        act.wait_ge(s["sw_vt"], 1)
                        A(svt[:], bank[3][:].rearrange("p (b d) -> p b d", b=NB), ACT.Copy).then_inc(s["sw_vcopied"], 1)
                    act.wait_ge(s["pack_used"], n + 1)
                    ps, free = bank[m % 2][:], s[f"pair_free{m % 2}"]
                    if m < T_XBC:
                        dst = ([sq[:, 0, :], sq[:, 1, :], sk[:], sv[:], misc[:], cq[:, 0, :], cq[:, 1, :], ckv[:]])[m]
                        A(dst, ps, ACT.Copy).then_inc(free, 1)
                        if m == T_MISC + 1:
                            act.wait_ge(s["pair_free0"], 3)
                            act.wait_ge(s["ada_part"], 2)
                            A(nt[0][0:8, :], misc[0:8, :], ACT.Abs, bias=hp[:, 0:1]).then_inc(s["dt_abs"], 1)
                            act.wait_ge(s["dt_abs"], 1)
                            A(nt[1][0:8, :], nt[0][0:8, :], ACT.Exp, scale=-1.0).then_inc(s["dt_exp"], 1)
                            A(hp[:, 1:2], hp[:, 1:2], ACT.Exp).then_inc(s["dt_exp"], 1)
                            act.wait_ge(s["dt_sum"], 1)
                            A(nt[3][0:8, :], nt[2][0:8, :], ACT.Ln).then_inc(s["dt_ln"], 1)
                    elif m < T_Z:
                        j = m - T_XBC
                        A(xbc[:, j, :], ps, ACT.Identity, bias=prm[:, R_CB + j:R_CB + j + 1],
                          scale=prm[:, R_CW + 24 + j:R_CW + 25 + j]).then_inc(s["conv_base"], 1)
                        if j >= 1:
                            silu_of(j - 1)
                    else:
                        if m == T_Z:
                            silu_of(7)
                            act.wait_ge(s["tail_saved"], 16)
                        A(zs[:, m - T_Z, :], ps, ACT.Silu).then_inc(free, 1)

                for h in range(MLA_H):
                    act.wait_ge(s["mp_full"], h + 1)
                    A(qh[h][0:64, :], bank[h][0:64, :], ACT.Copy).then_inc(s["mp_kv"], 1)
                for h in range(MLA_H):
                    act.wait_ge(s["mp_full"], 5 + h)
                    A(kh[h][0:64, :], bank[h][0:64, :], ACT.Copy).then_inc(s["mp_kv"], 1)
                for u in range(2):
                    act.wait_ge(s["mp_full"], 9 + u)
                    A(vt[:, 4 * u:4 * u + 4, :], bank[2 + u][:].rearrange("p (b d) -> p b d", b=4), ACT.Copy).then_inc(s["mp_kv"], 1)

                def y_hi(i, y_sem, hi_sem, dst):
                    act.wait_ge(s[y_sem], i + 1)
                    A(dst[:, :, i * BLK:(i + 1) * BLK], half(3, 1)[:, 0:256].rearrange("p (k t) -> p k t", k=2), ACT.Copy).then_inc(s[hi_sem], 1)

                def sw_exp(i):
                    act.wait_ge(s["sw_n"], i + 1)
                    st_ = stat[:, i % 3]
                    for h in range(SWA_H):
                        a = pr[i % 2][:, h * 256 + (0 if i else BLK):(h + 1) * 256]
                        A(a, a, ACT.Exp, bias=st_[:, 1, h:h + 1], accum_out=st_[:, 2, h:h + 1])
                    A(st_[:, 4, :], st_[:, 3, :], ACT.Exp).then_inc(s["sw_e"], 1)

                sw_exp(0)
                act.wait_ge(s["rope_dve"], 6)
                for i in range(NB):
                    if i + 1 < NB:
                        sw_exp(i + 1)
                    act.wait_ge(s["sw_t"], i + 1)
                    if i >= 2:
                        act.wait_ge(s["sw_o"], i - 1)
                    lo = 0 if i else 1
                    view = lambda t: t.rearrange("p (h b k) -> p h b k", h=2, b=2)[:, :, lo:2, :]
                    A(view(pt[i % 2][:, 0:HALF]), view(half(2, 0)), ACT.Copy).then_inc(s["sw_ca"], 1)
                    if i >= 2:
                        y_hi(i - 2, "sw_y", "sw_hi", sHi)
                y_hi(NB - 2, "sw_y", "sw_hi", sHi)
                y_hi(NB - 1, "sw_y", "sw_hi", sHi)

                def ml_exp(u):
                    i, hs = UNITS[u]
                    n = (i + 1) * BLK
                    act.wait_ge(s["ml_n"], u + 1)
                    if u < 2:
                        act.wait_ge(s["sw_t"], NB)
                    else:
                        act.wait_ge(s["ml_t"], u - 1)
                    for q, h in enumerate(hs):
                        last = A(pr[u % 2][:, q * HALF:q * HALF + n], bank[u % 2][:, q * HALF:q * HALF + n], ACT.Exp,
                                 bias=stat[:, i % 3, 1, h:h + 1], scale=MLA_SCALE, accum_out=stat[:, i % 3, 2, h:h + 1])
                    last.then_inc(s["ml_e"], 1)

                ml_exp(0)
                for u in range(NU):
                    if u + 1 < NU:
                        ml_exp(u + 1)
                    ml_copy(act, u, "a", "ml_ca")
                    i = UNITS[u][0]
                    if i and u == UNIT_END[i] - 1:
                        y_hi(i - 1, "ml_y", "ml_hi", mHi)
                y_hi(NB - 1, "ml_y", "ml_hi", mHi)

                def chunk_square(ch):
                    act.wait_ge(s["sd_y"], ch + 1)
                    if ch >= 2:
                        act.wait_ge(s["sd_ss"], ch - 1)
                    A(sqc[ch % 2][:], xbc[:, 0:4, ch * BLK:(ch + 1) * BLK], ACT.Square).then_inc(s["sd_sq"], 1)

                act.wait_ge(s["sd_t"], 1)
                A(adt[:], half(3, 0)[:, 0:320].rearrange("p (b r) -> p b r", b=NB), ACT.Copy).then_inc(s["sd_c"], 1)
                act.wait_ge(s["sd_t"], 2)
                A(aend[:], half(3, 1)[:, 0:64].rearrange("p (b r) -> p b r", b=NB), ACT.Copy).then_inc(s["sd_c"], 1)
                act.wait_ge(s["sd_c"], 2)
                A(dec[:], aend[:], ACT.Exp).then_inc(s["sd_c"], 1)
                act.wait_ge(s["sd_xe0"], 1)
                A(dte[:], dte[:], ACT.Exp).then_inc(s["sd_c"], 1)
                for g in range(2):
                    act.wait_ge(s["sd_xt"], 5 + g)
                    A(bt[g][:], bank[g][:].rearrange("p (b n) -> p b n", b=NB), ACT.Copy).then_inc(s["sd_bt"], 1)
                for v in range(2 * NB):
                    ch, g = divmod(v, 2)
                    if v in (4, 6):
                        split_pre(act, N_OUT0 + v // 2 - 2)
                    act.wait_ge(s["sd_bc"], v + 1)
                    if v >= 2:
                        act.wait_ge(s["sd_yd"], v - 1)
                    for q in range(4):
                        h = 4 * g + q
                        last = A(Mt[v % 2][:, q, :], half(v % 2, 0)[:, q * P:(q + 1) * P], ACT.Relu, bias=adt[:, ch, h:h + 1], scale=-1.0)
                    last.then_inc(s["sd_seg"], 1)
                    A(Cs[v % 2][:], half(v % 2, 0).rearrange("p (q l) -> p q l", q=4), ACT.Exp).then_inc(s["sd_eb"], 1)
                    act.wait_ge(s["sd_seg"], v + 1)
                    A(Mt[v % 2][:], Mt[v % 2][:], ACT.Exp, scale=-1.0).then_inc(s["sd_dec"], 1)
                    if g and ch >= 3:
                        chunk_square(ch - 3)
                for ch in range(NB - 3, NB):
                    chunk_square(ch)
                root(half(2, 1)[:, 256:256 + 2 * NB], rst[:], SSD_INNER // 2, "sd_ss", "sd_rstd", NB)
                for j in range(4):
                    act.wait_ge(s["sd_rd"], j + 1)
                    A(yHi[:, j, :], xbc[:, j, :], ACT.Copy).then_inc(s["sd_hi"], 1)

                for m in range(KT):
                    if m + 2 < KT:
                        split_pre(act, N_OUT0 + m + 2)
                    else:
                        split_up(act, 0, m + 2 - KT)
                    norm_squares(2, m)
                root(norm_sums(2), rst[:, 0:NB], D, "n2_sum", "n2_rstd")
                h_hi(2)

                def after_up(G, par, j):
                    c, is_b = divmod(j, 2)
                    act.wait_ge(s["pack_used"], N_PRE + 4 * G + j + 1)
                    first = type(G) is int and G == 0
                    if not first:
                        act.wait_ge(s["up_mul" if is_b else "up_lo"], 2 * G - 1 + c)
                    col = 2 * G + c + is_b * FT
                    A((ub if is_b else ua)[c][:], bank[is_b][:], ACT.Identity, bias=ffp[:, bass.ds(col + 3 * 2 * FT, 1)],
                      scale=ffp[:, bass.ds(col + 2 * 2 * FT, 1)]).then_inc(s["up_base"], 1)
                    if is_b:
                        act.wait_ge(s["up_tap"], 8 * G + 4 * c + 2)
                        A(ua[c][:], ua[c][:], ACT.Silu).then_inc(s["up_silu"], 1)
                    if j == 2:
                        g_hi(G, par, 0)

                def g_hi(G, par, c):
                    act.wait_ge(s["up_mul"], 2 * G + c + 1)
                    if not (type(G) is int and G < 2):
                        act.wait_ge(s["down_full"], 8 * (G - 1))
                    A(gHi[par][c][:], ua[c][:], ACT.Copy).then_inc(s["up_hi"], 1)

                run_splitter(act, after_up, lambda G, par: g_hi(G, par, 1))
                copy_params(act)
                for k in range(KT):
                    norm_squares(1, k)
                    if k == 3:
                        act.wait_ge(s["down_full"], 8 * (NG - 1) + 4)
                        split_ahead(act, 0)
                act.wait_ge(s["down_full"], 8 * NG)
                root(norm_sums(1), rst[:, 0:NB], D, "n1_sum", "n1_rstd")
                split_ahead(act, 1)

            @block.vector
            def _(dve):
                step = [0]

                def link(ins):
                    step[0] += 1
                    ins.then_inc(s["dve_step"], 1)
                    dve.wait_ge(s["dve_step"], step[0])

                def norm_adds(i, k):
                    dve.wait_ge(s[f"n{i}_sq"], k + 1)
                    if k >= 2:
                        dve.wait_ge(s[f"n{i}_acc"], k - 1)
                    dve.tensor_tensor(nt[2][:], nt[2][:], nt[k % 2][:], ALU.add).then_inc(s[f"n{i}_acc"], 1)

                def inverse(dst, sem):
                    dve.wait_ge(s[sem], 1)
                    dve.reciprocal(dst, dst).then_inc(s[sem], 1)

                def norm_apply(i):
                    shift = (i - 1) * 3 * KT

                    def scaled(k):
                        if k >= 2:
                            dve.wait_ge(s[f"n{i}_lo"], k - 1)
                        dve.scalar_tensor_tensor(out=nt[k % 2][:], in0=xT[:, k, :], scalar=scl[:, i - 1, k:k + 1], in1=bank[2][:],
                                                 op0=ALU.mult, op1=ALU.mult).then_inc(s[f"n{i}_scaled"], 1)

                    scaled(0)
                    for k in range(KT):
                        if k + 1 < KT:
                            scaled(k + 1)
                        dve.wait_ge(s[f"n{i}_hi"], k + 1)
                        dve.scalar_tensor_tensor(out=hLo[:, k, :], in0=nt[k % 2][:], scalar=mod[:, shift + k:shift + k + 1],
                                                 in1=fview(hHi[:, k, :]), op0=ALU.add, op1=ALU.subtract).then_inc(s[f"n{i}_lo"], 1)

                norm_apply(1)

                def dt_work():
                    dve.wait_ge(s["pair_free0"], 3)
                    n0, n1, n2, n3 = (t[0:8, :] for t in nt)
                    raw_dt = misc[0:8, :]
                    dve.wait_ge(s["dt_exp"], 2)
                    link(dve.tensor_scalar(hp[:, 1:2], hp[:, 1:2], -1.0, None, ALU.mult))
                    dve.tensor_scalar(n2, n1, 1.0, None, ALU.add).then_inc(s["dt_sum"], 1)
                    dve.wait_ge(s["dt_ln"], 1)
                    link(dve.tensor_scalar(n2, n2, -1.0, None, ALU.add))
                    link(dve.tensor_scalar(n0, n2, 0.0, None, ALU.is_equal))
                    link(dve.tensor_tensor(n2, n2, n0, ALU.add))
                    link(dve.reciprocal(n2, n2))
                    link(dve.tensor_tensor(n3, n3, n1, ALU.mult))
                    link(dve.tensor_tensor(n3, n3, n2, ALU.mult))
                    link(dve.tensor_tensor(n1, n1, n0, ALU.mult))
                    link(dve.tensor_tensor(n3, n3, n1, ALU.add))
                    link(dve.tensor_scalar(n0, raw_dt, hp[:, 0:1], 0.0, ALU.add, ALU.max))
                    link(dve.tensor_tensor(n2, n0, n3, ALU.add))
                    link(dve.tensor_copy(cs[32:40, :], n2))
                    link(dve.tensor_scalar(n1, n2, hp[:, 1:2], None, ALU.mult))
                    link(dve.tensor_scalar(n0, n2, 0.0, 1.0, ALU.mult, ALU.add))
                    for b in range(NB):
                        c0 = slice(b * BLK, (b + 1) * BLK)
                        last = dve.tensor_tensor_scan(cs[0:8, c0], n0[:, c0], n1[:, c0], 0.0, ALU.mult, ALU.add)
                    last.then_inc(s["dt_ready"], 1)

                for r in range(2 * KT):
                    j, k = divmod(r, KT)
                    acc = nt[2 + j]
                    if k == 0:
                        dve.wait_ge(s[f"ada_early_loaded{j}"], 16 * KT)
                        ins = dve.tensor_scalar(acc[:], adaE[k][:], cact[:, 0:1], None, ALU.mult)
                    else:
                        dve.wait_ge(s["ada_early"], r)
                        ins = dve.scalar_tensor_tensor(out=acc[:], in0=adaE[k][:], scalar=cact[:, k:k + 1], in1=acc[:],
                                                       op0=ALU.mult, op1=ALU.add)
                    ins.then_inc(s["ada_early"], 1)
                dve.wait_ge(s["ada_part"], 2)
                dve.tensor_tensor(mod[:, 2 * KT:4 * KT], half(3, 1)[:, 256:256 + 2 * KT], prm[:, R_ADAB + 2 * KT:R_ADAB + 4 * KT],
                                  ALU.add).then_inc(s["mod_rest"], 1)
                dt_work()
                for j in range(8):
                    if j == 7:
                        dve.wait_ge(s["mn_rstd"], 2)
                        dve.reciprocal(rst[:], rst[:]).then_inc(s["mn_rstd"], 1)
                    m = T_XBC + j
                    ps = bank[m % 2]
                    dve.wait_ge(s["conv_base"], j + 1)
                    for d in (1, 2, 3):
                        if d > 1:
                            dve.wait_ge(s["conv_tap"], 2 * j + d - 1)
                        col = R_CW + (3 - d) * 8 + j
                        ins = dve.scalar_tensor_tensor(out=xbc[:, j, d:T], in0=ps[:, 0:T - d], scalar=prm[:, col:col + 1],
                                                       in1=xbc[:, j, d:T], op0=ALU.mult, op1=ALU.add)
                        ins.then_inc(s["conv_tap"] if d < 3 else s[f"pair_free{m % 2}"], 1)

                dve.wait_ge(s["mn_sum"], 2)
                for k in range(2):
                    dve.scalar_tensor_tensor(out=cq[:, k, :], in0=cq[:, k, :], scalar=prm[:, R_QN + k:R_QN + k + 1], in1=bank[2][:],
                                             op0=ALU.mult, op1=ALU.mult).then_inc(s["mn_dve"], 1)
                dve.scalar_tensor_tensor(out=ckv[:], in0=ckv[:], scalar=prm[:, R_KN:R_KN + 1], in1=bank[3][:],
                                         op0=ALU.mult, op1=ALU.mult).then_inc(s["mn_dve"], 1)
                a, b = slice(64, 96), slice(96, 128)

                def rope(ins, n):
                    ins.then_inc(s["rope_dve"], 1)
                    dve.wait_ge(s["rope_dve"], n)

                rope(dve.tensor_tensor(misc[b, :], misc[b, :], cs[b, :], ALU.mult), 1)
                rope(dve.tensor_tensor(misc[a, :], misc[a, :], cs[a, :], ALU.mult), 2)
                dve.wait_ge(s["pack_used"], N_WIN)
                for h in range(MLA_H):
                    rope(dve.tensor_tensor(kh[h][a, :], misc[a, :], misc[b, :], ALU.add), 3 + h)
                for h in range(MLA_H):
                    dve.wait_ge(s["mp_full"], h + 1)
                    ps = bank[h]
                    if h:
                        dve.wait_ge(s["mp_q"], 3 * h)
                    dve.tensor_tensor(rt[a, :], ps[b, :], cs[b, :], ALU.mult).then_inc(s["mp_q"], 1)
                    dve.tensor_tensor(qh[h][a, :], ps[a, :], cs[a, :], ALU.mult).then_inc(s["mp_q"], 1)
                    dve.wait_ge(s["mp_q"], 3 * h + 2)
                    dve.tensor_tensor(qh[h][a, :], qh[h][a, :], rt[a, :], ALU.add).then_inc(s["mp_q"], 1)

                def sw_max(i):
                    dve.wait_ge(s["sw_s"], i + 1)
                    if i >= 2:
                        dve.wait_ge(s["sw_t"], i - 1)
                    lo = 0 if i else 1
                    p4 = pr[i % 2][:].rearrange("p (h b k) -> p h b k", h=4, b=2)
                    s4 = bank[i % 2][:].rearrange("p (h b k) -> p h b k", h=4, b=2)
                    st_ = stat[:, i % 3]
                    if i:
                        dve.scalar_tensor_tensor(out=p4.rearrange("p h b k -> p h (b k)"), in0=s4.rearrange("p h b k -> p h (b k)"), scalar=SWA_SCALE,
                                                 in1=band[:].rearrange("p b k -> p (b k)").unsqueeze(1).to_broadcast([P, 4, 2 * P]),
                                                 op0=ALU.mult, op1=ALU.add).then_inc(s["sw_m"], 1)
                    else:
                        dve.scalar_tensor_tensor(out=p4[:, :, 1, :], in0=s4[:, :, 1, :], scalar=SWA_SCALE,
                                                 in1=band[:, 1, :].unsqueeze(1).to_broadcast([P, 4, P]),
                                                 op0=ALU.mult, op1=ALU.add).then_inc(s["sw_m"], 1)
                    dve.wait_ge(s["sw_m"], i + 1)
                    src = p4.rearrange("p h b k -> p h (b k)") if i else p4[:, :, 1, :]
                    link(dve.tensor_reduce(st_[:, 0, :], src, AX.X, ALU.max))
                    link(dve.tensor_tensor(st_[:, 0, :], st_[:, 0, :], sink[:], ALU.max))
                    link(dve.tensor_scalar(st_[:, 1, :], st_[:, 0, :], -1.0, None, ALU.mult))
                    dve.tensor_tensor(st_[:, 3, :], st_[:, 1, :], sink[:], ALU.add).then_inc(s["sw_n"], 1)

                def sw_norm(i):
                    st_ = stat[:, i % 3]
                    dve.wait_ge(s["sw_e"], i + 1)
                    link(dve.tensor_tensor(st_[:, 5, :], st_[:, 2, :], st_[:, 4, :], ALU.add))
                    link(dve.reciprocal(st_[:, 5, :], st_[:, 5, :]))
                    normalise(i, "sw_o", i + 1, "sw_y", "sw_x")

                def normalise(i, o_sem, o_val, y_sem, x_sem):
                    dve.wait_ge(s[o_sem], o_val)
                    if i >= 2:
                        dve.wait_ge(s[y_sem], i - 1)
                    dve.tensor_tensor(otok[i % 2][:].rearrange("p (h d) -> p h d", h=4),
                                      half(3, 0)[:, 0:256].rearrange("p (h d) -> p h d", h=4),
                                      stat[:, i % 3, 5, :].unsqueeze(2).to_broadcast([P, 4, 64]), ALU.mult).then_inc(s[x_sem], 1)

                def y_lo(i, hi_sem, lo_sem, hi, lo):
                    dve.wait_ge(s[hi_sem], i + 1)
                    blk = slice(i * BLK, (i + 1) * BLK)
                    dve.tensor_tensor(lo[:, :, blk], half(3, 1)[:, 0:256].rearrange("p (k t) -> p k t", k=2),
                                      fview(hi[:, :, blk]), ALU.subtract).then_inc(s[lo_sem], 1)

                sw_max(0)
                for i in range(NB):
                    if i + 1 < NB:
                        sw_max(i + 1)
                    dve.wait_ge(s["sw_t"], i + 1)
                    if i >= 2:
                        dve.wait_ge(s["sw_o"], i - 1)
                    lo = 0 if i else 1
                    view = lambda t: t.rearrange("p (h b k) -> p h b k", h=2, b=2)[:, :, lo:2, :]
                    dve.tensor_copy(view(pt[i % 2][:, HALF:T]), view(half(2, 1))).then_inc(s["sw_cd"], 1)
                    if i >= 1:
                        sw_norm(i - 1)
                    if i >= 2:
                        y_lo(i - 2, "sw_hi", "sw_lo", sHi, sLo)
                sw_norm(NB - 1)
                y_lo(NB - 2, "sw_hi", "sw_lo", sHi, sLo)
                y_lo(NB - 1, "sw_hi", "sw_lo", sHi, sLo)

                def ml_max(u):
                    i, hs = UNITS[u]
                    n, k = (i + 1) * BLK, len(hs)
                    cols = slice(hs[0], hs[0] + k)
                    dve.wait_ge(s["ml_s"], u + 1)
                    sc = bank[u % 2][:].rearrange("p (q n) -> p q n", q=k)
                    diag = sc[:, :, i * BLK:n]
                    link(dve.tensor_tensor(diag, diag, band[:, 1, :].unsqueeze(1).to_broadcast([P, k, P]), ALU.add))
                    link(dve.tensor_reduce(stat[:, i % 3, 0, cols], sc[:, :, 0:n], AX.X, ALU.max))
                    dve.tensor_scalar(stat[:, i % 3, 1, cols], stat[:, i % 3, 0, cols], -MLA_SCALE, None, ALU.mult).then_inc(s["ml_n"], 1)

                def ml_norm(i):
                    dve.wait_ge(s["ml_e"], UNIT_END[i])
                    link(dve.reciprocal(stat[:, i % 3, 5, :], stat[:, i % 3, 2, :]))
                    normalise(i, "ml_o", UNIT_END[i], "ml_y", "ml_x")

                ml_max(0)
                for u in range(NU):
                    if u + 1 < NU:
                        ml_max(u + 1)
                    ml_copy(dve, u, "d", "ml_cd")
                    i = UNITS[u][0]
                    if i and u == UNIT_FIRST[i]:
                        ml_norm(i - 1)
                    if i and u == UNIT_END[i] - 1:
                        y_lo(i - 1, "ml_hi", "ml_lo", mHi, mLo)
                ml_norm(NB - 1)
                dve.wait_ge(s["ada_part"], 6)
                dve.tensor_tensor(mod[:, 4 * KT:6 * KT], half(3, 0)[:, 256 + 2 * KT:256 + 4 * KT], prm[:, R_ADAB + 4 * KT:R_ADAB + 6 * KT],
                                  ALU.add).then_inc(s["mod_rest"], 1)
                dve.tensor_copy(mod[:, 0:2 * KT], half(3, 0)[:, 256 + 4 * KT:256 + 6 * KT]).then_inc(s["mod_rest"], 1)
                dve.wait_ge(s["mod_rest"], 3)
                link(dve.scalar_tensor_tensor(out=scl[:, 1, :], in0=mod[:, 4 * KT:5 * KT], scalar=1.0, in1=prm[:, R_N2:R_N2 + KT],
                                              op0=ALU.add, op1=ALU.mult))
                y_lo(NB - 1, "ml_hi", "ml_lo", mHi, mLo)

                dve.wait_ge(s["sd_c"], 2)
                dve.tensor_tensor(dte[:], aend[:], adt[:, :, 0:8], ALU.subtract).then_inc(s["sd_xe0"], 1)
                dve.memset(hst[0][:], 0.0).then_inc(s["sd_h"], 1)

                for j in range(4):
                    dve.wait_ge(s["sd_xt"], j + 1)
                    o = slice(2 * j, 2 * j + 2)
                    dve.tensor_tensor(xd[:, :, o, :], bank[j % 2][:].rearrange("p (b h d) -> p b h d", b=NB, h=2),
                                      adt[:, :, 32 + 2 * j:34 + 2 * j].unsqueeze(3).to_broadcast([P, NB, 2, 64]), ALU.mult).then_inc(s["sd_xd"], 1)

                def mix(v):
                    ch, g = divmod(v, 2)
                    dve.wait_ge(s["sd_cb"], v + 1)
                    link(dve.tensor_tensor(cbm[v % 2][:], half(2, v % 2)[:, 0:P], caus01[:], ALU.mult))
                    dve.wait_ge(s["sd_dec"], v + 1)
                    dve.tensor_tensor(Mt[v % 2][:], Mt[v % 2][:], cbm[v % 2][:].unsqueeze(1).to_broadcast([P, 4, P]), ALU.mult).then_inc(s["sd_M"], 1)

                def next_state(ch):
                    old, new = hst[ch % 2], hst[(ch + 1) % 2]
                    if ch:
                        dve.wait_ge(s["sd_yd"], 2 * ch)
                    dve.wait_ge(s["sd_c"], 3)
                    dve.tensor_tensor(new[:], old[:], dec[:, ch, :].unsqueeze(2).to_broadcast([P, 8, 64]), ALU.mult).then_inc(s["sd_h"], 1)
                    dve.wait_ge(s["sd_h"], 2 + 2 * ch)
                    dve.wait_ge(s["sd_st"], 2 * ch + 2)
                    dve.tensor_tensor(new[:], new[:], half(ch % 2, 1).rearrange("p (h d) -> p h d", h=8), ALU.add).then_inc(s["sd_h"], 1)

                def chunk_out(ch):
                    c0 = slice(ch * BLK, (ch + 1) * BLK)
                    dve.wait_ge(s["sd_yd"], 2 * ch + 2)
                    for j in range(4):
                        last = dve.scalar_tensor_tensor(out=xbc[:, j, c0], in0=xbc[:, j, c0], scalar=dcol[:, j:j + 1],
                                                        in1=half(3, ch % 2)[:, j * P:(j + 1) * P], op0=ALU.mult, op1=ALU.add)
                    last.then_inc(s["sd_yd_read"], 1)

                for v in range(2 * NB):
                    mix(v)
                    if v % 2:
                        if v // 2 < NB - 1:
                            next_state(v // 2)
                        if v > 1:
                            chunk_out(v // 2 - 1)
                chunk_out(NB - 1)
                inverse(rst[:], "sd_rstd")
                dve.wait_ge(s["sd_spread"], 1)
                def ssd_scaled(j):
                    dve.scalar_tensor_tensor(out=xbc[:, j, :], in0=xbc[:, j, :], scalar=prm[:, R_SN + j:R_SN + j + 1],
                                             in1=bank[2 + j // 2][:], op0=ALU.mult, op1=ALU.mult).then_inc(s["sd_rd"], 1)

                ssd_scaled(0)
                for j in range(4):
                    if j < 3:
                        ssd_scaled(j + 1)
                    dve.wait_ge(s["sd_hi"], j + 1)
                    dve.tensor_tensor(yLo[:, j, :], xbc[:, j, :], fview(yHi[:, j, :]), ALU.subtract).then_inc(s["sd_lo"], 1)

                for m in range(KT):
                    dve.wait_ge(s["pack_used"], N_OUT0 + m + 1)
                    if m == 4:
                        dve.wait_ge(s["tail_loaded"], 16)
                    dve.scalar_tensor_tensor(out=xT[:, m, :], in0=bank[m % 2][:], scalar=mod[:, 2 * KT + m:2 * KT + m + 1],
                                             in1=xT[:, m, :], op0=ALU.mult, op1=ALU.add).then_inc(s["x_updated"], 1)
                    if m >= 2:
                        norm_adds(2, m - 1)
                norm_adds(2, KT - 1)
                inverse(rst[:, 0:NB], "n2_rstd")
                dve.wait_ge(s["n2_spread"], 1)
                norm_apply(2)

                due = []

                def tap(G, j, d):
                    c, is_b = divmod(j, 2)
                    y = (ub if is_b else ua)[c]
                    if d == 2:
                        dve.wait_ge(s["up_tap"], 8 * G + 2 * j + 1)
                    col = 2 * G + c + is_b * FT + (2 - d) * 2 * FT
                    dve.scalar_tensor_tensor(out=y[:, d:T], in0=bank[is_b][:, 0:T - d], scalar=ffp[:, bass.ds(col, 1)],
                                             in1=y[:, d:T], op0=ALU.mult, op1=ALU.add).then_inc(s["up_tap"], 1)

                def gate(G, c):
                    dve.wait_ge(s["up_silu"], 2 * G + c + 1)
                    dve.wait_ge(s["up_tap"], 8 * G + 4 * c + 4)
                    dve.tensor_tensor(ua[c][:], ua[c][:], ub[c][:], ALU.mult).then_inc(s["up_mul"], 1)

                def up(G, par, nxt):
                    for j in range(4):
                        dve.wait_ge(s["up_base"], 4 * G + j + 1)
                        tap(G, j, 1)
                        if j == 3 and nxt[0] == "down":
                            due.append(G)
                            continue
                        tap(G, j, 2)
                        if j % 2:
                            gate(G, j // 2)

                def down(G, par, nxt):
                    for m in range(KT):
                        dve.wait_ge(s["down_full"], 8 * G + m + 1)
                        if not (type(G) is int and G == 0):
                            dve.wait_ge(s[f"down_free{m % 2}"], 4 * (G - 1) + m // 2 + 1)
                        dve.scalar_tensor_tensor(out=xT[:, m, :], in0=bank[2 + m % 2][:], scalar=mod[:, 5 * KT + m:5 * KT + m + 1],
                                                 in1=xT[:, m, :], op0=ALU.mult, op1=ALU.add).then_inc(s[f"down_free{m % 2}"], 1)
                        if nxt is None and m >= 2:
                            norm_adds(1, m - 1)
                        if nxt is None and m == 4:
                            first_modulation(dve)
                        if due and m == 0:
                            tap(due[0], 3, 2)
                        elif due and m == 1:
                            gate(due.pop(), 1)

                run_mlp(dve, up, nothing, down)
                norm_adds(1, KT - 1)
                inverse(rst[:, 0:NB], "n1_rstd")

        with nc.Block() as block:
            @block.sync
            def _(sp):
                for name in names[0::5]:
                    sp.sem_clear(s[name])

            @block.gpsimd
            def _(pool):
                for name in names[1::5]:
                    pool.sem_clear(s[name])

            @block.scalar
            def _(act):
                for name in names[2::5]:
                    act.sem_clear(s[name])

            @block.vector
            def _(dve):
                for name in names[3::5]:
                    dve.sem_clear(s[name])

            @block.tensor
            def _(pe):
                for name in names[4::5]:
                    pe.sem_clear(s[name])

    xout = [place(f"xout{i}", [P, D], F32, E[i]) for i in range(NB)]
    gain = place("finalGain", [P, D], F32, E[8])
    BY_DVE = (0, 1, 3, 4, 6, 7)
    with ExitStack() as st:
        s = sems(st, ["gain_loaded", "transposed", "by_act", "made_pool", "made_dve", "out_written"])
        with nc.Block() as block:

            def freed(eng, t):
                if t in BY_DVE:
                    eng.wait_ge(s["made_dve"], BY_DVE.index(t) + 1)
                else:
                    eng.wait_ge(s["by_act"], 1 + (2, 5).index(t))

            @block.tensor
            def _(pe):
                for t in range(NB):
                    if t >= 4:
                        freed(pe, t - 4)
                    for k in range(KT):
                        last = pe.transpose(bank[t % 4][:, k * P:(k + 1) * P], xT[:, k, t * P:(t + 1) * P], ident[:])
                    last.then_inc(s["transposed"], 1)

            @block.scalar
            def _(act):
                for t in (2, 5):
                    act.wait_ge(s["transposed"], t + 1)
                    act.activation(xout[t][:], bank[t % 4][:], ACT.Copy, scale=rst[:, t:t + 1]).then_inc(s["by_act"], 1)

            @block.gpsimd
            def _(pool):
                pool.wait_ge(s["gain_loaded"], 16)
                for n, t in enumerate((2, 5)):
                    pool.wait_ge(s["by_act"], n + 1)
                    pool.tensor_tensor(xout[t][:], xout[t][:], gain[:], ALU.mult).then_inc(s["made_pool"], 1)

            @block.vector
            def _(dve):
                dve.wait_ge(s["gain_loaded"], 16)
                for t in BY_DVE:
                    dve.wait_ge(s["transposed"], t + 1)
                    dve.scalar_tensor_tensor(out=xout[t][:], in0=bank[t % 4][:], scalar=rst[:, t:t + 1], in1=gain[:],
                                             op0=ALU.mult, op1=ALU.mult).then_inc(s["made_dve"], 1)

            @block.sync
            def _(sp):
                sp.dma_start(gain[:], final_norm_g.rearrange("(o d) -> o d", o=1).to_broadcast([P, D])).then_inc(s["gain_loaded"], 16)
                for t in (0, 1, 3, 2, 4, 6, 5, 7):
                    if t in BY_DVE:
                        sp.wait_ge(s["made_dve"], BY_DVE.index(t) + 1)
                    else:
                        sp.wait_ge(s["made_pool"], 1 + (2, 5).index(t))
                    sp.dma_start(out[0, t * P:(t + 1) * P, :], xout[t][:]).then_inc(s["out_written"], 16)
                sp.wait_ge(s["out_written"], 16 * NB)


_INS = ["x", "c", "positions", "ada_w", "ada_b", "norm1_g", "norm2_g", "w_in", "ssd_conv_w", "ssd_conv_b",
        "ssd_dt_bias", "ssd_a_log", "ssd_d", "ssd_norm_g", "mla_q_norm_g", "mla_w_uq", "mla_kv_norm_g",
        "mla_w_ukv", "swa_sinks", "w_out", "ffn_w_up", "ffn_conv_w", "ffn_conv_b", "ffn_w_down", "final_norm_g"]


def rope_constants():
    k = np.zeros((P, 4), np.float32)
    inv = np.float32(10000.0) ** (-np.arange(0, MLA_ROPE, 2, dtype=np.float32) / np.float32(MLA_ROPE))
    k[64:, 0] = np.tile(inv, 4)
    k[64:96, 1], k[64:96, 2] = 0.25, np.pi / 2
    k[:, 3] = 1.0
    k[96:112, 3] = -1.0
    return k


def kernel(**inputs):
    import numpy as _np
    import concourse.bacc as _bacc
    from concourse import mybir as _mybir
    from concourse.bass_utils import run_bass_kernel_spmd as _run

    nc = _bacc.Bacc("TRN2", target_bir_lowering=False, num_devices=1)
    arrays, args = {}, []
    held = [(n, inputs[n]) for n in _INS] + [("rope_consts", rope_constants())]
    for name, a in held:
        a = _np.ascontiguousarray(a)
        arrays[f"in_{name}_dram"] = a
        args.append(nc.dram_tensor(f"in_{name}_dram", a.shape, _mybir.dt.from_np(a.dtype), kind="ExternalInput").ap())
    args.append(nc.dram_tensor("out_0_dram", (1, T, D), F32, kind="ExternalOutput").ap())
    build(nc, *args)
    r = _run(nc, [arrays], core_ids=[0])
    return r.results[0]["out_0_dram"]
```
